# Optimizing a Trainium2 kernel written in Bass

```python
import math
import jax, jax.numpy as jnp
from jax import lax
import numpy as np
import jax
import jax.numpy as jnp

D_MODEL = 1024
BATCH = 1
SEQ = 256
DEPTH = 2

CHUNK = 64
Q_BLOCK = 128
EPS = 1e-6
MAX_OFFSET = 4096

HG_HEADS = 4
HG_DK = 128
HG_DV = 128
HG_WIDTH = HG_HEADS * HG_DV

MLA_HEADS = 8
MLA_NOPE = 64
MLA_ROPE = 32
MLA_V = 64
MLA_Q_LORA = 384
MLA_KV_LORA = 256
MLA_DQK = MLA_NOPE + MLA_ROPE
MLA_WIDTH = MLA_HEADS * MLA_V
ROPE_BASE = 10000.0

N_EXPERTS = 16
N_GROUPS = 4
EXPERTS_PER_GROUP = N_EXPERTS // N_GROUPS
TOPK_GROUPS = 1
TOP_K = 2
D_EXPERT = 512

IN_SIZES = (HG_HEADS * HG_DK,
            HG_HEADS * HG_DK,
            HG_HEADS * HG_DV,
            HG_WIDTH,
            MLA_Q_LORA,
            MLA_KV_LORA,
            MLA_ROPE,
            2 * D_MODEL)
IN_COLS = int(sum(IN_SIZES))
IN_SPLITS = tuple(int(v) for v in np.cumsum(IN_SIZES)[:-1])


def rmsnorm(x, g):
    xf = x.astype(jnp.float32)
    y = xf * lax.rsqrt(jnp.mean(xf * xf, axis=-1, keepdims=True) + EPS)
    return (y * g.astype(jnp.float32)).astype(x.dtype)

def rotary(x, pos):
    half = x.shape[-1] // 2
    inv = ROPE_BASE ** (-jnp.arange(half, dtype=jnp.float32) / half)
    ang = pos.astype(jnp.float32)[..., None] * inv
    cos = jnp.cos(ang)[:, :, None, :]
    sin = jnp.sin(ang)[:, :, None, :]
    xf = x.astype(jnp.float32)
    x1, x2 = xf[..., :half], xf[..., half:]
    return jnp.concatenate([x1 * cos - x2 * sin, x1 * sin + x2 * cos], -1).astype(x.dtype)

def hgrn2_mix(q, f_logit, v, lb):
    B, S = q.shape[0], q.shape[1]
    nc = S // CHUNK
    lbh = lb.astype(jnp.float32).reshape(HG_HEADS, HG_DK)
    f = lbh + (1.0 - lbh) * jax.nn.sigmoid(f_logit.astype(jnp.float32))
    log_f = jnp.log(f)
    k = 1.0 - f
    qf = jax.nn.silu(q.astype(jnp.float32)) * (HG_DK ** -0.5)
    vf = v.astype(jnp.float32)

    def to_chunks(t):
        return t.reshape(B, nc, CHUNK, HG_HEADS, t.shape[-1]).transpose(1, 0, 3, 2, 4)

    qc, kc, vc, gc = to_chunks(qf), to_chunks(k), to_chunks(vf), to_chunks(log_f)
    causal = jnp.tril(jnp.ones((CHUNK, CHUNK), dtype=bool))[:, :, None]

    def step(state, inp):
        qb, kb, vb, gb = inp
        b = jnp.cumsum(gb, axis=2)
        rel = b[:, :, :, None, :] - b[:, :, None, :, :]
        decay = jnp.exp(jnp.where(causal, rel, -jnp.inf))
        attn = jnp.einsum('bhtd,bhtsd,bhsd->bhts', qb, decay, kb)
        intra = jnp.einsum('bhts,bhsv->bhtv', attn, vb)
        inter = jnp.einsum('bhtd,bhdv->bhtv', qb * jnp.exp(b), state)
        b_last = b[:, :, -1:, :]
        k_dec = kb * jnp.exp(b_last - b)
        new_state = state * jnp.exp(b_last[:, :, 0, :, None]) + jnp.einsum('bhsd,bhsv->bhdv', k_dec, vb)
        return new_state, intra + inter

    state0 = jnp.zeros((B, HG_HEADS, HG_DK, HG_DV), jnp.float32)
    _, out = lax.scan(step, state0, (qc, kc, vc, gc))
    return out.transpose(1, 0, 3, 2, 4).reshape(B, S, HG_HEADS, HG_DV)

def mla_mix(c_q, c_kv, k_rope, pos, q_norm_g, w_q_up, kv_norm_g, w_kv_up):
    B, S = c_q.shape[0], c_q.shape[1]
    q = (rmsnorm(c_q, q_norm_g) @ w_q_up).reshape(B, S, MLA_HEADS, MLA_DQK)
    q = jnp.concatenate([q[..., :MLA_NOPE], rotary(q[..., MLA_NOPE:], pos)], -1)
    kv = (rmsnorm(c_kv, kv_norm_g) @ w_kv_up).reshape(B, S, MLA_HEADS, MLA_NOPE + MLA_V)
    k_nope, v = kv[..., :MLA_NOPE], kv[..., MLA_NOPE:]
    k_pe = rotary(k_rope[:, :, None, :], pos)
    k = jnp.concatenate([k_nope, jnp.broadcast_to(k_pe, (B, S, MLA_HEADS, MLA_ROPE)).astype(k_nope.dtype)], -1)
    scale = MLA_DQK ** -0.5
    nb = S // Q_BLOCK
    qb = q.reshape(B, nb, Q_BLOCK, MLA_HEADS, MLA_DQK).transpose(1, 0, 2, 3, 4)
    key_chunk = jnp.arange(S) // CHUNK

    def block(args):
        qblk, start = args
        q_chunk = (start + jnp.arange(Q_BLOCK)) // CHUNK
        s = jnp.einsum('bqhd,bkhd->bhqk', qblk, k, preferred_element_type=jnp.float32) * scale
        mask = key_chunk[None, :] <= q_chunk[:, None]
        p = jax.nn.softmax(jnp.where(mask, s, -jnp.inf), axis=-1).astype(v.dtype)
        return jnp.einsum('bhqk,bkhd->bqhd', p, v)

    out = lax.map(block, (qb, jnp.arange(nb, dtype=jnp.int32) * Q_BLOCK))
    return out.transpose(1, 0, 2, 3, 4).reshape(B, S, MLA_WIDTH)

def token_mix(h, pos, w_in, lb, hg_norm_g, q_norm_g, w_q_up, kv_norm_g, w_kv_up, w_br_a, w_br_b, w_out):
    B, S, D = h.shape
    proj = h @ w_in
    hq, hf, hi, hgate, cq, ckv, kr, gates = jnp.split(proj, IN_SPLITS, axis=-1)
    o_a = hgrn2_mix(hq.reshape(B, S, HG_HEADS, HG_DK), hf.reshape(B, S, HG_HEADS, HG_DK),
                    hi.reshape(B, S, HG_HEADS, HG_DV), lb)
    o_a = rmsnorm(o_a, hg_norm_g.reshape(HG_HEADS, HG_DV)).reshape(B, S, HG_WIDTH)
    o_a = (o_a * jax.nn.silu(hgate.astype(jnp.float32))).astype(h.dtype)
    y_a = o_a @ w_br_a
    y_b = mla_mix(cq, ckv, kr, pos, q_norm_g, w_q_up, kv_norm_g, w_kv_up) @ w_br_b
    g = jax.nn.sigmoid(gates.astype(jnp.float32))
    g_a, g_b = g[..., :D], g[..., D:]
    merged = (g_a * y_a.astype(jnp.float32) + g_b * y_b.astype(jnp.float32)).astype(h.dtype)
    return merged @ w_out

def grouped_moe(h, w_router, router_bias, w_gate, w_up, w_down):
    B, S, D = h.shape
    t = h.reshape(-1, D)
    scores = jax.nn.sigmoid((t @ w_router).astype(jnp.float32))
    biased = (scores + router_bias.astype(jnp.float32)).reshape(-1, N_GROUPS, EXPERTS_PER_GROUP)
    group_score = lax.top_k(biased, 2)[0].sum(-1)
    _, gidx = lax.top_k(group_score, TOPK_GROUPS)
    gmask = jax.nn.one_hot(gidx, N_GROUPS, dtype=jnp.float32).sum(-2) > 0
    masked = jnp.where(gmask[:, :, None], biased, -jnp.inf).reshape(-1, N_EXPERTS)
    _, eidx = lax.top_k(masked, TOP_K)
    sel = jnp.take_along_axis(scores, eidx, axis=-1)
    w = sel / sel.sum(-1, keepdims=True)
    combine = (jax.nn.one_hot(eidx, N_EXPERTS, dtype=jnp.float32) * w[..., None]).sum(-2)
    y = jnp.zeros(t.shape, jnp.float32)
    for e in range(N_EXPERTS):
        he = jax.nn.silu(t @ w_gate[e]) * (t @ w_up[e])
        y = y + combine[:, e:e + 1] * (he @ w_down[e]).astype(jnp.float32)
    return y.astype(h.dtype).reshape(B, S, D)

def first_inputs(seed: int = 0) -> dict:
    key = jax.random.key(seed)
    ks = jax.random.split(key, 24)
    f32 = jnp.float32
    D = D_MODEL

    def nrm(k, shape, scale):
        return jax.random.normal(k, shape, f32) * scale

    positions = (jax.random.randint(ks[2], (BATCH, 1), 0, MAX_OFFSET, dtype=jnp.int32)
                 + jnp.arange(SEQ, dtype=jnp.int32)[None, :]).astype(jnp.int32)
    return {
        "x": nrm(ks[0], (BATCH, SEQ, D), 1.0),
        "c": nrm(ks[1], (BATCH, D), 1.0),
        "positions": positions,
        "ada_w": nrm(ks[3], (DEPTH, D, 6 * D), 0.5 * D ** -0.5),
        "ada_b": nrm(ks[4], (DEPTH, 6 * D), 0.02),
        "norm1_g": 1.0 + nrm(ks[5], (DEPTH, D), 0.02),
        "w_in": nrm(ks[6], (DEPTH, D, IN_COLS), D ** -0.5),
        "hg_lb_logits": nrm(ks[7], (DEPTH, HG_HEADS * HG_DK), 1.0),
        "hg_norm_g": 1.0 + nrm(ks[8], (DEPTH, HG_WIDTH), 0.02),
        "q_norm_g": 1.0 + nrm(ks[9], (DEPTH, MLA_Q_LORA), 0.02),
        "w_q_up": nrm(ks[10], (DEPTH, MLA_Q_LORA, MLA_HEADS * MLA_DQK), MLA_Q_LORA ** -0.5),
        "kv_norm_g": 1.0 + nrm(ks[11], (DEPTH, MLA_KV_LORA), 0.02),
        "w_kv_up": nrm(ks[12], (DEPTH, MLA_KV_LORA, MLA_HEADS * (MLA_NOPE + MLA_V)), MLA_KV_LORA ** -0.5),
        "w_br_a": nrm(ks[13], (DEPTH, HG_WIDTH, D), HG_WIDTH ** -0.5),
        "w_br_b": nrm(ks[14], (DEPTH, MLA_WIDTH, D), MLA_WIDTH ** -0.5),
        "w_out": nrm(ks[15], (DEPTH, D, D), D ** -0.5),
        "norm2_g": 1.0 + nrm(ks[16], (DEPTH, D), 0.02),
        "w_router": nrm(ks[17], (D, N_EXPERTS), D ** -0.5),
        "router_bias": nrm(ks[18], (N_EXPERTS,), 0.01),
        "w_gate": nrm(ks[19], (DEPTH, N_EXPERTS, D, D_EXPERT), D ** -0.5),
        "w_up": nrm(ks[20], (DEPTH, N_EXPERTS, D, D_EXPERT), D ** -0.5),
        "w_down": nrm(ks[21], (DEPTH, N_EXPERTS, D_EXPERT, D), D_EXPERT ** -0.5),
        "final_g": 1.0 + nrm(ks[22], (D,), 0.02),
    }

def first_block(x, c, positions, ada_w, ada_b, norm1_g, w_in, hg_lb_logits, hg_norm_g,
              q_norm_g, w_q_up, kv_norm_g, w_kv_up, w_br_a, w_br_b, w_out, norm2_g,
              w_router, router_bias, w_gate, w_up, w_down, final_g):
    D = D_MODEL
    lb_soft = jax.nn.softmax(hg_lb_logits.astype(jnp.float32), axis=0)
    lb_all = jnp.cumsum(lb_soft, axis=0) - lb_soft[0:1]
    c_act = jax.nn.silu(c)
    for l in range(DEPTH):
        mod = c_act @ ada_w[l] + ada_b[l]
        sh1, sc1, g1 = mod[:, None, 0:D], mod[:, None, D:2 * D], mod[:, None, 2 * D:3 * D]
        sh2, sc2, g2 = mod[:, None, 3 * D:4 * D], mod[:, None, 4 * D:5 * D], mod[:, None, 5 * D:6 * D]
        h = rmsnorm(x, norm1_g[l]) * (1.0 + sc1) + sh1
        x = x + g1 * token_mix(h, positions, w_in[l], lb_all[l], hg_norm_g[l], q_norm_g[l], w_q_up[l],
                               kv_norm_g[l], w_kv_up[l], w_br_a[l], w_br_b[l], w_out[l])
        h = rmsnorm(x, norm2_g[l]) * (1.0 + sc2) + sh2
        x = x + g2 * grouped_moe(h, w_router, router_bias, w_gate[l], w_up[l], w_down[l])
    return rmsnorm(x, final_g)


GRID_W = 64
CTX_LEN = 256
N_MIXERS = 4
BLOCK = 128
WINDOW = 128
WIN_HEADS = 16
WIN_KV = 4
WIN_HD = 64
AX_HEADS = 8
AX_KV = 2
AX_HD = 128
ML_HEADS = 4
ML_DK = 128
ML_DV = 256
ML_CHUNK = 128
D_FF = 2816
ROPE_THETA = 10000.0
NEG = -1e30


def rms_norm(x, g):
    xf = x.astype(jnp.float32)
    y = xf * lax.rsqrt(jnp.mean(xf * xf, axis=-1, keepdims=True) + EPS)
    return (y * g.astype(jnp.float32)).astype(x.dtype)

def dwconv3(x, w):
    xp = jnp.pad(x, ((0, 0), (1, 1), (0, 0)))
    return xp[:, :-2] * w[0] + xp[:, 1:-1] * w[1] + xp[:, 2:] * w[2]

def adaln(cvec, w, b):
    m = (jax.nn.silu(cvec) @ w + b)[..., None, :]
    return jnp.split(m, 6, axis=-1)

def modulate(x, shift, scale):
    return x * (1 + scale) + shift

def axial_rope(n_tok, hd):
    rows = n_tok // GRID_W
    row = jnp.repeat(jnp.arange(rows, dtype=jnp.float32), GRID_W)
    col = jnp.tile(jnp.arange(GRID_W, dtype=jnp.float32), rows)
    n_freq = hd // 4
    inv = jnp.power(ROPE_THETA, -jnp.arange(n_freq, dtype=jnp.float32) / n_freq)
    ang = jnp.concatenate([row[:, None] * inv, col[:, None] * inv], axis=-1)
    return jnp.cos(ang), jnp.sin(ang)

def apply_rope(t, cos, sin):
    t1, t2 = jnp.split(t, 2, axis=-1)
    cos = cos.astype(t.dtype)
    sin = sin.astype(t.dtype)
    return jnp.concatenate([t1 * cos - t2 * sin, t2 * cos + t1 * sin], axis=-1)

def split_heads(t, n_heads, hd):
    b, s, _ = t.shape
    return t.reshape(b, s, n_heads, hd).transpose(0, 2, 1, 3)

def merge_heads(o):
    b, _, _, s, _ = o.shape
    return o.transpose(0, 3, 1, 2, 4).reshape(b, s, -1)

def qkv_heads(a, w_qkv, q_norm, k_norm, n_heads, n_kv, hd):
    b, s, _ = a.shape
    q, k, v = jnp.split(a @ w_qkv, [n_heads * hd, (n_heads + n_kv) * hd], axis=-1)
    q = rms_norm(split_heads(q, n_heads, hd), q_norm).reshape(b, n_kv, n_heads // n_kv, s, hd)
    k = rms_norm(split_heads(k, n_kv, hd), k_norm)
    v = split_heads(v, n_kv, hd)
    return q, k, v

def gqa_softmax(q, k, v, mask, sink):
    s = jnp.einsum('bkgqd,bkjd->bkgqj', q, k, preferred_element_type=jnp.float32) * (q.shape[-1] ** -0.5)
    if mask is not None:
        s = jnp.where(mask, s, NEG)
    if sink is None:
        p = jax.nn.softmax(s, axis=-1)
    else:
        sk = sink.astype(jnp.float32)[None, :, :, None, None]
        m = jnp.maximum(s.max(axis=-1, keepdims=True), sk)
        e = jnp.exp(s - m)
        p = e / (e.sum(axis=-1, keepdims=True) + jnp.exp(sk - m))
    return jnp.einsum('bkgqj,bkjd->bkgqd', p.astype(v.dtype), v)

def window_attention_mixer(a_lat, a_ctx, w_qkv, q_norm, k_norm, sink, w_o, ctx_out):
    b, s, _ = a_lat.shape
    nb = s // BLOCK
    g = WIN_HEADS // WIN_KV
    span = BLOCK + 2 * WINDOW
    q, k, v = qkv_heads(a_lat, w_qkv, q_norm, k_norm, WIN_HEADS, WIN_KV, WIN_HD)
    qc, kc, vc = qkv_heads(a_ctx, w_qkv, q_norm, k_norm, WIN_HEADS, WIN_KV, WIN_HD)
    cos, sin = axial_rope(s, WIN_HD)
    q = apply_rope(q, cos, sin)
    k = apply_rope(k, cos, sin)
    sink = sink.reshape(WIN_KV, g)
    kp = jnp.pad(k, ((0, 0), (0, 0), (WINDOW, WINDOW), (0, 0)))
    vp = jnp.pad(v, ((0, 0), (0, 0), (WINDOW, WINDOW), (0, 0)))
    qb = jnp.moveaxis(q.reshape(b, WIN_KV, g, nb, BLOCK, WIN_HD), 3, 0)
    offs = jnp.arange(span) - WINDOW
    ctx_cols = jnp.ones((BLOCK, kc.shape[2]), bool)

    def block(args):
        bi, qblk = args
        start = bi * BLOCK
        kw = jnp.concatenate([lax.dynamic_slice_in_dim(kp, start, span, axis=2), kc], axis=2)
        vw = jnp.concatenate([lax.dynamic_slice_in_dim(vp, start, span, axis=2), vc], axis=2)
        qpos = start + jnp.arange(BLOCK)
        kpos = start + offs
        band = (jnp.abs(qpos[:, None] - kpos[None, :]) <= WINDOW) & (kpos >= 0)[None, :] & (kpos < s)[None, :]
        return gqa_softmax(qblk, kw, vw, jnp.concatenate([band, ctx_cols], axis=1), sink)

    o = lax.map(block, (jnp.arange(nb), qb))
    o = jnp.moveaxis(o, 0, 3).reshape(b, WIN_KV, g, s, WIN_HD)
    y_lat = merge_heads(o) @ w_o
    y_ctx = merge_heads(gqa_softmax(qc, kc, vc, None, sink)) @ w_o if ctx_out else None
    return y_lat, y_ctx

def short_conv_mixer(a, w_in, conv_w, w_out):
    gate_b, gate_c, u = jnp.split(a @ w_in, 3, axis=-1)
    return (gate_b * dwconv3(gate_c * u, conv_w)) @ w_out

def axial_attention_mixer(a_lat, a_ctx, w_qkv, q_norm, k_norm, w_o, ctx_out):
    b, s, _ = a_lat.shape
    nb = s // BLOCK
    g = AX_HEADS // AX_KV
    q, k, v = qkv_heads(a_lat, w_qkv, q_norm, k_norm, AX_HEADS, AX_KV, AX_HD)
    qc, kc, vc = qkv_heads(a_ctx, w_qkv, q_norm, k_norm, AX_HEADS, AX_KV, AX_HD)
    cos, sin = axial_rope(s, AX_HD)
    q = apply_rope(q, cos, sin)
    k = apply_rope(k, cos, sin)
    k_all = jnp.concatenate([k, kc], axis=2)
    v_all = jnp.concatenate([v, vc], axis=2)
    qb = jnp.moveaxis(q.reshape(b, AX_KV, g, nb, BLOCK, AX_HD), 3, 0)

    def block(qblk):
        return gqa_softmax(qblk, k_all, v_all, None, None)

    o = lax.map(block, qb)
    o = jnp.moveaxis(o, 0, 3).reshape(b, AX_KV, g, s, AX_HD)
    y_lat = merge_heads(o) @ w_o
    y_ctx = merge_heads(gqa_softmax(qc, kc, vc, None, None)) @ w_o if ctx_out else None
    return y_lat, y_ctx

def mlstm_chunk_summary(k, v, log_i, log_f):
    cum = jnp.cumsum(log_f, axis=-1)
    a = cum[..., -1:] - cum + log_i
    m = a.max(axis=-1)
    w = jnp.exp(a - m[..., None])
    c_bar = jnp.einsum('...lv,...lk->...vk', v * w[..., None], k)
    n_bar = jnp.einsum('...l,...lk->...k', w, k)
    return c_bar, n_bar, m, cum

def mlstm_final_state(k, v, log_i, log_f):
    c_bar, n_bar, m, _ = mlstm_chunk_summary(k, v, log_i, log_f)
    return (c_bar, n_bar, m)

def mlstm_chunkwise(q, k, v, log_i, log_f, state):
    b, h, s, dk = q.shape
    dv = v.shape[-1]
    nc = s // ML_CHUNK
    qc = q.reshape(b, h, nc, ML_CHUNK, dk)
    kc = k.reshape(b, h, nc, ML_CHUNK, dk)
    vc = v.reshape(b, h, nc, ML_CHUNK, dv)
    lic = log_i.reshape(b, h, nc, ML_CHUNK)
    lfc = log_f.reshape(b, h, nc, ML_CHUNK)
    c_bar, n_bar, m_bar, cum = mlstm_chunk_summary(kc, vc, lic, lfc)

    def step(carry, xs):
        c_prev, n_prev, m_prev = carry
        cb, nb_, mb, gb = xs
        m_new = jnp.maximum(gb + m_prev, mb)
        decay = jnp.exp(gb + m_prev - m_new)
        inj = jnp.exp(mb - m_new)
        c_new = decay[..., None, None] * c_prev + inj[..., None, None] * cb
        n_new = decay[..., None] * n_prev + inj[..., None] * nb_
        return (c_new, n_new, m_new), (c_prev, n_prev, m_prev)

    xs = (jnp.moveaxis(c_bar, 2, 0), jnp.moveaxis(n_bar, 2, 0), jnp.moveaxis(m_bar, 2, 0), jnp.moveaxis(cum[..., -1], 2, 0))
    final, (c_start, n_start, m_start) = lax.scan(step, state, xs)
    c_start = jnp.moveaxis(c_start, 0, 2)
    n_start = jnp.moveaxis(n_start, 0, 2)
    m_start = jnp.moveaxis(m_start, 0, 2)
    tri = jnp.tril(jnp.ones((ML_CHUNK, ML_CHUNK), bool))
    d = jnp.where(tri, cum[..., :, None] - cum[..., None, :] + lic[..., None, :], NEG)
    inter = cum + m_start[..., None]
    m_t = jnp.maximum(inter, d.max(axis=-1))
    w_intra = jnp.exp(d - m_t[..., None])
    w_inter = jnp.exp(inter - m_t)
    qk = jnp.einsum('bhcld,bhcsd->bhcls', qc, kc) * w_intra
    num = jnp.einsum('bhcls,bhcsv->bhclv', qk, vc) + w_inter[..., None] * jnp.einsum('bhcld,bhcvd->bhclv', qc, c_start)
    den = qk.sum(axis=-1) + w_inter * jnp.einsum('bhcld,bhcd->bhcl', qc, n_start)
    out = num / jnp.maximum(jnp.abs(den), jnp.exp(-m_t))[..., None]
    return out.reshape(b, h, s, dv), final

def mlstm_mixer(a_lat, a_ctx, w_in, b_gate, h_norm, w_out, ctx_out):
    qk_w = ML_HEADS * ML_DK
    v_w = ML_HEADS * ML_DV

    def proj(a):
        b, s, _ = a.shape
        q, k, v, o, gates = jnp.split(a @ w_in, [qk_w, 2 * qk_w, 2 * qk_w + v_w, 2 * qk_w + 2 * v_w], axis=-1)
        q = split_heads(q, ML_HEADS, ML_DK).astype(jnp.float32) * (ML_DK ** -0.5)
        k = split_heads(k, ML_HEADS, ML_DK).astype(jnp.float32)
        v = split_heads(v, ML_HEADS, ML_DV).astype(jnp.float32)
        gates = (gates + b_gate).astype(jnp.float32).reshape(b, s, 4, ML_HEADS).transpose(2, 0, 3, 1)
        fwd = (gates[0], jax.nn.log_sigmoid(gates[1]))
        bwd = (gates[2], jax.nn.log_sigmoid(gates[3]))
        return q, k, v, o, fwd, bwd

    def flip(t):
        return jnp.flip(t, axis=2)

    def readout(h_f, h_b, o):
        hs = rms_norm(h_f + flip(h_b), h_norm)
        b, h, s, dv = hs.shape
        hs = hs.transpose(0, 2, 1, 3).reshape(b, s, h * dv).astype(o.dtype)
        return (jax.nn.sigmoid(o) * hs) @ w_out

    qc, kc, vc, oc, gfc, gbc = proj(a_ctx)
    bsz = a_ctx.shape[0]
    zero = (jnp.zeros((bsz, ML_HEADS, ML_DV, ML_DK), jnp.float32),
            jnp.zeros((bsz, ML_HEADS, ML_DK), jnp.float32),
            jnp.full((bsz, ML_HEADS), NEG, jnp.float32))
    if ctx_out:
        hc_f, st_f = mlstm_chunkwise(qc, kc, vc, gfc[0], gfc[1], zero)
        hc_b, st_b = mlstm_chunkwise(flip(qc), flip(kc), flip(vc), flip(gbc[0]), flip(gbc[1]), zero)
        y_ctx = readout(hc_f, hc_b, oc)
    else:
        st_f = mlstm_final_state(kc, vc, gfc[0], gfc[1])
        st_b = mlstm_final_state(flip(kc), flip(vc), flip(gbc[0]), flip(gbc[1]))
        y_ctx = None
    ql, kl, vl, ol, gfl, gbl = proj(a_lat)
    hl_f, _ = mlstm_chunkwise(ql, kl, vl, gfl[0], gfl[1], st_f)
    hl_b, _ = mlstm_chunkwise(flip(ql), flip(kl), flip(vl), flip(gbl[0]), flip(gbl[1]), st_b)
    return readout(hl_f, hl_b, ol), y_ctx

def conv_ffn(a, w_up, conv_w, w_down):
    g, u = jnp.split(dwconv3(a @ w_up, conv_w), 2, axis=-1)
    return (jax.nn.silu(g) * u) @ w_down

def second_inputs(seed: int = 0) -> dict:
    d = D_MODEL
    n_win, n_sc, n_ax, n_ml = [len(range(kind, DEPTH, N_MIXERS)) for kind in range(N_MIXERS)]
    keys = iter(jax.random.split(jax.random.key(seed), 40))

    def normal(shape, std):
        return std * jax.random.normal(next(keys), shape, jnp.float32)

    def gain(shape):
        return 1.0 + normal(shape, 0.1)

    ml_in = 2 * ML_HEADS * ML_DK + 2 * ML_HEADS * ML_DV + 4 * ML_HEADS
    f_base = jnp.linspace(3.0, 6.0, ML_HEADS, dtype=jnp.float32)
    zeros_h = jnp.zeros((ML_HEADS,), jnp.float32)
    gate_base = jnp.concatenate([zeros_h, f_base, zeros_h, f_base])
    return {
        'x': normal((BATCH, SEQ, d), 1.0),
        'c': normal((BATCH, d), 1.0),
        'ctx': normal((BATCH, CTX_LEN, d), 1.0),
        'c_ctx': normal((d,), 1.0),
        'ada_w': normal((DEPTH, d, 6 * d), 0.5 * d ** -0.5),
        'ada_b': normal((DEPTH, 6 * d), 0.02),
        'norm_mix': gain((DEPTH, d)),
        'norm_ffn': gain((DEPTH, d)),
        'ffn_w_up': normal((DEPTH, d, 2 * D_FF), d ** -0.5),
        'ffn_conv': normal((DEPTH, 3, 2 * D_FF), 3 ** -0.5),
        'ffn_w_down': normal((DEPTH, D_FF, d), D_FF ** -0.5),
        'win_w_qkv': normal((n_win, d, (WIN_HEADS + 2 * WIN_KV) * WIN_HD), d ** -0.5),
        'win_q_norm': gain((n_win, WIN_HD)),
        'win_k_norm': gain((n_win, WIN_HD)),
        'win_sink': normal((n_win, WIN_HEADS), 0.5),
        'win_w_o': normal((n_win, WIN_HEADS * WIN_HD, d), (WIN_HEADS * WIN_HD) ** -0.5),
        'sc_w_in': normal((n_sc, d, 3 * d), d ** -0.5),
        'sc_conv': normal((n_sc, 3, d), 3 ** -0.5),
        'sc_w_out': normal((n_sc, d, d), d ** -0.5),
        'ax_w_qkv': normal((n_ax, d, (AX_HEADS + 2 * AX_KV) * AX_HD), d ** -0.5),
        'ax_q_norm': gain((n_ax, AX_HD)),
        'ax_k_norm': gain((n_ax, AX_HD)),
        'ax_w_o': normal((n_ax, AX_HEADS * AX_HD, d), (AX_HEADS * AX_HD) ** -0.5),
        'ml_w_in': normal((n_ml, d, ml_in), d ** -0.5),
        'ml_b_gate': gate_base + normal((n_ml, 4 * ML_HEADS), 0.1),
        'ml_h_norm': gain((n_ml, ML_DV)),
        'ml_w_out': normal((n_ml, ML_HEADS * ML_DV, d), (ML_HEADS * ML_DV) ** -0.5),
    }

def second_block(x, c, ctx, c_ctx, ada_w, ada_b, norm_mix, norm_ffn, ffn_w_up, ffn_conv, ffn_w_down,
              win_w_qkv, win_q_norm, win_k_norm, win_sink, win_w_o,
              sc_w_in, sc_conv, sc_w_out,
              ax_w_qkv, ax_q_norm, ax_k_norm, ax_w_o,
              ml_w_in, ml_b_gate, ml_h_norm, ml_w_out):
    h, hc = x, ctx
    for i in range(DEPTH):
        kind, j = i % N_MIXERS, i // N_MIXERS
        ctx_out = i < DEPTH - 1
        sh1, sc1, g1, sh2, sc2, g2 = adaln(c, ada_w[i], ada_b[i])
        a_lat = modulate(rms_norm(h, norm_mix[i]), sh1, sc1)
        if ctx_out or kind != 1:
            csh1, csc1, cg1, csh2, csc2, cg2 = adaln(c_ctx, ada_w[i], ada_b[i])
            a_ctx = modulate(rms_norm(hc, norm_mix[i]), csh1, csc1)
        if kind == 0:
            y_lat, y_ctx = window_attention_mixer(a_lat, a_ctx, win_w_qkv[j], win_q_norm[j], win_k_norm[j],
                                                  win_sink[j], win_w_o[j], ctx_out)
        elif kind == 1:
            y_lat = short_conv_mixer(a_lat, sc_w_in[j], sc_conv[j], sc_w_out[j])
            y_ctx = short_conv_mixer(a_ctx, sc_w_in[j], sc_conv[j], sc_w_out[j]) if ctx_out else None
        elif kind == 2:
            y_lat, y_ctx = axial_attention_mixer(a_lat, a_ctx, ax_w_qkv[j], ax_q_norm[j], ax_k_norm[j],
                                                 ax_w_o[j], ctx_out)
        else:
            y_lat, y_ctx = mlstm_mixer(a_lat, a_ctx, ml_w_in[j], ml_b_gate[j], ml_h_norm[j], ml_w_out[j], ctx_out)
        h = h + g1 * y_lat
        h = h + g2 * conv_ffn(modulate(rms_norm(h, norm_ffn[i]), sh2, sc2), ffn_w_up[i], ffn_conv[i], ffn_w_down[i])
        if ctx_out:
            hc = hc + cg1 * y_ctx
            hc = hc + cg2 * conv_ffn(modulate(rms_norm(hc, norm_ffn[i]), csh2, csc2),
                                     ffn_w_up[i], ffn_conv[i], ffn_w_down[i])
    return h


def setup_inputs(seed=0):
    out = dict(first_inputs(seed))
    for name, value in second_inputs(seed + 1).items():
        if name != "x":
            out[name + "_2"] = value
    return out


def reference(
    x, c, positions, ada_w, ada_b, norm1_g, w_in, hg_lb_logits, hg_norm_g, q_norm_g, w_q_up,
    kv_norm_g, w_kv_up, w_br_a, w_br_b, w_out, norm2_g, w_router, router_bias, w_gate, w_up,
    w_down, final_g, c_2, ctx_2, c_ctx_2, ada_w_2, ada_b_2, norm_mix_2, norm_ffn_2, ffn_w_up_2,
    ffn_conv_2, ffn_w_down_2, win_w_qkv_2, win_q_norm_2, win_k_norm_2, win_sink_2, win_w_o_2,
    sc_w_in_2, sc_conv_2, sc_w_out_2, ax_w_qkv_2, ax_q_norm_2, ax_k_norm_2, ax_w_o_2, ml_w_in_2,
    ml_b_gate_2, ml_h_norm_2, ml_w_out_2,
):
    x = first_block(
        x, c, positions, ada_w, ada_b, norm1_g, w_in, hg_lb_logits, hg_norm_g, q_norm_g, w_q_up,
        kv_norm_g, w_kv_up, w_br_a, w_br_b, w_out, norm2_g, w_router, router_bias, w_gate, w_up,
        w_down, final_g,
    )
    return second_block(
        x, c_2, ctx_2, c_ctx_2, ada_w_2, ada_b_2, norm_mix_2, norm_ffn_2, ffn_w_up_2,
        ffn_conv_2, ffn_w_down_2, win_w_qkv_2, win_q_norm_2, win_k_norm_2, win_sink_2,
        win_w_o_2, sc_w_in_2, sc_conv_2, sc_w_out_2, ax_w_qkv_2, ax_q_norm_2, ax_k_norm_2,
        ax_w_o_2, ml_w_in_2, ml_b_gate_2, ml_h_norm_2, ml_w_out_2,
    )


_drawn_inputs = setup_inputs


def setup_inputs(seed=0):
    import zlib

    import numpy as np

    out = dict(_drawn_inputs(seed))
    spreads = {}
    factors = {'norm1_g': 3.889,
     'hg_lb_logits': 3.277,
     'hg_norm_g': 3.274,
     'q_norm_g': 3.676,
     'kv_norm_g': 5.863,
     'win_q_norm_2': 8.0,
     'win_k_norm_2': 8.0,
     'win_sink_2': 8.0}
    for name, (base, spread) in spreads.items():
        noise = np.random.default_rng([zlib.crc32(name.encode()), seed]).standard_normal(out[name].shape)
        drawn = base * np.exp(spread * noise) if base else spread * noise
        out[name] = jnp.asarray(drawn.astype(out[name].dtype))
    for name, factor in factors.items():
        out[name] = (out[name] * factor).astype(out[name].dtype)
    return out
```

```python
import concourse.bass as bass
from concourse import mybir
from contextlib import ExitStack
import numpy as np

F32 = mybir.dt.float32
I32 = mybir.dt.int32
ALU = mybir.AluOpType
ACT = mybir.ActivationFunctionType
AXX = mybir.AxisListType.X

P = 128
D = 1024
KT = D // P
S = 256
DEPTH = 2
EPS = 1e-6
RING, CHUNK = 6, 4096

HG_HEADS, HG_D, CH = 4, 128, 64
MLA_HEADS, NOPE, ROPE, MLA_V = 8, 64, 32, 64
DQK = NOPE + ROPE
QL, KVL = 384, 256
NE, NG, EG, DE = 16, 4, 4, 512
WH, WKV, WHD = 16, 4, 64
FF = 2816
FT = FF // P
LEVELS = (32, 16, 8, 4, 2, 1, 0)

C_ID, C_ONE, C_INV, C_PR, C_MM, N_C1 = np.cumsum([0, 128, 128, 1, 32, 384]).tolist()
C_LV = N_C1
C_RT = C_LV + 64 * len(LEVELS)
C1_OVER = C_PR
D_B64, D_P64, D_SEL, D_COS, D_SIN, D_WM, N_C2 = np.cumsum([0, 128, 128, 256, 256, 256, 512]).tolist()

V_NG = 0
V_FIN = V_NG + 64
V_HG = V_FIN + 8
V_CL = V_HG + 8
V_LB = V_CL + 10
V_RB = V_LB + 8
V_C = V_RB + 16
V_ADAB = V_C + 32
V_WQ = V_ADAB + 192
V_WK = V_WQ + 1
V_SINK = V_WK + 1
V_FC = V_SINK + 16
V_SC = V_FC + 264
N_V = V_SC + 24

LAYER1 = 64
ADA = 48


def stack_program(nc, T, out):
    ctx = ExitStack()
    with ctx:
        def sb(name, shape, dt=F32):
            return ctx.enter_context(nc.sbuf_tensor(name, shape, dt))

        def sem(name):
            return ctx.enter_context(nc.semaphore(name))

        ring = [sb(f"ring{i}", [P, CHUNK]) for i in range(RING)]
        XH = sb("XH", [P, 8192])
        AR = sb("AR", [P, 16 * 1024])
        CS = sb("CS", [P, C1_OVER + N_C2])
        VEC = sb("VEC", [P, N_V])
        WR = sb("WR", [P, KT, NE])
        CACT = sb("CACT", [P, 2, KT, 2])
        MOD = sb("MOD", [P, 2, DEPTH, 48, 2])
        COEF = sb("COEF", [P, 2, DEPTH, 2, KT, 2])
        RST = sb("RST", [P, 512])
        LB = sb("LB", [P, 2, 2, 4])
        SM = sb("SM", [P, 208])
        EPSC = sb("EPSC", [P, 1])
        pair = [ctx.enter_context(nc.psum_tensor(f"pair{i}", [P, 1024], F32)) for i in range(4)]
        PA, PB, PC, PD = [q[:, :] for q in pair]

        def blk(i, n=1024):
            return AR[:, i * 1024:i * 1024 + n]

        ident, ones = CS[:, C_ID:C_ID + P], CS[:, C_ONE:C_ONE + P]
        X1 = XH[:, 0:2048].rearrange("p (t n) -> p t n", t=KT)
        H1 = XH[:, 2048:4096].rearrange("p (t n) -> p t n", t=KT)
        F = [XH[:, 4096 + 1024 * i:5120 + 1024 * i] for i in range(4)]
        X2 = XH[:, 4096:8192].rearrange("p (t n) -> p t n", t=KT)
        H2 = XH[:, 0:4096].rearrange("p (t n) -> p t n", t=KT)

        SCO_, R_BI, R_RK, R_GE = [SM[:, 32 * i:32 * i + 32] for i in range(4)]
        R_GS, R_GR, R_GG = [SM[:, 128 + 8 * i:136 + 8 * i] for i in range(3)]
        R_DN = SM[:, 152:154]
        DEC, BLAST = SM[:, 156:172], SM[:, 172:188]
        NM, RSUM = SM[:, 188:196], SM[:, 196:204]
        WNM, WRS, WES = [SM[:, 8 * i:8 * i + 8].rearrange("p (a n) -> p a n", a=2) for i in range(3)]
        LVM = CS[:, C_LV:C_RT].bitcast(mybir.dt.bfloat16)
        RT = CS[:, C_RT:C_RT + 2 * S]
        KR = XH[64:96, 4096 + 1536:4096 + 1536 + S]
        LRS = F[3][:, 0:512].rearrange("p (a n) -> p a n", a=2)
        CVT = [AR[:, (12 + j) * 1024:(13 + j) * 1024].rearrange("p (h n) -> p h n", h=2) for j in range(2)]
        GU = [blk(12), blk(13)]
        POS, ANG, KK = [AR[0:DQK, 1024 * i:1024 * i + S] for i in range(3)]

        def h_count(n):
            return n + 1 if n < 4 else n

        names = """multiplied const1_in levels_in const2_in vec_in router_in x_in ctx_in pos_in out_stored
        act_step dve_step pool_step
        cact_ready mod_ready coef_ready rope_ready lb_ready angle_ready
        squares_ready sums_ready std_ready scaled_ready h_act h_dve x_done
        hf_sig hq_silu hq_scaled v_copied hg_silu lat1_copied lat2_copied gates_act
        lat_sums lat_std latn_ready f_ready lnf_ready b_ready eb_ready qb_ready kdiff_ready kexp_ready kd_ready
        kd_turned kdt_ready u_ready dec_ready states_ready
        lvl_diff lvl_exp lvl_qk lvl_score lvl_masked lvl_added o_ready o_copied o_sums o_std oa_ready
        q_copied kr_turned rope_done k_copied v2_copied
        sc_ready sm_max sm_exp p_ready p_turned pt_ready om_ready om_copied
        bra_mul brb_mul merged_ready
        rt_ready rt_sig comb_ready diag_ready cbc_ready cbc_copied sg_ready gu_ready he_ready acc_zero
        wq_copied wsum_ready wstd_ready wn_ready wrot_ready wroped k_dup kdup_copied wv_copied
        wsq_ready ot_ready ot_copied
        cv_mid cv_conv cv_silu ff_act gc_copied scv_ready sc_mid scz_ready""".split()
        s = {n: sem(n) for n in names}
        full = [sem(f"slot{i}_full") for i in range(RING)]
        block = ctx.enter_context(nc.Block())

        def first(l):
            return ADA + l * LAYER1
        HFc, HQc, HIc, HGc, L1c, L2c, GTc, QUc, KVc, BAc, BBc, WOc, MOEc = 0, 1, 2, 3, 4, 5, 6, 10, 11, 12, 13, 14, 16
        B2 = ADA + DEPTH * LAYER1
        WQKV, WWO, FF0 = B2, B2 + 3, B2 + 5
        FFC = 11 + 6
        SCI, SCO, FF1 = FF0 + FFC, FF0 + FFC + 6, FF0 + FFC + 8

        @block.sync
        def _(sp):
            def put(c, src, shape, i=0):
                if not isinstance(c, int) or c >= RING:
                    sp.wait_ge(s["multiplied"], i + (c - RING + 1))
                dst = ring[c % RING][:, 0:shape[0] * shape[1]].rearrange("p (t n) -> p t n", t=shape[0])
                sp.dma_start(dst, src).then_inc(full[c % RING], 16)

            def cols(w, a, n):
                return w[:, a:a + n].rearrange("(t p) n -> p t n", p=P)

            sp.dma_start(VEC[:, :], T["vec"]).then_inc(s["vec_in"], 16)
            sp.dma_start(CS[:, 0:N_C1], T["const1"]).then_inc(s["const1_in"], 16)
            sp.dma_start(LVM, T["levels"]).then_inc(s["levels_in"], 16)
            sp.dma_start(POS.bitcast(I32), T["pos"]).then_inc(s["pos_in"], 16)
            sp.dma_start(X1, T["x"].rearrange("(t p) n -> p t n", p=P)).then_inc(s["x_in"], 16)
            sp.dma_start(WR[:, :, :], T["w_router"].rearrange("(t p) n -> p t n", p=P)).then_inc(s["router_in"], 16)
            for a, w in enumerate((T["ada_w"], T["ada_w_2"])):
                for l in range(DEPTH):
                    for k in range(12):
                        put(24 * a + 12 * l + k, cols(w[l, :, :], 512 * k, 512), (8, 512))
            for l in range(DEPTH):
                c0, w_in = first(l), T["w_in"][l, :, :]
                put(c0 + HFc, cols(w_in, 512, 512), (8, 512))
                put(c0 + HQc, cols(w_in, 0, 512), (8, 512))
                put(c0 + HIc, cols(w_in, 1024, 512), (8, 512))
                put(c0 + HGc, cols(w_in, 1536, 512), (8, 512))
                put(c0 + L1c, cols(w_in, 2048, 512), (8, 512))
                put(c0 + L2c, cols(w_in, 2560, 160), (8, 160))
                for k in range(4):
                    put(c0 + GTc + k, cols(w_in, 2720 + 512 * k, 512), (8, 512))
                put(c0 + QUc, cols(T["w_q_up"][l, :, :], 0, 768), (3, 768))
                put(c0 + KVc, cols(T["w_kv_up"][l, :, :], 0, 1024), (2, 1024))
                put(c0 + BAc, cols(T["w_br_a"][l, :, :], 0, 1024), (4, 1024))
                put(c0 + BBc, cols(T["w_br_b"][l, :, :], 0, 1024), (4, 1024))
                for k in range(2):
                    put(c0 + WOc + k, cols(T["w_out"][l, :, :], 512 * k, 512), (8, 512))
                m0 = c0 + MOEc

                def expert(w, e, t):
                    return w[l, bass.ds(e, 1), :, :].rearrange("a (t p) n -> p (a t) n", p=P)
                put(m0, expert(T["w_gate"], 0, 8), (8, 512))
                put(m0 + 1, expert(T["w_up"], 0, 8), (8, 512))
                with sp.Fori(0, 7) as i:
                    for j in range(2):
                        c = m0 + 2 + 3 * j
                        put(c, expert(T["w_gate"], i * 2 + (1 + j), 8), (8, 512), i * 6)
                        put(c + 1, expert(T["w_up"], i * 2 + (1 + j), 8), (8, 512), i * 6)
                        put(c + 2, expert(T["w_down"], i * 2 + j, 4), (4, 1024), i * 6)
                put(m0 + 44, expert(T["w_gate"], 15, 8), (8, 512))
                put(m0 + 45, expert(T["w_up"], 15, 8), (8, 512))
                put(m0 + 46, expert(T["w_down"], 14, 4), (4, 1024))
                put(m0 + 47, expert(T["w_down"], 15, 4), (4, 1024))
                if l == DEPTH - 1:
                    sp.wait_ge(s["om_copied"], 3 * DEPTH)
                    sp.wait_ge(s["bra_mul"], 2 * DEPTH)
                    sp.dma_start(CS[:, C1_OVER:C1_OVER + N_C2], T["const2"]).then_inc(s["const2_in"], 16)
                    sp.dma_start(X2[:, :, S:2 * S], T["ctx"].rearrange("(t p) n -> p t n", p=P)).then_inc(s["ctx_in"], 16)
            for k in range(3):
                put(WQKV + k, cols(T["win_w_qkv"], 512 * k, 512), (8, 512))
            for k in range(2):
                put(WWO + k, cols(T["win_w_o"], 512 * k, 512), (8, 512))

            def ffn(c0, l):
                up = T["ffn_w_up"][l, :, :].rearrange("(t p) (h n) -> p t h n", p=P, h=2)
                for k in range(11):
                    c = c0 + k
                    sp.wait_ge(s["multiplied"], c - RING + 1)
                    dst = ring[c % RING][:, :].rearrange("p (t h n) -> p t h n", t=KT, h=2)
                    for h in range(2):
                        sp.dma_start(dst[:, :, h, :], up[:, :, h, 256 * k:256 * k + 256])\
                            .then_inc(full[c % RING], 8 * 2)
                dn = T["ffn_w_down"][l, :, :]
                for half in range(2):
                    for k, (a, n) in enumerate(((0, 8), (8, 8), (16, 6))):
                        put(c0 + 11 + 3 * half + k, cols(dn[a * P:(a + n) * P, :], 512 * half, 512), (n, 512))
            ffn(FF0, 0)
            for half in range(2):
                for k, part in enumerate((1, 2, 0)):
                    put(SCI + 3 * half + k, cols(T["sc_w_in"], 1024 * part + 512 * half, 512), (8, 512))
            for k in range(2):
                put(SCO + k, cols(T["sc_w_out"], 512 * k, 512), (8, 512))
            ffn(FF1, 1)
            sp.wait_ge(s["x_done"], 9)
            sp.dma_start(out.rearrange("(t p) n -> p t n", p=P), X2[:, :, 0:S]).then_inc(s["out_stored"], 16)
            sp.wait_ge(s["out_stored"], 16)

        def extra(c):
            n = 0
            for f in (FF0, FF1):
                n += sum(1 for k in range(f, f + 11) if k <= c and k % RING == c % RING)
            return n

        @block.tensor
        def _(pe):
            def arrived(c, i=0):
                pe.wait_ge(full[c % RING], i * 16 + 16 * (c // RING + 1 + extra(c)))

            def view(c, t, n):
                return ring[c % RING][:, 0:t * n].rearrange("p (t n) -> p t n", t=t)

            def mm(o, lhsT, rhs, start, stop, **kw):
                return pe.matmul(o, lhsT, rhs, start=start, stop=stop, **kw)

            def features(c, outs, rhs, n_k=KT, width=512, M=P, i=0):
                arrived(c, i)
                w = view(c, n_k, width)
                for m, o in enumerate(outs):
                    for t in range(n_k):
                        last = mm(o, w[:, t, m * M:m * M + M], rhs(t), t == 0, t == n_k - 1)
                return last

            def done(last):
                last.then_inc(s["multiplied"], 1)

            pe.wait_ge(s["const1_in"], 16)
            for a in range(2):
                if a == 0:
                    pe.wait_ge(s["cact_ready"], 1)
                with pe.Fori(0, 4) as i:
                    for k in range(RING):
                        pe.wait_ge(full[k], i * 16 + 16 * (4 * a + 1))
                        w = view(k, KT, 512)
                        for m in range(4):
                            col = (i + 4 * a) * 48 + (8 * k + 2 * m)
                            for t in range(KT):
                                last = mm(PA[:, bass.ds(col, 2)], w[:, t, m * P:m * P + P], CACT[:, a, t, :],
                                          t == 0, t == KT - 1)
                        done(last)

            def sums(n, H, N):
                pe.wait_ge(s["squares_ready"], n + 1)
                for t in range(KT):
                    last = mm(PD[:, 0:N], ones, H[:, t, :], t == 0, t == KT - 1)
                last.then_inc(s["sums_ready"], 1)

            def h_arrived(n):
                pe.wait_ge(s["h_act"], h_count(n))
                pe.wait_ge(s["h_dve"], h_count(n))

            def half(q, m, N=S):
                return q[:, m * N:m * N + N]

            for l in range(DEPTH):
                c0 = first(l)
                sums(2 * l, H1, S)
                h_arrived(2 * l)
                hk = lambda t: H1[:, t, :]
                done(features(c0 + HFc, [half(PA, m) for m in range(4)], hk))
                done(features(c0 + HQc, [half(PB, m) for m in range(4)], hk))
                arrived(c0 + HIc)
                w = view(c0 + HIc, KT, 512)
                for m in range(2):
                    for t in range(KT):
                        last = mm(PC[:, 512 * m:512 * m + 512], H1[:, t, m * P:m * P + P], w[:, t, :], t == 0, t == KT - 1)
                done(last)
                done(features(c0 + HGc, [half(PD, m) for m in range(4)], hk))
                pe.wait_ge(s["hf_sig"], l + 1)
                done(features(c0 + L1c, [half(PA, m) for m in range(4)], hk))
                pe.wait_ge(s["hq_silu"], l + 1)
                arrived(c0 + L2c)
                w = view(c0 + L2c, KT, 160)
                for t in range(KT):
                    mm(PB[:, 0:S], w[:, t, 0:P], hk(t), t == 0, t == KT - 1)
                for t in range(KT):
                    last = mm(PB[64:96, 512:512 + S], w[:, t, P:160], hk(t), t == 0, t == KT - 1)
                done(last)
                pe.wait_ge(s["v_copied"], l + 1)
                done(features(c0 + GTc, [half(PC, m) for m in range(4)], hk))
                pe.wait_ge(s["lat1_copied"], l + 1)
                pe.wait_ge(s["lat2_copied"], l + 1)
                pe.wait_ge(s["hg_silu"], l + 1)
                sq = AR[:, 4 * 1024:4 * 1024 + 1280].rearrange("p (t n) -> p t n", t=5)
                for t in range(3):
                    mm(PD[:, 0:S], ones, sq[:, t, :], t == 0, t == 2)
                for t in range(3, 5):
                    last = mm(PD[:, 512:512 + S], ones, sq[:, t, :], t == 3, t == 4)
                last.then_inc(s["lat_sums"], 1)
                done(features(c0 + GTc + 1, [half(PA, m) for m in range(4)], hk))
                done(features(c0 + GTc + 2, [half(PB, m) for m in range(4)], hk))
                pe.wait_ge(s["gates_act"], 4 * l + 1)
                done(features(c0 + GTc + 3, [half(PC, m) for m in range(4)], hk))
                KD, KDT = blk(7), F[2]
                pe.wait_ge(s["kd_ready"], l + 1)
                pe.wait_ge(s["gates_act"], 4 * l + 2)
                for m in range(8):
                    last = pe.transpose(PA[:, m * P:m * P + P], KD[:, m * P:m * P + P], ident)
                last.then_inc(s["kd_turned"], 1)
                QE = [blk(5), blk(0)]
                KE = [blk(6), blk(1)]

                def level(n):
                    o = PB if n % 2 == 0 else PD
                    if n < 6:
                        pe.wait_ge(s["lvl_qk"], 6 * l + n + 1)
                    if n == 0:
                        pe.wait_ge(s["gates_act"], 4 * l + 3)
                    if n == 1:
                        pe.wait_ge(s["lat_std"], l + 1)
                    if n >= 2:
                        pe.wait_ge(s["lvl_masked"], 7 * l + n - 1)
                    q, k = (QE[0], KE[0]) if n < 6 else (QE[1], KE[1])
                    for m in range(8):
                        last = mm(o[:, m * P:m * P + P], k[:, m * P:m * P + P], q[:, m * P:m * P + P], True, True)
                    last.then_inc(s["lvl_score"], 1)

                level(0)
                VT = blk(9)
                pe.wait_ge(s["kdt_ready"], l + 1)
                pe.wait_ge(s["gates_act"], 4 * l + 4)
                for c in range(3):
                    lo = 64 * (c % 2)
                    for h in range(4):
                        o = (PA[:, 512 * c:512 * c + 512] if c < 2 else PC[:, 0:512])[:, h * P:h * P + P]
                        last = mm(o, KDT[lo:lo + 64, (2 * h + c // 2) * P:(2 * h + c // 2) * P + P],
                                  VT[lo:lo + 64, 512 * (c // 2) + h * P:512 * (c // 2) + h * P + P], True, True)
                last.then_inc(s["u_ready"], 1)
                for n in range(1, 7):
                    level(n)
                ST = XH[:, 2048:2048 + 1536]
                pe.wait_ge(s["lvl_added"], l + 1)
                pe.wait_ge(s["states_ready"], l + 1)
                pe.wait_ge(s["qb_ready"], l + 1)
                ATT, QB = blk(10), blk(8)
                for h in range(4):
                    for m in range(2):
                        mm(PA[:, h * S + m * P:h * S + m * P + P], VT[:, 512 * m + h * P:512 * m + h * P + P],
                           ATT[:, (2 * h + m) * P:(2 * h + m) * P + P], m == 0, False, skip_group_check=True)
                    for c in range(1, 4):
                        last = mm(PA[:, h * S + c * CH:h * S + c * CH + CH], ST[:, 512 * (c - 1) + h * P:512 * (c - 1) + h * P + P],
                                  QB[:, h * S + c * CH:h * S + c * CH + CH], False, c == 3, skip_group_check=True)
                last.then_inc(s["o_ready"], 1)
                CL = XH[:, 4096:4096 + 1280].rearrange("p (t n) -> p t n", t=5)
                pe.wait_ge(s["latn_ready"], l + 1)
                pe.wait_ge(s["lvl_masked"], 7 * l + 7)
                arrived(c0 + QUc)
                w = view(c0 + QUc, 3, 768)
                for h in range(8):
                    o = (PC if h < 4 else PD)[0:DQK, (h % 4) * S:(h % 4) * S + S]
                    for t in range(3):
                        last = mm(o, w[:, t, h * DQK:h * DQK + DQK], CL[:, t, :], t == 0, t == 2)
                done(last)
                pe.wait_ge(s["o_copied"], l + 1)
                for m in range(2):
                    last = mm(PB[:, 512 * m:512 * m + 512], ones, F[2][:, 512 * m:512 * m + 512], True, True)
                last.then_inc(s["o_sums"], 1)
                arrived(c0 + KVc)
                w = view(c0 + KVc, 2, 1024)
                pe.wait_ge(s["o_std"], l + 1)
                for h in range(8):
                    o = (PA if h < 4 else PB)[0:NOPE, (h % 4) * S:(h % 4) * S + S]
                    for t in range(2):
                        mm(o, w[:, t, h * P:h * P + NOPE], CL[:, 3 + t, :], t == 0, t == 1)
                pe.wait_ge(s["q_copied"], l + 1)
                wv = w.rearrange("p t (h d) -> p t h d", d=P)
                for m in range(2):
                    for t in range(2):
                        last = mm(PC[:, 512 * m:512 * m + 512], CL[:, 3 + t, m * P:m * P + P],
                                  wv[:, t, :, NOPE:P], t == 0, t == 1)
                done(last)
                QH = AR[:, 4 * 1024:4 * 1024 + 9 * S]
                rot = CS[64:96, C_PR:C_PR + 32]
                for m in range(2):
                    mm(PD[64:96, 512 * m:512 * m + 512], rot, QH[64:96, 512 * m:512 * m + 512], True, True)
                pe.wait_ge(s["k_copied"], l + 1)
                for m in range(2):
                    mm(PA[64:96, 512 * m:512 * m + 512], rot, QH[64:96, 1024 + 512 * m:1536 + 512 * m], True, True)
                mm(PB[64:96, 0:S], rot, QH[64:96, 2048:2048 + S], True, True).then_inc(s["kr_turned"], 1)
                KH = AR[:, 7 * 1024:9 * 1024].rearrange("p (h n) -> p h n", h=8)
                Q3 = QH.rearrange("p (h n) -> p h n", h=9)
                units = [(0, 0, 8, 128), (1, 0, 4, 256), (1, 4, 4, 256)]
                V2 = blk(9)

                def scores(u):
                    qb, h0, nh, nk = units[u]
                    o = PA if u % 2 == 0 else PC
                    for h in range(nh):
                        last = mm(o[:, h * nk:h * nk + nk], Q3[0:DQK, h0 + h, qb * P:qb * P + P],
                                  KH[0:DQK, h0 + h, 0:nk], True, True)
                    last.then_inc(s["sc_ready"], 1)

                def weighted(u):
                    qb, h0, nh, nk = units[u]
                    pe.wait_ge(s["p_ready"], 3 * l + u + 1)
                    if u == 0:
                        pe.wait_ge(s["rope_done"], 2 * l + 2)
                    pr = blk(10)
                    for m in range(8):
                        last = pe.transpose(PB[:, m * P:m * P + P], pr[:, m * P:m * P + P], ident)
                    last.then_inc(s["p_turned"], 1)
                    pe.wait_ge(s["pt_ready"], 3 * l + u + 1)
                    pt = blk(0).rearrange("p (h k q) -> p h k q", h=nh, q=P)
                    for h in range(nh):
                        g = h0 + h
                        o = PD[64 * (g % 2):64 * (g % 2) + 64, (g // 2) * S + qb * P:(g // 2) * S + qb * P + P]
                        for k in range(nk // P):
                            last = mm(o, V2[:, 512 * k + g * 64:512 * k + g * 64 + 64], pt[:, h, k, :],
                                      k == 0, k == nk // P - 1)
                    last.then_inc(s["om_ready"], 1)

                pe.wait_ge(s["rope_done"], 2 * l + 2)
                pe.wait_ge(s["v2_copied"], l + 1)
                scores(0)
                scores(1)
                weighted(0)
                pe.wait_ge(s["sm_max"], 3 * l + 1)
                scores(2)
                weighted(1)
                weighted(2)
                pe.wait_ge(s["oa_ready"], l + 1)
                OA = F[3].rearrange("p (t n) -> p t n", t=4)
                OM = blk(2).rearrange("p (t n) -> p t n", t=4)
                pe.wait_ge(s["sm_max"], 3 * l + 3)
                done(features(c0 + BAc, [half(PA if m < 4 else PB, m % 4) for m in range(8)],
                              lambda t: OA[:, t, :], 4, 1024))
                pe.wait_ge(s["om_copied"], 3 * l + 3)
                done(features(c0 + BBc, [half(PC if m < 4 else PD, m % 4) for m in range(8)],
                              lambda t: OM[:, t, :], 4, 1024))
                MG = AR[:, 12 * 1024:14 * 1024].rearrange("p (t n) -> p t n", t=8)
                pe.wait_ge(s["merged_ready"], l + 1)
                done(features(c0 + WOc, [half(PA, m) for m in range(4)], lambda t: MG[:, t, :]))
                done(features(c0 + WOc + 1, [half(PB, m) for m in range(4)], lambda t: MG[:, t, :]))

                n = 2 * l + 1
                sums(n, H1, S)
                h_arrived(n)
                pe.wait_ge(s["router_in"], 16)
                for m in range(2):
                    for t in range(KT):
                        last = mm(PD[:, 512 + NE * m:512 + NE * m + NE], H1[:, t, m * P:m * P + P], WR[:, t, :],
                                  t == 0, t == KT - 1)
                last.then_inc(s["rt_ready"], 1)
                m0 = c0 + MOEc
                HE = [AR[:, (6 + j) * 1024:(7 + j) * 1024].rearrange("p (t n) -> p t n", t=4) for j in range(2)]

                def gate(c, e, i=0, wait=True):
                    if wait:
                        pe.wait_ge(s["sg_ready"], i * 2 + (16 * l + e))
                    done(features(c, [half(PA, m) for m in range(4)], hk, i=i))

                def up(c, e, i=0, wait=True):
                    if wait:
                        pe.wait_ge(s["gu_ready"], i * 2 + (16 * l + e))
                    done(features(c, [half(PB, m) for m in range(4)], hk, i=i))

                def down(c, e, i=0, parity=0):
                    arrived(c, i)
                    pe.wait_ge(s["he_ready"], i * 2 + (16 * l + e + 1))
                    w = view(c, 4, 1024)
                    for m in range(8):
                        for t in range(4):
                            last = mm(half(PC if m < 4 else PD, m % 4), w[:, t, m * P:m * P + P], HE[parity][:, t, :],
                                      False, False, skip_group_check=True)
                    done(last)

                gate(m0, 0, wait=False)
                up(m0 + 1, 0, wait=False)
                for g in range(4):
                    for m in range(2):
                        pe.wait_ge(s["diag_ready"], 8 * l + 2 * g + m + 1)
                        if g >= 1 and m == 0:
                            pe.wait_ge(s["cbc_copied"], 4 * l + g)
                        mm(PC[:, 512 * m:512 * m + 512], ones, blk(9 + m, 512), True, True).then_inc(s["cbc_ready"], 1)
                pe.wait_ge(s["cbc_copied"], 4 * l + 4)
                pe.wait_ge(s["rt_sig"], l + 1)
                pe.wait_ge(s["acc_zero"], l + 1)
                for q in (PC, PD):
                    for m in range(2):
                        mm(q[:, 512 * m:512 * m + 512], blk(11, 128), XH[:, 2048:2560], True, False, skip_group_check=True)
                with pe.Fori(0, 7) as i:
                    for j in range(2):
                        c = m0 + 2 + 3 * j
                        gate(c, 1 + j, i)
                        up(c + 1, 1 + j, i)
                        down(c + 2, j, i, j)
                gate(m0 + 44, 15)
                up(m0 + 45, 15)
                down(m0 + 46, 14, 0, 0)
                down(m0 + 47, 15, 0, 1)

            sums(4, H1, S)
            pe.wait_ge(s["const2_in"], 16)
            cB, cP = CS[:, C1_OVER + D_B64:C1_OVER + D_B64 + P], CS[:, C1_OVER + D_P64:C1_OVER + D_P64 + P]
            sums(5, H2, 512)
            h_arrived(5)

            def banks(n0):
                return [(PA, PB, PC, PD)[(n0 + k) // 2 % 4][:, ((n0 + k) % 2) * 512:((n0 + k) % 2) * 512 + 512]
                        for k in range(4)]
            h2k = lambda t: H2[:, t, :]
            done(features(WQKV, banks(0), h2k))
            done(features(WQKV + 1, banks(4), h2k))
            pe.wait_ge(s["wq_copied"], 2)
            arrived(WQKV + 2)
            w = view(WQKV + 2, KT, 512)
            for m in range(2):
                for t in range(KT):
                    mm(PA[:, 512 * m:512 * m + 512], w[:, t, m * P:m * P + P], h2k(t), t == 0, t == KT - 1)
            for m in range(4):
                for t in range(KT):
                    last = mm(PB[:, S * m:S * m + S], H2[:, t, m * P:m * P + P], w[:, t, 256:512], t == 0, t == KT - 1)
            done(last)
            QT = [AR[:, k * 1024:k * 1024 + 1024] for k in range(5)]
            for u in range(5):
                pe.wait_ge(s["wsq_ready"], u + 1)
                if u >= 1:
                    pe.wait_ge(s["wstd_ready"], u)
                for m in range(2):
                    last = mm(PC[:, 512 * m:512 * m + 512], cB, XH[:, 2048 * (u % 2) + 512 * m:2048 * (u % 2) + 512 * m + 512],
                              True, True)
                last.then_inc(s["wsum_ready"], 1)
                pe.wait_ge(s["wn_ready"], u + 1)
                if u >= 1:
                    pe.wait_ge(s["wroped"], u)
                for m in range(2):
                    last = mm(PD[:, S * m:S * m + S], cP, QT[u][:, 512 * m:512 * m + S], True, True)
                last.then_inc(s["wrot_ready"], 1)
            pe.wait_ge(s["wroped"], 5)
            for g in range(4):
                sel = CS[:, C1_OVER + D_SEL + P * (g % 2):C1_OVER + D_SEL + P * (g % 2) + P]
                o = (PA, PC)[g // 2][:, 512 * (g % 2):512 * (g % 2) + 512]
                last = mm(o, sel, QT[4][:, 512 * (g // 2):512 * (g // 2) + 512], True, True)
            last.then_inc(s["k_dup"], 1)
            KDUP = AR[:, 5 * 1024:7 * 1024].rearrange("p (g n) -> p g n", g=4)
            WV = blk(7).rearrange("p (t n) -> p t n", t=4)
            Q2 = AR[:, 0:4096].rearrange("p (t n) -> p t n", t=8)
            units = [(t, k) for t in range(8) for k in range(3)]

            def wscores(u):
                t, kind = units[u]
                g = t // 2
                o = (PA, PB)[u % 2]
                if u >= 2:
                    pe.wait_ge(s["sm_max"], 3 * DEPTH + u - 1)
                if kind < 2:
                    lo = 64 * kind
                    for b in range(2):
                        last = mm(o[:, 512 * b:512 * b + 512], Q2[lo:lo + 64, t, b * P:b * P + P],
                                  KDUP[lo:lo + 64, g, :], True, True)
                else:
                    for h in range(2):
                        for b in range(2):
                            last = mm(o[:, 512 * h + S * b:512 * h + S * b + S],
                                      Q2[64 * h:64 * h + 64, t, S + b * P:S + b * P + P],
                                      KDUP[64 * h:64 * h + 64, g, S:2 * S], True, True)
                last.then_inc(s["sc_ready"], 1)

            def wweighted(u):
                t, kind = units[u]
                g = t // 2
                pe.wait_ge(s["p_ready"], 3 * DEPTH + u + 1)
                if u >= 1:
                    pe.wait_ge(s["pt_ready"], 3 * DEPTH + u)
                pr = blk(12 + u % 2)
                for m in range(8):
                    if kind < 2:
                        src = pr[:, (m % 2) * 512 + (m // 2) * P:(m % 2) * 512 + (m // 2) * P + P]
                    else:
                        h, k, b = m // 4, (m // 2) % 2, m % 2
                        src = pr[:, 512 * h + S * b + P * k:512 * h + S * b + P * k + P]
                    last = pe.transpose(PC[:, m * P:m * P + P], src, ident)
                last.then_inc(s["p_turned"], 1)
                pe.wait_ge(s["pt_ready"], 3 * DEPTH + u + 1)
                pt = blk(14 + u % 2)
                o = PD[:, 512 * (t % 2):512 * (t % 2) + 512]
                if kind == 0 and t >= 2:
                    pe.wait_ge(s["ot_copied"], t - 1)
                if kind < 2:
                    for k in range(4):
                        last = mm(o[64 * kind:64 * kind + 64, 0:S], WV[:, k, g * 64:g * 64 + 64],
                                  pt[:, S * k:S * k + S], k == 0, k == 3)
                else:
                    for h in range(2):
                        for k in range(2):
                            last = mm(o[64 * h:64 * h + 64, S:2 * S], WV[:, 2 + k, g * 64:g * 64 + 64],
                                      pt[:, 512 * h + S * k:512 * h + S * k + S], k == 0, k == 1)
                last.then_inc(s["ot_ready"], 1)

            pe.wait_ge(s["kdup_copied"], 1)
            pe.wait_ge(s["wv_copied"], 1)
            wscores(0)
            for u in range(24):
                if u + 1 < 24:
                    wscores(u + 1)
                wweighted(u)
            OT = AR[:, 8 * 1024:12 * 1024].rearrange("p (t n) -> p t n", t=8)
            pe.wait_ge(s["ot_copied"], 8)
            done(features(WWO, banks(0), lambda t: OT[:, t, :]))
            done(features(WWO + 1, banks(4), lambda t: OT[:, t, :]))

            def ffn(l, c0, n, H, N):
                sums(n, H, N)
                h_arrived(n)
                done_tiles = 22 * l
                for k in range(11):
                    c = c0 + k
                    arrived(c)
                    w = ring[c % RING][:, :].rearrange("p (t h n) -> p t h n", t=KT, h=2)
                    bs = banks(4 * (k % 2))
                    if k >= 2:
                        pe.wait_ge(s["cv_conv"], 2 * (done_tiles + 2 * (k - 1)))
                    for j in range(2):
                        for h in range(2):
                            for t in range(KT):
                                last = mm(bs[2 * j + h][:, 0:N], w[:, t, h, j * P:j * P + P], H[:, t, :],
                                          t == 0, t == KT - 1)
                    done(last)
                A = AR[:, 0:22 * N].rearrange("p (t n) -> p t n", n=N)
                for hf in range(2):
                    if hf == 0:
                        pe.wait_ge(s["cv_conv"], 2 * (done_tiles + 22))
                    for k, (a, nk) in enumerate(((0, 8), (8, 8), (16, 6))):
                        c = c0 + 11 + 3 * hf + k
                        arrived(c)
                        w = view(c, nk, 512)
                        pe.wait_ge(s["ff_act"], done_tiles + a + nk)
                        for m in range(4):
                            for t in range(nk):
                                last = mm(banks(4 * hf)[m][:, 0:N], w[:, t, m * P:m * P + P], A[:, a + t, :],
                                          a + t == 0, a + t == 21)
                        done(last)

            ffn(0, FF0, 6, H2, 512)
            HL = XH[:, 0:2048].rearrange("p (t n) -> p t n", t=8)
            sums(7, HL, S)
            h_arrived(7)
            hl = lambda t: HL[:, t, :]
            for hf in range(2):
                if hf:
                    pe.wait_ge(s["gc_copied"], 1)
                done(features(SCI + 3 * hf, [half(PA, m) for m in range(4)], hl))
                if hf:
                    pe.wait_ge(s["scv_ready"], 1)
                done(features(SCI + 3 * hf + 1, [half(PB, m) for m in range(4)], hl))
                done(features(SCI + 3 * hf + 2, [half((PC, PD)[hf], m) for m in range(4)], hl))
            Z = AR[:, 0:2048].rearrange("p (t n) -> p t n", t=8)
            pe.wait_ge(s["scz_ready"], 2)
            done(features(SCO, [half(PA, m) for m in range(4)], lambda t: Z[:, t, :]))
            done(features(SCO + 1, [half(PB, m) for m in range(4)], lambda t: Z[:, t, :]))
            ffn(1, FF1, 8, HL, S)

        @block.scalar
        def _(act):
            steps = [0]

            def step(ins):
                steps[0] += 1
                ins.then_inc(s["act_step"], 1)

            def settle():
                act.wait_ge(s["act_step"], steps[0])

            def multiplied(c):
                act.wait_ge(s["multiplied"], c + 1)

            A = act.activation
            act.wait_ge(s["vec_in"], 16)
            A(CACT[:, :, :, :].rearrange("p a t w -> p (a t w)"), VEC[:, V_C:V_C + 32], ACT.Silu).then_inc(s["cact_ready"], 1)
            act.wait_ge(s["lb_ready"], 1)
            A(LB[:, 0, :, :].rearrange("p a b -> p (a b)"), LB[:, 0, :, :].rearrange("p a b -> p (a b)"), ACT.Exp).then_inc(s["lb_ready"], 1)
            act.wait_ge(s["angle_ready"], 1)
            A(RT[0:DQK, :], RT[0:DQK, :], ACT.Sin).then_inc(s["rope_ready"], 1)

            def squares(n, X, H):
                if n == 0:
                    act.wait_ge(s["x_in"], 16)
                else:
                    act.wait_ge(s["x_done"], n)
                if n == 5:
                    act.wait_ge(s["ctx_in"], 16)
                A(H, X, ACT.Square).then_inc(s["squares_ready"], 1)

            def norm(n, X, H, N, a, l, which, ws):
                squares(n, X, H)
                act.wait_ge(s["sums_ready"], n + 1)
                A(RST[:, 0:N], PD[:, 0:N], ACT.Sqrt, scale=1.0 / D, bias=EPSC[:, 0:1]).then_inc(s["std_ready"], 1)
                act.wait_ge(s["scaled_ready"], h_count(n))
                if n == 0:
                    act.wait_ge(s["coef_ready"], 1)
                for t in range(4):
                    for w in range(ws):
                        sl = H[:, t, w * S:w * S + S]
                        ins = A(sl, sl, ACT.Identity, scale=COEF[:, a, l, which, t, w:w + 1],
                                bias=MOD[:, a, l, 24 * which + t, w:w + 1])
                        if t == 3 and w == ws - 1:
                            ins.then_inc(s["h_act"], 1)

            EE = blk(4)
            for l in range(DEPTH):
                c0 = first(l)
                norm(2 * l, X1, H1, S, 0, l, 0, 1)
                multiplied(c0 + HFc)
                A(EE, PA, ACT.Sigmoid).then_inc(s["hf_sig"], 1)
                multiplied(c0 + HQc)
                A(blk(0), PB, ACT.Silu).then_inc(s["hq_silu"], 1)
                multiplied(c0 + HIc)
                A(blk(9), PC, ACT.Copy).then_inc(s["v_copied"], 1)
                multiplied(c0 + HGc)
                A(blk(3), PD, ACT.Silu).then_inc(s["hg_silu"], 1)
                CLf = XH[:, 4096:4096 + 1280]
                SQ = AR[:, 4 * 1024:4 * 1024 + 1280]
                multiplied(c0 + L1c)
                A(CLf[:, 0:1024], PA, ACT.Copy)
                act.wait_ge(s["f_ready"], l + 1)
                A(SQ[:, 0:1024], PA, ACT.Square).then_inc(s["lat1_copied"], 1)
                multiplied(c0 + L2c)
                A(CLf[:, 1024:1280], PB[:, 0:S], ACT.Copy)
                A(KR, PB[64:96, 512:512 + S], ACT.Copy)
                A(SQ[:, 1024:1280], PB[:, 0:S], ACT.Square).then_inc(s["lat2_copied"], 1)
                A(blk(2), blk(2), ACT.Ln).then_inc(s["lnf_ready"], 1)
                multiplied(c0 + GTc)
                A(blk(12), PC, ACT.Sigmoid).then_inc(s["gates_act"], 1)
                multiplied(c0 + GTc + 1)
                A(blk(13), PA, ACT.Sigmoid).then_inc(s["gates_act"], 1)
                multiplied(c0 + GTc + 2)
                A(blk(14), PB, ACT.Sigmoid).then_inc(s["gates_act"], 1)
                act.wait_ge(s["lat_sums"], l + 1)
                A(LRS[:, 0, :], PD[:, 0:S], ACT.Sqrt, scale=1.0 / QL, bias=EPSC[:, 0:1])
                A(LRS[:, 1, :], PD[:, 512:512 + S], ACT.Sqrt, scale=1.0 / KVL, bias=EPSC[:, 0:1]).then_inc(s["lat_std"], 1)
                act.wait_ge(s["kdiff_ready"], l + 1)
                A(blk(7), blk(7), ACT.Exp).then_inc(s["kexp_ready"], 1)
                A(DEC, BLAST, ACT.Exp).then_inc(s["dec_ready"], 1)
                A(blk(8), blk(2), ACT.Exp).then_inc(s["eb_ready"], 1)
                for n in range(6):
                    act.wait_ge(s["lvl_diff"], 6 * l + n + 1)
                    A(EE, EE, ACT.Exp).then_inc(s["lvl_exp"], 1)
                    if n == 0:
                        act.wait_ge(s["kd_turned"], l + 1)
                        A(F[2], PA, ACT.Copy).then_inc(s["kdt_ready"], 1)
                    if n == 1:
                        multiplied(c0 + GTc + 3)
                        A(blk(15), PC, ACT.Sigmoid).then_inc(s["gates_act"], 1)
                act.wait_ge(s["o_ready"], l + 1)
                A(F[3], PA, ACT.Copy)
                A(F[2], PA, ACT.Square).then_inc(s["o_copied"], 1)
                multiplied(c0 + QUc)
                QH = AR[:, 4 * 1024:4 * 1024 + 9 * S]
                A(QH[0:DQK, 0:1024], PC[0:DQK, :], ACT.Copy)
                A(QH[64:96, 2048:2048 + S], KR, ACT.Copy)
                A(QH[0:DQK, 1024:2048], PD[0:DQK, :], ACT.Copy).then_inc(s["q_copied"], 1)
                act.wait_ge(s["o_sums"], l + 1)
                A(blk(11), PB, ACT.Sqrt, scale=1.0 / HG_D, bias=EPSC[:, 0:1]).then_inc(s["o_std"], 1)
                multiplied(c0 + KVc)
                A(AR[0:NOPE, 7 * 1024:8 * 1024], PA[0:NOPE, :], ACT.Copy)
                A(AR[0:NOPE, 8 * 1024:9 * 1024], PB[0:NOPE, :], ACT.Copy).then_inc(s["k_copied"], 1)
                A(blk(9), PC, ACT.Copy).then_inc(s["v2_copied"], 1)

                def soft(u, nh, nk):
                    act.wait_ge(s["sm_max"], 3 * l + u + 1)
                    pr = blk(10)
                    for h in range(nh):
                        ins = A(pr[:, h * nk:h * nk + nk], pr[:, h * nk:h * nk + nk], ACT.Exp,
                                bias=NM[:, h:h + 1], accum_out=RSUM[:, h:h + 1])
                    ins.then_inc(s["sm_exp"], 1)

                def turned(u):
                    act.wait_ge(s["p_turned"], 3 * l + u + 1)
                    A(blk(0), PB, ACT.Copy).then_inc(s["pt_ready"], 1)
                OMf = blk(2).rearrange("p (t n) -> p t n", t=4)
                for u, (nh, nk) in enumerate(((8, 128), (4, 256), (4, 256))):
                    soft(u, nh, nk)
                    turned(u)
                    act.wait_ge(s["om_ready"], 3 * l + u + 1)
                    if u == 0:
                        o_, i_ = OMf[:, :, 0:P], PD.rearrange("p (t n) -> p t n", t=4)[:, :, 0:P]
                    else:
                        o_ = OMf[:, 2 * u - 2:2 * u, P:2 * P]
                        i_ = PD.rearrange("p (t n) -> p t n", t=4)[:, 2 * u - 2:2 * u, P:2 * P]
                    A(o_, i_, ACT.Copy).then_inc(s["om_copied"], 1)
                norm(2 * l + 1, X1, H1, S, 0, l, 1, 1)
                act.wait_ge(s["rt_ready"], l + 1)
                A(SCO_, PD[:, 512:512 + 2 * NE], ACT.Sigmoid).then_inc(s["rt_sig"], 1)
                m0 = c0 + MOEc
                SG = [blk(4), blk(5)]
                multiplied(m0)
                A(SG[0], PA, ACT.Silu).then_inc(s["sg_ready"], 1)
                CB = AR[:, 0:4096].rearrange("p (e t) -> p e t", e=16)
                for g in range(4):
                    act.wait_ge(s["cbc_ready"], 8 * l + 2 * g + 2)
                    for m in range(2):
                        ins = A(CB[:, 4 * g:4 * g + 4, m * P:m * P + P],
                                PC[:, 512 * m:512 * m + 512].rearrange("p (e t) -> p e t", e=4), ACT.Copy)
                    ins.then_inc(s["cbc_copied"], 1)
                with act.Fori(0, 7) as i:
                    for j in range(2):
                        act.wait_ge(s["gu_ready"], i * 2 + (16 * l + 1 + j))
                        act.wait_ge(s["multiplied"], i * 6 + (m0 + 2 + 3 * j + 1))
                        A(SG[(1 + j) % 2], PA, ACT.Silu).then_inc(s["sg_ready"], 1)
                multiplied(m0 + 44)
                act.wait_ge(s["gu_ready"], 16 * l + 14)
                A(SG[1], PA, ACT.Silu).then_inc(s["sg_ready"], 1)

            squares(4, X1, H1)
            act.wait_ge(s["sums_ready"], 5)
            A(RST[:, 0:S], PD[:, 0:S], ACT.Sqrt, scale=1.0 / D, bias=EPSC[:, 0:1]).then_inc(s["std_ready"], 1)
            norm(5, X2, H2, 512, 1, 0, 0, 2)
            QT = [AR[:, k * 1024:k * 1024 + 1024] for k in range(5)]
            pairs = [(PA, WQKV), (PB, WQKV), (PC, WQKV + 1), (PD, WQKV + 1), (PA, WQKV + 2)]
            for u in range(4):
                multiplied(pairs[u][1])
                A(QT[u], pairs[u][0], ACT.Copy).then_inc(s["wq_copied"], 1)
            multiplied(WQKV + 2)
            A(blk(7), PB, ACT.Copy).then_inc(s["wv_copied"], 1)
            A(QT[4], PA, ACT.Copy).then_inc(s["wq_copied"], 1)
            del pairs

            def wsquare(u):
                act.wait_ge(s["wq_copied"], u + 1)
                if u >= 2:
                    act.wait_ge(s["wsum_ready"], u - 1)
                A(XH[:, 2048 * (u % 2):2048 * (u % 2) + 1024], QT[u], ACT.Square).then_inc(s["wsq_ready"], 1)
            for u in range(5):
                if u == 0:
                    wsquare(0)
                if u + 1 < 5:
                    wsquare(u + 1)
                act.wait_ge(s["wsum_ready"], u + 1)
                if u >= 1:
                    act.wait_ge(s["wn_ready"], u)
                A(blk(8), PC, ACT.Sqrt, scale=1.0 / WHD, bias=EPSC[:, 0:1]).then_inc(s["wstd_ready"], 1)
            act.wait_ge(s["k_dup"], 1)
            A(blk(5), PA, ACT.Copy)
            A(blk(6), PC, ACT.Copy).then_inc(s["kdup_copied"], 1)

            def wsoft(u):
                t, kind = u // 3, u % 3
                act.wait_ge(s["sm_max"], 3 * DEPTH + u + 1)
                pr = blk(12 + u % 2)
                if kind < 2:
                    for b in range(2):
                        A(pr[:, 512 * b:512 * b + 512], pr[:, 512 * b:512 * b + 512], ACT.Exp,
                          bias=WNM[:, u % 2, b:b + 1], accum_out=WRS[:, u % 2, b:b + 1])
                    h = 2 * t + kind
                    A(WES[:, u % 2, 0:2], WNM[:, u % 2, 0:2], ACT.Exp,
                      bias=VEC[:, V_SINK + h:V_SINK + h + 1]).then_inc(s["sm_exp"], 1)
                else:
                    for b in range(4):
                        A(pr[:, S * b:S * b + S], pr[:, S * b:S * b + S], ACT.Exp,
                          bias=WNM[:, u % 2, b:b + 1], accum_out=WRS[:, u % 2, b:b + 1])
                    for h in range(2):
                        ins = A(WES[:, u % 2, 2 * h:2 * h + 2], WNM[:, u % 2, 2 * h:2 * h + 2], ACT.Exp,
                                bias=VEC[:, V_SINK + 2 * t + h:V_SINK + 2 * t + h + 1])
                    ins.then_inc(s["sm_exp"], 1)

            OT = AR[:, 8 * 1024:12 * 1024].rearrange("p (t n) -> p t n", t=8)
            wsoft(0)
            for u in range(24):
                if u + 1 < 24:
                    wsoft(u + 1)
                act.wait_ge(s["p_turned"], 3 * DEPTH + u + 1)
                if u >= 2:
                    act.wait_ge(s["ot_ready"], u - 1)
                A(blk(14 + u % 2), PC, ACT.Copy).then_inc(s["pt_ready"], 1)
                if u % 3 == 0 and u:
                    t = u // 3 - 1
                    act.wait_ge(s["ot_ready"], 3 * t + 3)
                    A(OT[:, t, :], PD[:, 512 * (t % 2):512 * (t % 2) + 512], ACT.Copy).then_inc(s["ot_copied"], 1)
            act.wait_ge(s["ot_ready"], 24)
            A(OT[:, 7, :], PD[:, 512:1024], ACT.Copy).then_inc(s["ot_copied"], 1)

            def bank(k):
                return (PA, PB, PC, PD)[k // 2][:, (k % 2) * 512:(k % 2) * 512 + 512]

            def ffn(l, c0, n, X, H, N):
                norm(n, X, H, N, 1, l, 1, N // S)
                for j in range(22):
                    b0 = (4 * ((j // 2) % 2) + 2 * (j % 2))
                    multiplied(c0 + j // 2)
                    tmp = CVT[j % 2]
                    if j >= 2:
                        act.wait_ge(s["ff_act"], 22 * l + j - 1)
                    for h in range(2):
                        w1 = VEC[:, V_FC + 132 * l + 44 + 22 * h + j:V_FC + 132 * l + 44 + 22 * h + j + 1]
                        A(tmp[:, h, 0:N], bank(b0 + h)[:, 0:N], ACT.Copy, scale=w1).then_inc(s["cv_mid"], 1)
                    act.wait_ge(s["cv_conv"], 2 * (22 * l + j) + 1)
                    A(tmp[:, 0, 0:N], tmp[:, 0, 0:N], ACT.Silu).then_inc(s["cv_silu"], 1)
            ffn(0, FF0, 6, X2, H2, 512)
            HL = XH[:, 0:2048].rearrange("p (t n) -> p t n", t=8)
            XL = X2[:, :, 0:S]
            norm(7, XL, HL, S, 1, 1, 0, 1)
            GC, CV = blk(2), blk(3)
            for hf in range(2):
                if hf:
                    act.wait_ge(s["scv_ready"], 1)
                multiplied(SCI + 3 * hf)
                A(GC, PA, ACT.Copy).then_inc(s["gc_copied"], 1)
                act.wait_ge(s["scv_ready"], hf + 1)
                if hf:
                    act.wait_ge(s["scz_ready"], 1)
                for m in range(4):
                    w1 = VEC[:, V_SC + 8 + 4 * hf + m:V_SC + 8 + 4 * hf + m + 1]
                    ins = A(blk(5)[:, m * S:m * S + S], CV[:, m * S:m * S + S], ACT.Copy, scale=w1)
                ins.then_inc(s["sc_mid"], 1)
            ffn(1, FF1, 8, XL, HL, S)

        @block.vector
        def _(dve):
            steps = [0]

            def step(ins):
                steps[0] += 1
                ins.then_inc(s["dve_step"], 1)

            def settle():
                dve.wait_ge(s["dve_step"], steps[0])

            def link(ins):
                step(ins)
                settle()

            def multiplied(c):
                dve.wait_ge(s["multiplied"], c + 1)

            V = dve
            V.memset(EPSC[:, :], EPS)
            V.wait_ge(s["vec_in"], 16)
            L0, L1 = VEC[:, V_LB:V_LB + 4], VEC[:, V_LB + 4:V_LB + 8]
            link(V.tensor_tensor(LB[:, 1, 0, :], L0, L1, ALU.max))
            link(V.tensor_tensor(LB[:, 0, 0, :], L0, LB[:, 1, 0, :], ALU.subtract))
            V.tensor_tensor(LB[:, 0, 1, :], L1, LB[:, 1, 0, :], ALU.subtract).then_inc(s["lb_ready"], 1)
            V.wait_ge(s["lb_ready"], 2)
            link(V.tensor_tensor(LB[:, 1, 0, :], LB[:, 0, 0, :], LB[:, 0, 1, :], ALU.add))
            link(V.reciprocal(LB[:, 1, 1, :], LB[:, 1, 0, :]))
            for l in range(2):
                link(V.tensor_tensor(LB[:, 0, l, :], LB[:, 0, l, :], LB[:, 1, 1, :], ALU.mult))
            link(V.tensor_tensor(LB[:, 1, 0, :], LB[:, 0, 0, :], LB[:, 0, 1, :], ALU.add))
            link(V.tensor_tensor(LB[:, 0, 1, :], LB[:, 1, 0, :], LB[:, 0, 0, :], ALU.subtract))
            link(V.tensor_tensor(LB[:, 0, 0, :], LB[:, 0, 0, :], LB[:, 0, 0, :], ALU.subtract))
            for l in range(2):
                link(V.tensor_scalar(LB[:, 1, l, :], LB[:, 0, l, :], -1.0, 1.0, ALU.mult, ALU.add))
            V.wait_ge(s["pos_in"], 16)
            V.wait_ge(s["const1_in"], 16)
            ang, kk = ANG, KK
            link(V.tensor_copy(kk, POS.bitcast(I32)))
            link(V.tensor_scalar(ang, kk, CS[0:DQK, C_INV:C_INV + 1], None, ALU.mult))
            two_pi = 2.0 * np.pi
            p1 = 6.28125
            p2 = float(np.float32(np.round((two_pi - p1) * 2 ** 22) / 2 ** 22))
            p3 = float(np.float32(two_pi - p1 - p2))
            magic = float(1.5 * 2 ** 23)
            for k, off in enumerate((0.25, 0.0)):
                r = RT[0:DQK, k * S:k * S + S]
                link(V.tensor_scalar(kk, ang, float(1.0 / two_pi), off, ALU.mult, ALU.add))
                link(V.tensor_scalar(kk, kk, magic, None, ALU.add))
                link(V.tensor_scalar(kk, kk, -magic, None, ALU.add))
                link(V.scalar_tensor_tensor(r, kk, -p1, ang, ALU.mult, ALU.add))
                link(V.scalar_tensor_tensor(r, kk, -p2, r, ALU.mult, ALU.add))
                link(V.scalar_tensor_tensor(r, kk, -p3, r, ALU.mult, ALU.add))
                if off:
                    link(V.tensor_scalar(r, r, float(np.pi / 2), None, ALU.add))
                ins = V.tensor_scalar(r, r, 3.1415925, -3.1415925, ALU.min, ALU.max)
                if k:
                    ins.then_inc(s["angle_ready"], 1)
                else:
                    link(ins)
            COS, SIN = RT[64:96, 0:S], RT[64:96, S:2 * S]
            V.wait_ge(s["multiplied"], ADA)
            b = VEC[:, V_ADAB:V_ADAB + 192].rearrange("p (n a) -> p n a", a=1).to_broadcast([P, 192, 2])
            link(V.tensor_tensor(MOD[:, :, :, :, :].rearrange("p a l n w -> p (a l n) w"),
                                 PA[:, 0:384].rearrange("p (n w) -> p n w", w=2), b, ALU.add))
            for a in range(2):
                for l in range(DEPTH):
                    for k in range(2):
                        g0 = V_NG + ((a * 2 + l) * 2 + k) * 8
                        g = VEC[:, g0:g0 + 8].rearrange("p (n a) -> p n a", a=1).to_broadcast([P, 8, 2])
                        ins = V.scalar_tensor_tensor(COEF[:, a, l, k, :, :], MOD[:, a, l, 24 * k + 8:24 * k + 16, :], 1.0,
                                                     g, ALU.add, ALU.mult)
            ins.then_inc(s["coef_ready"], 1)
            V.wait_ge(s["coef_ready"], 1)

            def norm(n, X, H, N, a, l, which, ws):
                V.wait_ge(s["std_ready"], n + 1)
                link(V.reciprocal(RST[:, 0:N], RST[:, 0:N]))
                r = RST[:, 0:N].rearrange("p (a n) -> p a n", a=1).to_broadcast([P, KT, N])
                V.tensor_tensor(H, X, r, ALU.mult).then_inc(s["scaled_ready"], 1)
                V.wait_ge(s["scaled_ready"], h_count(n))
                for t in range(4, 8):
                    for w in range(ws):
                        sl = H[:, t, w * S:w * S + S]
                        ins = V.tensor_scalar(sl, sl, COEF[:, a, l, which, t, w:w + 1],
                                              MOD[:, a, l, 24 * which + t, w:w + 1], ALU.mult, ALU.add)
                ins.then_inc(s["h_dve"], 1)

            def residual(X, ts, a, l, col, w=0):
                for n, (t, q) in enumerate(ts):
                    ins = V.scalar_tensor_tensor(X[:, t, :], q, MOD[:, a, l, col + t, w:w + 1], X[:, t, :], ALU.mult, ALU.add)
                return ins

            EE = blk(4)
            T = blk(11)
            MK = float(2.0 ** 64 - 2.0 ** 40)
            for l in range(DEPTH):
                c0 = first(l)
                norm(2 * l, X1, H1, S, 0, l, 0, 1)
                RM, EE2 = blk(11), blk(8)
                link(V.memset(RM, 1.0))
                step(V.memset(RM.rearrange("p (c n) -> p c n", n=CH)[:, :, 0:1], 0.0))
                V.wait_ge(s["hf_sig"], l + 1)
                for h in range(4):
                    step(V.tensor_scalar(blk(2)[:, h * S:h * S + S], EE[:, h * S:h * S + S],
                                         LB[:, 1, l, h:h + 1], LB[:, 0, l, h:h + 1], ALU.mult, ALU.add))
                settle()
                step(V.tensor_scalar(blk(1), blk(2), -1.0, 1.0, ALU.mult, ALU.add))
                link(V.tensor_scalar(EE2, blk(2), float(2.0 ** -60), MK, ALU.is_lt, ALU.mult))
                V.scalar_tensor_tensor(blk(2), EE2, 1.0, blk(2), ALU.add, ALU.mult).then_inc(s["f_ready"], 1)
                V.wait_ge(s["hq_silu"], l + 1)
                V.tensor_scalar(blk(0), blk(0), float(HG_D ** -0.5), None, ALU.mult).then_inc(s["hq_scaled"], 1)
                V.wait_ge(s["lnf_ready"], l + 1)
                link(V.scalar_tensor_tensor(blk(2), EE2, -float(np.log1p(MK) / MK), blk(2), ALU.mult, ALU.add))
                B = blk(2)
                link(V.tensor_tensor_scan(B, RM, B, 0.0, ALU.mult, ALU.add))
                B4 = B.rearrange("p (c n) -> p c n", n=CH)
                link(V.tensor_copy(BLAST, B4[:, :, CH - 1]))
                bl = BLAST.rearrange("p (c a) -> p c a", a=1).to_broadcast([P, 16, CH])
                V.tensor_tensor(blk(7).rearrange("p (c n) -> p c n", n=CH), bl, B4, ALU.subtract).then_inc(s["kdiff_ready"], 1)
                V.wait_ge(s["lat_std"], l + 1)
                link(V.reciprocal(LRS[:, :, :].rearrange("p a n -> p (a n)"), LRS[:, :, :].rearrange("p a n -> p (a n)")))
                CL = XH[:, 4096:4096 + 1280].rearrange("p (t n) -> p t n", t=5)
                for t in range(5):
                    ins = V.scalar_tensor_tensor(CL[:, t, :], CL[:, t, :], VEC[:, V_CL + 5 * l + t:V_CL + 5 * l + t + 1],
                                                 LRS[:, t // 3, :], ALU.mult, ALU.mult)
                ins.then_inc(s["latn_ready"], 1)
                V.wait_ge(s["kexp_ready"], l + 1)
                V.tensor_tensor(blk(7), blk(7), blk(1), ALU.mult).then_inc(s["kd_ready"], 1)

                def diff(n):
                    hs = LEVELS[n]
                    nb = 1024 // (2 * hs)
                    b3 = B.rearrange("p (c n) -> p c n", n=2 * hs)
                    e3 = EE.rearrange("p (c n) -> p c n", n=2 * hs)
                    ref = b3[:, :, hs - 1:hs].to_broadcast([P, nb, hs])
                    if n == 0:
                        V.wait_ge(s["lat_sums"], l + 1)
                    else:
                        V.wait_ge(s["lvl_qk"], 6 * l + n)
                    V.tensor_tensor(e3[:, :, hs:2 * hs], b3[:, :, hs:2 * hs], ref, ALU.subtract)
                    V.tensor_tensor(e3[:, :, 0:hs], ref, b3[:, :, 0:hs], ALU.subtract).then_inc(s["lvl_diff"], 1)

                def qk(n):
                    if n >= 1:
                        V.wait_ge(s["lvl_score"], 7 * l + n)
                    V.wait_ge(s["lvl_exp"], 6 * l + n + 1)
                    V.tensor_tensor(blk(5), blk(0), EE, ALU.mult)
                    V.tensor_tensor(blk(6), blk(1), EE, ALU.mult).then_inc(s["lvl_qk"], 1)

                def masked(n):
                    if n == 0:
                        V.wait_ge(s["levels_in"], 16)
                    o = PB if n % 2 == 0 else PD
                    V.wait_ge(s["lvl_score"], 7 * l + n + 1)
                    mk = LVM[:, P * n:P * n + P].rearrange("p (a n) -> p a n", a=1).to_broadcast([P, 8, P])
                    dst = blk(10) if n == 0 else T
                    V.tensor_tensor(dst.rearrange("p (c n) -> p c n", n=P), o.rearrange("p (c n) -> p c n", n=P),
                                    mk, ALU.mult).then_inc(s["lvl_masked"], 1)
                    V.wait_ge(s["lvl_masked"], 7 * l + n + 1)
                    if n:
                        ins = V.tensor_tensor(blk(10), blk(10), T, ALU.add)
                        if n == 6:
                            ins.then_inc(s["lvl_added"], 1)
                        else:
                            link(ins)

                diff(0)
                qk(0)
                V.wait_ge(s["eb_ready"], l + 1)
                V.tensor_tensor(blk(8), blk(8), blk(0), ALU.mult).then_inc(s["qb_ready"], 1)
                for n in range(6):
                    if n < 5:
                        diff(n + 1)
                        if n == 1:
                            V.wait_ge(s["u_ready"], l + 1)
                            V.wait_ge(s["dec_ready"], l + 1)
                            ST = XH[:, 2048:2048 + 1536]
                            link(V.tensor_copy(ST[:, 0:512], PA[:, 0:512]))
                            for c in (1, 2):
                                src = PA[:, 512:1024] if c == 1 else PC[:, 0:512]
                                for h in range(4):
                                    ins = V.scalar_tensor_tensor(
                                        ST[:, 512 * c + h * P:512 * c + h * P + P],
                                        ST[:, 512 * (c - 1) + h * P:512 * (c - 1) + h * P + P],
                                        DEC[:, 4 * h + c:4 * h + c + 1], src[:, h * P:h * P + P], ALU.mult, ALU.add)
                                    if c == 1:
                                        step(ins)
                                settle()
                            ins.then_inc(s["states_ready"], 1)
                        masked(n)
                        qk(n + 1)
                    else:
                        masked(5)
                masked(6)
                V.wait_ge(s["o_std"], l + 1)
                link(V.reciprocal(T, T))
                link(V.tensor_tensor(T, T, blk(3), ALU.mult))
                for h in range(4):
                    sl = slice(h * S, h * S + S)
                    ins = V.scalar_tensor_tensor(F[3][:, sl], F[3][:, sl], VEC[:, V_HG + 4 * l + h:V_HG + 4 * l + h + 1],
                                                 T[:, sl], ALU.mult, ALU.mult)
                ins.then_inc(s["oa_ready"], 1)
                QH = AR[:, 4 * 1024:4 * 1024 + 9 * S].rearrange("p (h n) -> p h n", h=9)
                KH = AR[:, 7 * 1024:9 * 1024].rearrange("p (h n) -> p h n", h=8)
                V.wait_ge(s["kr_turned"], l + 1)
                V.wait_ge(s["rope_ready"], 1)
                V.wait_ge(s["q_copied"], l + 1)
                tmp = blk(0)[64:96, :].rearrange("p (h n) -> p h n", h=4)

                def wide(a, n):
                    return a.rearrange("p (a n) -> p a n", a=1).to_broadcast([ROPE, n, S])
                for k, (src, n) in enumerate(((PD, 4), (PA, 4), (PB, 1))):
                    link(V.tensor_tensor(tmp[:, 0:n, :], src[64:96, 0:n * S].rearrange("p (h n) -> p h n", h=n),
                                         wide(SIN, n), ALU.mult))
                    q = QH[64:96, 4 * k:4 * k + n, :]
                    link(V.tensor_tensor(q, q, wide(COS, n), ALU.mult))
                    link(V.tensor_tensor(q, q, tmp[:, 0:n, :], ALU.add))
                V.tensor_copy(KH[64:96, :, :], QH[64:96, 8:9, :].to_broadcast([ROPE, 8, S])).then_inc(s["rope_done"], 2)

                def softmax(u, nh, nk):
                    o = PA if u % 2 == 0 else PC
                    pr = blk(10).rearrange("p (h k) -> p h k", h=nh)
                    V.wait_ge(s["sc_ready"], 3 * l + u + 1)
                    if u:
                        V.wait_ge(s["p_turned"], 3 * l + u)
                    m0_ = C_MM if u == 0 else C_MM + 128
                    mk = CS[:, m0_:m0_ + nk].rearrange("p (a k) -> p a k", a=1).to_broadcast([P, nh, nk])
                    link(V.scalar_tensor_tensor(pr, o.rearrange("p (h k) -> p h k", h=nh), float(DQK ** -0.5), mk,
                                                ALU.mult, ALU.add))
                    link(V.tensor_reduce(NM[:, 0:nh], pr, axis=AXX, op=ALU.max))
                    V.tensor_scalar(NM[:, 0:nh], NM[:, 0:nh], -1.0, None, ALU.mult).then_inc(s["sm_max"], 1)
                    V.wait_ge(s["sm_exp"], 3 * l + u + 1)
                    link(V.reciprocal(RSUM[:, 0:nh], RSUM[:, 0:nh]))
                    V.tensor_tensor(pr, pr, RSUM[:, 0:nh].rearrange("p (h a) -> p h a", a=1).to_broadcast([P, nh, nk]),
                                    ALU.mult).then_inc(s["p_ready"], 1)
                softmax(0, 8, 128)
                softmax(1, 4, 256)
                softmax(2, 4, 256)
                multiplied(c0 + BAc)
                V.wait_ge(s["gates_act"], 4 * l + 4)
                V.tensor_tensor(blk(12), blk(12), PA, ALU.mult).then_inc(s["bra_mul"], 1)
                V.tensor_tensor(blk(13), blk(13), PB, ALU.mult).then_inc(s["bra_mul"], 1)
                multiplied(c0 + BBc)
                step(V.tensor_tensor(blk(14), blk(14), PC, ALU.mult))
                link(V.tensor_tensor(blk(15), blk(15), PD, ALU.mult))
                V.wait_ge(s["bra_mul"], 2 * l + 2)
                V.tensor_tensor(AR[:, 12 * 1024:14 * 1024], AR[:, 12 * 1024:14 * 1024], AR[:, 14 * 1024:16 * 1024],
                                ALU.add).then_inc(s["merged_ready"], 1)
                multiplied(c0 + WOc + 1)
                residual(X1, [(m, (PA, PB)[m // 4][:, (m % 4) * S:(m % 4) * S + S]) for m in range(8)], 0, l, 16)\
                    .then_inc(s["x_done"], 1)
                norm(2 * l + 1, X1, H1, S, 0, l, 1, 1)
                V.wait_ge(s["rt_sig"], l + 1)
                sc = SCO_.rearrange("p (m g e) -> p (m g) e", m=2, g=NG)
                bi = R_BI.rearrange("p (q e) -> p q e", e=EG)
                rb = VEC[:, V_RB:V_RB + 16].rearrange("p (a n) -> p a n", a=1).to_broadcast([P, 2, 16])
                link(V.tensor_tensor(R_BI.rearrange("p (m n) -> p m n", m=2), SCO_.rearrange("p (m n) -> p m n", m=2), rb, ALU.add))

                def rank(val, rk, ge, q, n):
                    link(V.memset(rk, 0.0))
                    for d in range(1, n):
                        lo, hi = val[:, :, 0:n - d], val[:, :, d:n]
                        g_ = ge[:, :, 0:n - d]
                        link(V.tensor_tensor(g_, lo, hi, ALU.is_ge))
                        link(V.tensor_tensor(rk[:, :, d:n], rk[:, :, d:n], g_, ALU.add))
                        link(V.tensor_scalar(g_, g_, -1.0, 1.0, ALU.mult, ALU.add))
                        link(V.tensor_tensor(rk[:, :, 0:n - d], rk[:, :, 0:n - d], g_, ALU.add))
                rk, ge = R_RK.rearrange("p (q e) -> p q e", e=EG), R_GE.rearrange("p (q e) -> p q e", e=EG)
                rank(bi, rk, ge, 8, EG)
                link(V.tensor_scalar(R_RK, R_RK, 2.0, None, ALU.is_lt))
                link(V.tensor_tensor(R_GE, R_BI, R_RK, ALU.mult))
                link(V.tensor_reduce(R_GS, ge, axis=AXX, op=ALU.add))
                gs = R_GS.rearrange("p (m g) -> p m g", m=2)
                gr = R_GR.rearrange("p (m g) -> p m g", m=2)
                gg = R_GG.rearrange("p (m g) -> p m g", m=2)
                rank(gs, gr, gg, 2, NG)
                link(V.tensor_scalar(R_GR, R_GR, 1.0, None, ALU.is_lt))
                link(V.tensor_tensor(rk, rk, R_GR.rearrange("p (q a) -> p q a", a=1).to_broadcast([P, 8, 4]), ALU.mult))
                link(V.tensor_tensor(R_GE, SCO_, R_RK, ALU.mult))
                link(V.tensor_reduce(R_DN, R_GE.rearrange("p (m n) -> p m n", m=2), axis=AXX, op=ALU.add))
                link(V.reciprocal(R_DN, R_DN))
                link(V.tensor_tensor(R_GE.rearrange("p (m n) -> p m n", m=2), R_GE.rearrange("p (m n) -> p m n", m=2),
                                     R_DN.rearrange("p (m a) -> p m a", a=1).to_broadcast([P, 2, 16]), ALU.mult))
                idb = ident.rearrange("p (a n) -> p a n", a=1).to_broadcast([P, 4, P])
                for g in range(4):
                    for m in range(2):
                        if g >= 1:
                            V.wait_ge(s["cbc_ready"], 8 * l + 2 * (g - 1) + m + 1)
                        cw = R_GE[:, 16 * m + 4 * g:16 * m + 4 * g + 4].rearrange("p (e a) -> p e a", a=1).to_broadcast([P, 4, P])
                        V.tensor_tensor(blk(9 + m, 512).rearrange("p (e n) -> p e n", e=4), idb, cw, ALU.mult)\
                            .then_inc(s["diag_ready"], 1)
                V.memset(blk(11, 128), 0.0).then_inc(s["acc_zero"], 1)
                m0 = c0 + MOEc
                SG, HE = [blk(4), blk(5)], [blk(6), blk(7)]

                def weigh(e, i, j, loop):
                    cu = m0 + 1 if e == 0 else (m0 + 45 if e == 15 else m0 + 2 + 3 * (e - 1) + 1)
                    V.wait_ge(s["multiplied"], i * 6 + (cu + 1))
                    V.wait_ge(s["sg_ready"], i * 2 + (16 * l + e + 1))
                    V.tensor_tensor(GU[j], SG[j], PB, ALU.mult).then_inc(s["gu_ready"], 1)
                    V.wait_ge(s["gu_ready"], i * 2 + (16 * l + e + 1))
                    cb = AR[:, bass.ds((i * 2 + e) * S, S)] if loop else AR[:, e * S:e * S + S]
                    V.tensor_tensor(HE[j].rearrange("p (t n) -> p t n", t=4), GU[j].rearrange("p (t n) -> p t n", t=4),
                                    cb.rearrange("p (a n) -> p a n", a=1).to_broadcast([P, 4, S]), ALU.mult)\
                        .then_inc(s["he_ready"], 1)
                V.wait_ge(s["cbc_copied"], 4 * l + 4)
                weigh(0, 0, 0, False)
                with V.Fori(0, 7) as i:
                    for j in range(2):
                        weigh(1 + j, i, (1 + j) % 2, True)
                weigh(15, 0, 1, False)
                multiplied(m0 + 47)
                residual(X1, [(m, (PC, PD)[m // 4][:, (m % 4) * S:(m % 4) * S + S]) for m in range(8)], 0, l, 40)\
                    .then_inc(s["x_done"], 1)

            V.wait_ge(s["std_ready"], 5)
            link(V.reciprocal(RST[:, 0:S], RST[:, 0:S]))
            for t in range(8):
                ins = V.scalar_tensor_tensor(X2[:, t, 0:S], X1[:, t, :], VEC[:, V_FIN + t:V_FIN + t + 1], RST[:, 0:S],
                                             ALU.mult, ALU.mult)
            ins.then_inc(s["x_done"], 1)
            norm(5, X2, H2, 512, 1, 0, 0, 2)
            V.wait_ge(s["const2_in"], 16)
            wcos = CS[:, C1_OVER + D_COS:C1_OVER + D_COS + S].rearrange("p (a n) -> p a n", a=1).to_broadcast([P, 2, S])
            wsin = CS[:, C1_OVER + D_SIN:C1_OVER + D_SIN + S].rearrange("p (a n) -> p a n", a=1).to_broadcast([P, 2, S])
            QT = [AR[:, k * 1024:k * 1024 + 1024] for k in range(5)]
            for u in range(5):
                gcol = V_WQ if u < 4 else V_WK
                V.wait_ge(s["wstd_ready"], u + 1)
                link(V.reciprocal(blk(8), blk(8)))
                V.scalar_tensor_tensor(QT[u], QT[u], VEC[:, gcol:gcol + 1], blk(8), ALU.mult, ALU.mult).then_inc(s["wn_ready"], 1)
                V.wait_ge(s["wrot_ready"], u + 1)
                q = QT[u].rearrange("p (t n) -> p t n", t=2)[:, :, 0:S]
                t_ = blk(9, 512).rearrange("p (t n) -> p t n", t=2)
                step(V.tensor_tensor(t_, PD[:, 0:512].rearrange("p (t n) -> p t n", t=2), wsin, ALU.mult))
                link(V.tensor_tensor(q, q, wcos, ALU.mult))
                V.tensor_tensor(q, q, t_, ALU.add).then_inc(s["wroped"], 1)

            def finish_softmax(u):
                nb = 2 if u % 3 < 2 else 4
                V.wait_ge(s["sm_exp"], 3 * DEPTH + u + 1)
                link(V.tensor_tensor(WRS[:, u % 2, 0:nb], WRS[:, u % 2, 0:nb], WES[:, u % 2, 0:nb], ALU.add))
                link(V.reciprocal(WRS[:, u % 2, 0:nb], WRS[:, u % 2, 0:nb]))
                p3 = blk(12 + u % 2).rearrange("p (b k) -> p b k", b=nb)
                V.tensor_tensor(p3, p3, WRS[:, u % 2, 0:nb].rearrange("p (b a) -> p b a", a=1)
                                .to_broadcast([P, nb, 1024 // nb]), ALU.mult).then_inc(s["p_ready"], 1)

            for u in range(24):
                t, kind = u // 3, u % 3
                o = (PA, PB)[u % 2]
                pr = blk(12 + u % 2)
                nb = 2 if kind < 2 else 4
                V.wait_ge(s["sc_ready"], 3 * DEPTH + u + 1)
                if u >= 2:
                    V.wait_ge(s["p_turned"], 3 * DEPTH + u - 1)
                if kind < 2:
                    o3, p3_ = o.rearrange("p (b k) -> p b k", b=2), pr.rearrange("p (b k) -> p b k", b=2)
                    mk = CS[:, C1_OVER + D_WM:C1_OVER + D_WM + 512].rearrange("p (b k) -> p b k", b=2)
                    step(V.scalar_tensor_tensor(p3_[:, :, 0:S], o3[:, :, 0:S], float(WHD ** -0.5), mk, ALU.mult, ALU.add))
                    link(V.tensor_scalar(p3_[:, :, S:512], o3[:, :, S:512], float(WHD ** -0.5), None, ALU.mult))
                else:
                    link(V.tensor_scalar(pr, o, float(WHD ** -0.5), None, ALU.mult))
                link(V.tensor_reduce(WNM[:, u % 2, 0:nb], pr.rearrange("p (b k) -> p b k", b=nb), axis=AXX, op=ALU.max))
                if kind < 2:
                    h = 2 * t + kind
                    V.tensor_scalar(WNM[:, u % 2, 0:2], WNM[:, u % 2, 0:2], VEC[:, V_SINK + h:V_SINK + h + 1], -1.0,
                                    ALU.max, ALU.mult).then_inc(s["sm_max"], 1)
                else:
                    for h in range(2):
                        ins = V.tensor_scalar(WNM[:, u % 2, 2 * h:2 * h + 2], WNM[:, u % 2, 2 * h:2 * h + 2],
                                              VEC[:, V_SINK + 2 * t + h:V_SINK + 2 * t + h + 1], -1.0, ALU.max, ALU.mult)
                    ins.then_inc(s["sm_max"], 1)
                if u:
                    finish_softmax(u - 1)
            finish_softmax(23)

            def bank(k):
                return (PA, PB, PC, PD)[k // 2][:, (k % 2) * 512:(k % 2) * 512 + 512]
            multiplied(WWO + 1)
            for w in range(2):
                ins = residual(X2[:, :, w * S:w * S + S], [(m, bank(m)[:, w * S:w * S + S]) for m in range(8)], 1, 0, 16, w)
            ins.then_inc(s["x_done"], 1)

            def ffn(l, c0, n, X, H, N):
                norm(n, X, H, N, 1, l, 1, N // S)
                A = AR[:, 0:22 * N].rearrange("p (t n) -> p t n", n=N)
                ws = N // S
                for j in range(22):
                    b0 = (4 * ((j // 2) % 2) + 2 * (j % 2))
                    tmp = CVT[j % 2]
                    for h in range(2):
                        V.wait_ge(s["cv_mid"], 2 * (22 * l + j) + h + 1)
                        x3 = bank(b0 + h)[:, 0:N].rearrange("p (w n) -> p w n", w=ws)
                        t3 = tmp[:, h, 0:N].rearrange("p (w n) -> p w n", w=ws)
                        wc = V_FC + 132 * l + 22 * h + j
                        link(V.scalar_tensor_tensor(t3[:, :, 1:S], x3[:, :, 0:S - 1], VEC[:, wc:wc + 1], t3[:, :, 1:S],
                                                    ALU.mult, ALU.add))
                        V.scalar_tensor_tensor(t3[:, :, 0:S - 1], x3[:, :, 1:S], VEC[:, wc + 88:wc + 89], t3[:, :, 0:S - 1],
                                               ALU.mult, ALU.add).then_inc(s["cv_conv"], 1)
                    V.wait_ge(s["cv_silu"], 22 * l + j + 1)
                    V.wait_ge(s["cv_conv"], 2 * (22 * l + j) + 2)
                    V.tensor_tensor(A[:, j, :], tmp[:, 0, 0:N], tmp[:, 1, 0:N], ALU.mult).then_inc(s["ff_act"], 1)
                multiplied(c0 + 16)
                for w in range(ws):
                    ins = residual(X[:, :, w * S:w * S + S], [(m, bank(m)[:, w * S:w * S + S]) for m in range(8)], 1, l, 40, w)
                ins.then_inc(s["x_done"], 1)
            ffn(0, FF0, 6, X2, H2, 512)
            HL = XH[:, 0:2048].rearrange("p (t n) -> p t n", t=8)
            XL = X2[:, :, 0:S]
            norm(7, XL, HL, S, 1, 1, 0, 1)
            GC, CV, CM = blk(2), blk(3), blk(5)
            for hf in range(2):
                multiplied(SCI + 3 * hf + 1)
                V.wait_ge(s["gc_copied"], hf + 1)
                V.tensor_tensor(CV, GC, PB, ALU.mult).then_inc(s["scv_ready"], 1)
                V.wait_ge(s["sc_mid"], hf + 1)
                for m in range(4):
                    wc = V_SC + 4 * hf + m
                    o = m * S
                    link(V.scalar_tensor_tensor(CM[:, o + 1:o + S], CV[:, o:o + S - 1], VEC[:, wc:wc + 1], CM[:, o + 1:o + S],
                                                ALU.mult, ALU.add))
                    step(V.scalar_tensor_tensor(CM[:, o:o + S - 1], CV[:, o + 1:o + S], VEC[:, wc + 16:wc + 17],
                                                CM[:, o:o + S - 1], ALU.mult, ALU.add))
                settle()
                multiplied(SCI + 3 * hf + 2)
                V.tensor_tensor(AR[:, 1024 * hf:1024 * hf + 1024], CM, (PC, PD)[hf], ALU.mult).then_inc(s["scz_ready"], 1)
            multiplied(SCO + 1)
            residual(XL, [(m, (PA, PB)[m // 4][:, (m % 4) * S:(m % 4) * S + S]) for m in range(8)], 1, 1, 16)\
                .then_inc(s["x_done"], 1)
            ffn(1, FF1, 8, XL, HL, S)


def level_masks():
    s_, t_ = np.arange(P)[:, None], np.arange(P)[None, :]
    out = [(s_ // (2 * h) == t_ // (2 * h)) & (s_ % (2 * h) < h) & (t_ % (2 * h) >= h) if h else s_ == t_ for h in LEVELS]
    return np.concatenate(out, 1).astype(np.float32)


def constants():
    c1 = np.zeros((P, N_C1), np.float32)
    c1[:, C_ID:C_ID + P] = np.eye(P)
    c1[:, C_ONE:C_ONE + P] = 1.0
    inv = np.float32(10000.0) ** (-np.arange(16, dtype=np.float32) / np.float32(16))
    c1[64:80, C_INV] = inv
    c1[80:96, C_INV] = inv
    for i in range(16):
        c1[80 + i, C_PR + i] = -1.0
        c1[64 + i, C_PR + 16 + i] = 1.0
    q, k = np.arange(P)[:, None] // CH, np.arange(S)[None, :] // CH
    c1[:, C_MM:C_MM + P] = np.where(k[:, :P] <= q, 0.0, -1e30)
    c1[:, C_MM + P:C_MM + P + S] = np.where(k <= q + 2, 0.0, -1e30)
    c2 = np.zeros((P, N_C2), np.float32)
    for i in range(2):
        c2[64 * i:64 * i + 64, D_B64 + 64 * i:D_B64 + 64 * i + 64] = 1.0
        for d in range(32):
            c2[64 * i + 32 + d, D_P64 + 64 * i + d] = -1.0
            c2[64 * i + d, D_P64 + 64 * i + 32 + d] = 1.0
        for h in range(2):
            c2[64 * i:64 * i + 64, D_SEL + P * i + 64 * h:D_SEL + P * i + 64 * h + 64] = np.eye(64)
    inv = np.float32(10000.0) ** (-np.arange(16, dtype=np.float32) / np.float32(16))
    tok = np.arange(S)
    ang = np.concatenate([(tok // 64)[None, :] * inv[:, None], (tok % 64)[None, :] * inv[:, None]], 0).astype(np.float32)
    c2[:, D_COS:D_COS + S] = np.tile(np.cos(ang), (4, 1))
    c2[:, D_SIN:D_SIN + S] = np.tile(np.sin(ang), (4, 1))
    q, k = np.arange(P)[:, None], np.arange(S)[None, :]
    for b in range(2):
        c2[:, D_WM + S * b:D_WM + S * b + S] = np.where(np.abs(q + P * b - k) <= 128, 0.0, -1e30)
    return c1, c2


def packed(i):
    def fm(a):
        a = np.asarray(a)
        return np.moveaxis(a.reshape(a.shape[:-1] + (a.shape[-1] // P, P)), -1, 0).reshape(P, -1)

    out = [fm(i["norm1_g"][0]), fm(i["norm2_g"][0]), fm(i["norm1_g"][1]), fm(i["norm2_g"][1]),
           fm(i["norm_mix_2"][0]), fm(i["norm_ffn_2"][0]), fm(i["norm_mix_2"][1]), fm(i["norm_ffn_2"][1]),
           fm(i["final_g"]), fm(i["hg_norm_g"]),
           fm(i["q_norm_g"][0]), fm(i["kv_norm_g"][0]), fm(i["q_norm_g"][1]), fm(i["kv_norm_g"][1]),
           fm(i["hg_lb_logits"]), np.tile(i["router_bias"][None, :], (P, 1))]
    for pair in ((i["c"][0], i["c"][0]), (i["c_2"][0], i["c_ctx_2"])):
        out.append(np.stack([fm(v) for v in pair], -1).reshape(P, -1))
    out += [fm(i["ada_b"]), fm(i["ada_b_2"]),
            np.tile(i["win_q_norm_2"][0], 2)[:, None], np.tile(i["win_k_norm_2"][0], 2)[:, None],
            np.tile(i["win_sink_2"], (P, 1)), fm(i["ffn_conv_2"]), fm(i["sc_conv_2"][0])]
    return np.ascontiguousarray(np.concatenate(out, 1))


WEIGHTS = ["ada_w", "ada_w_2", "w_in", "w_q_up", "w_kv_up", "w_br_a", "w_br_b", "w_out", "w_router", "w_gate", "w_up",
           "w_down"]
WEIGHTS_2 = {"win_w_qkv": "win_w_qkv_2", "win_w_o": "win_w_o_2", "ffn_w_up": "ffn_w_up_2", "ffn_w_down": "ffn_w_down_2",
             "sc_w_in": "sc_w_in_2", "sc_w_out": "sc_w_out_2"}


def kernel(**inputs):
    import concourse.bacc as _bacc
    from concourse.bass_utils import run_bass_kernel_spmd as _run

    i = {k: np.asarray(v) for k, v in inputs.items()}
    a = {n: i[n] for n in WEIGHTS}
    for n, m in WEIGHTS_2.items():
        a[n] = i[m][0] if i[m].shape[0] == 1 else i[m]
    c1, c2 = constants()
    import ml_dtypes
    a["levels"] = level_masks().astype(ml_dtypes.bfloat16)
    a["const1"], a["const2"], a["vec"] = c1, c2, packed(i)
    a["x"], a["ctx"] = i["x"][0].T, i["ctx_2"][0].T
    a["pos"] = np.tile(i["positions"].astype(np.int32), (DQK, 1))
    nc = _bacc.Bacc("TRN2", target_bir_lowering=False, num_devices=1)
    arrays, aps = {}, {}
    for n, v in a.items():
        v = np.ascontiguousarray(v)
        arrays["in_" + n] = v
        aps[n] = nc.dram_tensor("in_" + n, v.shape, mybir.dt.from_np(v.dtype), kind="ExternalInput").ap()
    out = nc.dram_tensor("out_0", (D, S), F32, kind="ExternalOutput").ap()
    stack_program(nc, aps, out)
    r = _run(nc, [arrays], core_ids=[0])
    return np.ascontiguousarray(r.results[0]["out_0"].T)[None]
```

```python
import concourse.bass as bass
from concourse import mybir
from contextlib import ExitStack
import numpy as np

F32 = mybir.dt.float32
I32 = mybir.dt.int32
ALU = mybir.AluOpType
ACT = mybir.ActivationFunctionType
AXX = mybir.AxisListType.X

P = 128
D = 1024
KT = D // P
S = 256
DEPTH = 2
EPS = 1e-6
RING, CHUNK = 6, 4096

HG_HEADS, HG_D, CH = 4, 128, 64
MLA_HEADS, NOPE, ROPE, MLA_V = 8, 64, 32, 64
DQK = NOPE + ROPE
QL, KVL = 384, 256
NE, NG, EG, DE = 16, 4, 4, 512
CAP = 96
WH, WKV, WHD = 16, 4, 64
FF = 2816
FT = FF // P
LEVELS = (32, 16, 8, 4, 2, 1, 0)

C_ID, C_ONE, C_INV, C_PR, C_MM, N_C1 = np.cumsum([0, 128, 128, 1, 32, 384]).tolist()
C_LV = N_C1
C_RT = C_LV + 64 * len(LEVELS)
C_U = C_RT + 512
C1_OVER = C_PR
D_B64, D_P64, D_SEL, D_COS, D_SIN, D_WM, N_C2 = np.cumsum([0, 128, 128, 256, 256, 256, 512]).tolist()
C_IOTA = C1_OVER + N_C2

V_NG = 0
V_FIN = V_NG + 64
V_HG = V_FIN + 8
V_CL = V_HG + 8
V_LB = V_CL + 10
V_RB = V_LB + 8
V_C = V_RB + 16
V_ADAB = V_C + 32
V_WQ = V_ADAB + 192
V_WK = V_WQ + 1
V_SINK = V_WK + 1
V_FC = V_SINK + 16
V_SC = V_FC + 264
N_V = V_SC + 24

PROJ = ["hf", "hq", "hi", "hg", "lat1", "lat2", "gt0", "gt1", "gt2", "gt3"]
LATE = ["bb", "wo0", "wo1"]
FIRST_ADA = [(0, 0, k) for k in range(4)]


def plan():
    order, before = [("ada", m) for m in FIRST_ADA], {}
    jobs = [[(0, 0, k) for k in range(4, 12)] + [(0, 1, k) for k in range(12)], [(1, 0, k) for k in range(12)]]
    for l in range(DEPTH):
        for n, name in enumerate(PROJ):
            count = 2 if l == 0 and n < 4 else (0 if l == 1 and n == 9 else 1)
            before[name, l] = [jobs[l].pop(0) for _ in range(count)]
            order += [("ada", m) for m in before[name, l]] + [(name, l)]
        order += [("qu", l), ("kv", l), ("ba", l)]
        for name in LATE:
            before[name, l] = [jobs[l].pop(0) for _ in range(2 - l)]
            order += [("ada", m) for m in before[name, l]] + [(name, l)]
        order += [("moe", l)] + [("", l)] * 47
    order += [("wqkv", k) for k in range(3)] + [("wwo", k) for k in range(2)]
    job = [(1, 1, k) for k in range(12)]
    for l in range(DEPTH):
        for k in range(11):
            before[f"up{k}", l] = [job.pop(0) for _ in range(2 if k == 0 else 1)] if l == 0 else []
            order += [("ada", m) for m in before[f"up{k}", l]] + [(f"up{k}", l)]
        order += [(f"down{k}", l) for k in range(6)]
        if l == 0:
            order += [("sci", k) for k in range(6)] + [("sco", k) for k in range(2)]
    return order, before


ORDER, BEFORE = plan()
CHUNK_OF = {key: n for n, key in enumerate(ORDER) if key[0]}
LATE_ADA = [m for l in range(DEPTH) for name in LATE for m in BEFORE[name, l]]
ADA_NO = {m: n for n, m in enumerate(m for key, m in ORDER if key == "ada")}


def stack_program(nc, T, out):
    ctx = ExitStack()
    with ctx:
        def sb(name, shape, dt=F32):
            return ctx.enter_context(nc.sbuf_tensor(name, shape, dt))

        def sem(name):
            return ctx.enter_context(nc.semaphore(name))

        ring = [sb(f"ring{i}", [P, CHUNK]) for i in range(RING)]
        XH = sb("XH", [P, 8192])
        AR = sb("AR", [P, 16 * 1024])
        CS = sb("CS", [P, C_IOTA + CAP])
        VEC = sb("VEC", [P, N_V])
        WR = sb("WR", [P, KT, NE])
        CACT = sb("CACT", [P, 2, KT, 2])
        MOD = sb("MOD", [P, 2, DEPTH, 48, 2])
        COEF = sb("COEF", [P, 2, DEPTH, 2, KT, 2])
        RST = sb("RST", [P, 512])
        LB = sb("LB", [P, 2, 2, 4])
        SM = sb("SM", [P, 208])
        EPSC = sb("EPSC", [P, 1])
        pair = [ctx.enter_context(nc.psum_tensor(f"pair{i}", [P, 1024], F32)) for i in range(4)]
        PA, PB, PC, PD = [q[:, :] for q in pair]

        def blk(i, n=1024):
            return AR[:, i * 1024:i * 1024 + n]

        ident, ones = CS[:, C_ID:C_ID + P], CS[:, C_ONE:C_ONE + P]
        X1 = XH[:, 0:2048].rearrange("p (t n) -> p t n", t=KT)
        H1 = XH[:, 2048:4096].rearrange("p (t n) -> p t n", t=KT)
        F = [XH[:, 4096 + 1024 * i:5120 + 1024 * i] for i in range(4)]
        X2 = XH[:, 4096:8192].rearrange("p (t n) -> p t n", t=KT)
        H2 = XH[:, 0:4096].rearrange("p (t n) -> p t n", t=KT)

        SCO_, R_BI, R_RK, R_GE = [SM[:, 32 * i:32 * i + 32] for i in range(4)]
        R_GS, R_GR, R_GG = [SM[:, 128 + 8 * i:136 + 8 * i] for i in range(3)]
        R_DN, OVERFLOW = SM[:, 152:154], SM[:, 154:155].bitcast(I32)
        DEC, BLAST = SM[:, 156:172], SM[:, 172:188]
        NM, RSUM = SM[:, 188:196], SM[:, 196:204]
        WNM, WRS, WES = [SM[:, 8 * i:8 * i + 8].rearrange("p (a n) -> p a n", a=2) for i in range(3)]
        LVM = CS[:, C_LV:C_RT].bitcast(mybir.dt.bfloat16)
        RT = CS[:, C_RT:C_RT + 2 * S]
        KR = XH[64:96, 4096 + 1536:4096 + 1536 + S]
        LRS = F[3][:, 0:512].rearrange("p (a n) -> p a n", a=2)
        CVT = [AR[:, (12 + j) * 1024:(13 + j) * 1024].rearrange("p (h n) -> p h n", h=2) for j in range(2)]
        GU = [blk(12), blk(13)]
        HT = [blk(14), blk(15)]
        XE = [blk(1, KT * CAP).rearrange("p (t n) -> p t n", t=KT), blk(2, KT * CAP).rearrange("p (t n) -> p t n", t=KT)]
        SGC, HEC, YES = blk(4, 4 * CAP), [blk(5, 4 * CAP), blk(7, 4 * CAP)], blk(8)
        TOK = [AR[0:CAP, 1024 * i + 512:1024 * i + 768] for i in (9, 10)]
        SLOT = [AR[:, 13 * 1024 + 4 * CAP * j:13 * 1024 + 4 * CAP * (j + 1)].rearrange("p (w m n) -> p w m n", w=2, m=2)
                for j in range(2)]
        POS, ANG, KK = [AR[0:DQK, 1024 * i:1024 * i + S] for i in range(3)]

        def n_vec(a, l):
            return 2 if (a, l) == (1, 0) else 1

        def acc_of(a, l, k, w):
            base = 14 if (a, l) == (1, 1) else 10
            which = w if n_vec(a, l) == 2 else k % 2
            if (a, l, k) in LATE_ADA:
                return F[0][:, 512 * which:512 * which + 512]
            return AR[:, base * 1024 + 512 * which:base * 1024 + 512 * which + 512]

        def h_count(n):
            return n + 1 if n < 4 else n

        names = """multiplied const1_in levels_in const2_in vec_in router_in x_in ctx_in pos_in out_stored
        act_step dve_step pool_step
        cact_ready rows_summed mod_taken coef_ready rope_ready lb_ready angle_ready
        squares_ready sums_ready std_ready scaled_ready h_act h_dve x_done
        hf_sig hq_silu hq_scaled v_copied hg_silu lat1_copied lat2_copied gates_act
        lat_sums lat_std latn_ready f_ready lnf_ready b_ready eb_ready qb_ready kdiff_ready kexp_ready kd_ready
        kd_turned kdt_ready u_ready dec_ready states_ready
        lvl_diff lvl_exp lvl_qk lvl_score lvl_masked lvl_added o_ready o_copied o_sums o_std oa_ready
        q_copied kr_turned rope_done k_copied v2_copied
        sc_ready sm_max sm_exp p_ready p_turned pt_ready om_ready om_copied
        bra_mul brb_mul merged_ready
        rt_ready rt_sig diag_ready cbc_ready cbc_copied sg_ready gu_ready he_ready acc_zero
        slots_in iota_in sel_ready places_ready overflow_ready h_turned ht_ready
        slot_ready gathered xe_ready scattered tok0_ready tok1_ready yes_ready
        wq_copied wsum_ready wstd_ready wn_ready wrot_ready wroped k_dup kdup_copied wv_copied
        wsq_ready ot_ready ot_copied
        cv_mid cv_conv cv_silu ff_act gc_copied scv_ready sc_mid scz_ready""".split()
        s = {n: sem(n) for n in names}
        full = [sem(f"slot{i}_full") for i in range(RING)]
        block = ctx.enter_context(nc.Block())

        def ck(name, l):
            return CHUNK_OF[name, l]

        @block.sync
        def _(sp):
            def put(c, src, shape, i=0):
                if not isinstance(c, int) or c >= RING:
                    sp.wait_ge(s["multiplied"], i + (c - RING + 1))
                dst = ring[c % RING][:, 0:shape[0] * shape[1]].rearrange("p (t n) -> p t n", t=shape[0])
                sp.dma_start(dst, src).then_inc(full[c % RING], 16)

            def cols(w, a, n):
                return w[:, a:a + n].rearrange("(t p) n -> p t n", p=P)

            sp.dma_start(VEC[:, :], T["vec"]).then_inc(s["vec_in"], 16)
            sp.dma_start(CS[:, 0:N_C1], T["const1"]).then_inc(s["const1_in"], 16)
            sp.dma_start(LVM, T["levels"]).then_inc(s["levels_in"], 16)
            sp.dma_start(CS[:, C_U:C_U + P], T["before"]).then_inc(s["slots_in"], 16)
            sp.dma_start(CS[:, C_IOTA:C_IOTA + CAP], T["iota"]).then_inc(s["iota_in"], 16)
            sp.dma_start(POS.bitcast(I32), T["pos"]).then_inc(s["pos_in"], 16)
            sp.dma_start(X1, T["x"].rearrange("(t p) n -> p t n", p=P)).then_inc(s["x_in"], 16)
            sp.dma_start(WR[:, :, :], T["w_router"].rearrange("(t p) n -> p t n", p=P)).then_inc(s["router_in"], 16)
            def put_ada(jobs):
                for a, l, k in jobs:
                    put(CHUNK_OF["ada", (a, l, k)], cols(T["ada_w_2" if a else "ada_w"][l, :, :], 512 * k, 512), (8, 512))

            put_ada(FIRST_ADA)
            proj = dict(hf=512, hq=0, hi=1024, hg=1536, lat1=2048, lat2=2560, gt0=2720, gt1=3232, gt2=3744, gt3=4256)
            for l in range(DEPTH):
                w_in = T["w_in"][l, :, :]
                for name in PROJ:
                    n = 160 if name == "lat2" else 512
                    put_ada(BEFORE[name, l])
                    put(ck(name, l), cols(w_in, proj[name], n), (8, n))
                put(ck("qu", l), cols(T["w_q_up"][l, :, :], 0, 768), (3, 768))
                put(ck("kv", l), cols(T["w_kv_up"][l, :, :], 0, 1024), (2, 1024))
                put(ck("ba", l), cols(T["w_br_a"][l, :, :], 0, 1024), (4, 1024))
                put_ada(BEFORE["bb", l])
                put(ck("bb", l), cols(T["w_br_b"][l, :, :], 0, 1024), (4, 1024))
                for k in range(2):
                    put_ada(BEFORE[f"wo{k}", l])
                    put(ck(f"wo{k}", l), cols(T["w_out"][l, :, :], 512 * k, 512), (8, 512))
                m0 = ck("moe", l)

                def expert(w, e, t):
                    return w[l, bass.ds(e, 1), :, :].rearrange("a (t p) n -> p (a t) n", p=P)
                put(m0, expert(T["w_gate"], 0, 8), (8, 512))
                put(m0 + 1, expert(T["w_up"], 0, 8), (8, 512))
                with sp.Fori(0, 7) as i:
                    for j in range(2):
                        c = m0 + 2 + 3 * j
                        put(c, expert(T["w_gate"], i * 2 + (1 + j), 8), (8, 512), i * 6)
                        put(c + 1, expert(T["w_up"], i * 2 + (1 + j), 8), (8, 512), i * 6)
                        put(c + 2, expert(T["w_down"], i * 2 + j, 4), (4, 1024), i * 6)
                put(m0 + 44, expert(T["w_gate"], 15, 8), (8, 512))
                put(m0 + 45, expert(T["w_up"], 15, 8), (8, 512))
                put(m0 + 46, expert(T["w_down"], 14, 4), (4, 1024))
                put(m0 + 47, expert(T["w_down"], 15, 4), (4, 1024))
                if l == DEPTH - 1:
                    sp.wait_ge(s["om_copied"], 3 * DEPTH)
                    sp.wait_ge(s["bra_mul"], 2 * DEPTH)
                    sp.wait_ge(s["places_ready"], DEPTH)
                    sp.dma_start(CS[:, C1_OVER:C1_OVER + N_C2], T["const2"]).then_inc(s["const2_in"], 16)
                    sp.dma_start(X2[:, :, S:2 * S], T["ctx"].rearrange("(t p) n -> p t n", p=P)).then_inc(s["ctx_in"], 16)
            for k in range(3):
                put(ck("wqkv", k), cols(T["win_w_qkv"], 512 * k, 512), (8, 512))
            for k in range(2):
                put(ck("wwo", k), cols(T["win_w_o"], 512 * k, 512), (8, 512))

            def ffn(l):
                up = T["ffn_w_up"][l, :, :].rearrange("(t p) (h n) -> p t h n", p=P, h=2)
                for k in range(11):
                    put_ada(BEFORE[f"up{k}", l])
                    c = ck(f"up{k}", l)
                    sp.wait_ge(s["multiplied"], c - RING + 1)
                    dst = ring[c % RING][:, :].rearrange("p (t h n) -> p t h n", t=KT, h=2)
                    for h in range(2):
                        sp.dma_start(dst[:, :, h, :], up[:, :, h, 256 * k:256 * k + 256])\
                            .then_inc(full[c % RING], 8 * 2)
                dn = T["ffn_w_down"][l, :, :]
                for half in range(2):
                    for k, (a, n) in enumerate(((0, 8), (8, 8), (16, 6))):
                        put(ck(f"down{3 * half + k}", l), cols(dn[a * P:(a + n) * P, :], 512 * half, 512), (n, 512))
            ffn(0)
            for half in range(2):
                for k, part in enumerate((1, 2, 0)):
                    put(ck("sci", 3 * half + k), cols(T["sc_w_in"], 1024 * part + 512 * half, 512), (8, 512))
            for k in range(2):
                put(ck("sco", k), cols(T["sc_w_out"], 512 * k, 512), (8, 512))
            ffn(1)
            sp.wait_ge(s["x_done"], 9)
            sp.dma_start(out.rearrange("(t p) n -> p t n", p=P), X2[:, :, 0:S]).then_inc(s["out_stored"], 16)
            sp.wait_ge(s["out_stored"], 16)

        def extra(c):
            return sum(1 for l in range(DEPTH) for k in range(11)
                       if ck(f"up{k}", l) <= c and (ck(f"up{k}", l) - c) % RING == 0)

        @block.tensor
        def _(pe):
            def arrived(c, i=0):
                pe.wait_ge(full[c % RING], i * 16 + 16 * (c // RING + 1 + extra(c)))

            def view(c, t, n):
                return ring[c % RING][:, 0:t * n].rearrange("p (t n) -> p t n", t=t)

            def mm(o, lhsT, rhs, start, stop, **kw):
                return pe.matmul(o, lhsT, rhs, start=start, stop=stop, **kw)

            def turn_modulation(jobs, q):
                for n, (a, l, k) in enumerate(jobs):
                    no = ADA_NO[a, l, k]
                    pe.wait_ge(s["rows_summed"], no + 1)
                    for w in range(n_vec(a, l)):
                        acc = acc_of(a, l, k, w)
                        for m in range(4):
                            last = mm(q[:, 8 * n + 4 * w + m:8 * n + 4 * w + m + 1], acc[:, m * P:m * P + P], ones[:, 0:1],
                                      True, True)
                    done(last)

            def features(c, outs, rhs, n_k=KT, width=512, M=P, i=0, ada=()):
                turn_modulation(ada, outs[-1])
                arrived(c, i)
                w = view(c, n_k, width)
                for m, o in enumerate(outs):
                    if ada and m == len(outs) // 2:
                        pe.wait_ge(s["mod_taken"], ADA_NO[ada[-1]] + 1)
                    for t in range(n_k):
                        last = mm(o, w[:, t, m * M:m * M + M], rhs(t), t == 0, t == n_k - 1)
                return last

            def done(last):
                last.then_inc(s["multiplied"], 1)

            pe.wait_ge(s["const1_in"], 16)
            turn_modulation(FIRST_ADA, PA)

            def sums(n, H, N):
                pe.wait_ge(s["squares_ready"], n + 1)
                for t in range(KT):
                    last = mm(PD[:, 0:N], ones, H[:, t, :], t == 0, t == KT - 1)
                last.then_inc(s["sums_ready"], 1)

            def h_arrived(n):
                pe.wait_ge(s["h_act"], h_count(n))
                pe.wait_ge(s["h_dve"], h_count(n))

            def half(q, m, N=S):
                return q[:, m * N:m * N + N]

            for l in range(DEPTH):
                sums(2 * l, H1, S)
                h_arrived(2 * l)
                hk = lambda t: H1[:, t, :]
                if l == 0:
                    pe.wait_ge(s["mod_taken"], len(FIRST_ADA))
                done(features(ck("hf", l), [half(PA, m) for m in range(4)], hk, ada=BEFORE["hf", l]))
                done(features(ck("hq", l), [half(PB, m) for m in range(4)], hk, ada=BEFORE["hq", l]))
                turn_modulation(BEFORE["hi", l], PC[:, 512:1024])
                arrived(ck("hi", l))
                w = view(ck("hi", l), KT, 512)
                for m in range(2):
                    if m:
                        pe.wait_ge(s["mod_taken"], ADA_NO[BEFORE["hi", l][-1]] + 1)
                    for t in range(KT):
                        last = mm(PC[:, 512 * m:512 * m + 512], H1[:, t, m * P:m * P + P], w[:, t, :], t == 0, t == KT - 1)
                done(last)
                done(features(ck("hg", l), [half(PD, m) for m in range(4)], hk, ada=BEFORE["hg", l]))
                pe.wait_ge(s["hf_sig"], l + 1)
                done(features(ck("lat1", l), [half(PA, m) for m in range(4)], hk, ada=BEFORE["lat1", l]))
                pe.wait_ge(s["hq_silu"], l + 1)
                turn_modulation(BEFORE["lat2", l], PB[:, 768:])
                arrived(ck("lat2", l))
                w = view(ck("lat2", l), KT, 160)
                for t in range(KT):
                    mm(PB[:, 0:S], w[:, t, 0:P], hk(t), t == 0, t == KT - 1)
                pe.wait_ge(s["mod_taken"], ADA_NO[BEFORE["lat2", l][-1]] + 1)
                for t in range(KT):
                    last = mm(PB[64:96, 512:512 + S], w[:, t, P:160], hk(t), t == 0, t == KT - 1)
                done(last)
                pe.wait_ge(s["v_copied"], l + 1)
                done(features(ck("gt0", l), [half(PC, m) for m in range(4)], hk, ada=BEFORE["gt0", l]))
                pe.wait_ge(s["lat1_copied"], l + 1)
                pe.wait_ge(s["lat2_copied"], l + 1)
                pe.wait_ge(s["hg_silu"], l + 1)
                sq = AR[:, 4 * 1024:4 * 1024 + 1280].rearrange("p (t n) -> p t n", t=5)
                for t in range(3):
                    mm(PD[:, 0:S], ones, sq[:, t, :], t == 0, t == 2)
                for t in range(3, 5):
                    last = mm(PD[:, 512:512 + S], ones, sq[:, t, :], t == 3, t == 4)
                last.then_inc(s["lat_sums"], 1)
                done(features(ck("gt1", l), [half(PA, m) for m in range(4)], hk, ada=BEFORE["gt1", l]))
                done(features(ck("gt2", l), [half(PB, m) for m in range(4)], hk, ada=BEFORE["gt2", l]))
                pe.wait_ge(s["gates_act"], 4 * l + 1)
                done(features(ck("gt3", l), [half(PC, m) for m in range(4)], hk, ada=BEFORE["gt3", l]))
                KD, KDT = blk(7), F[2]
                pe.wait_ge(s["kd_ready"], l + 1)
                pe.wait_ge(s["gates_act"], 4 * l + 2)
                for m in range(8):
                    last = pe.transpose(PA[:, m * P:m * P + P], KD[:, m * P:m * P + P], ident)
                last.then_inc(s["kd_turned"], 1)
                QE = [blk(5), blk(0)]
                KE = [blk(6), blk(1)]

                def level(n):
                    o = PB if n % 2 == 0 else PD
                    if n < 6:
                        pe.wait_ge(s["lvl_qk"], 6 * l + n + 1)
                    if n == 0:
                        pe.wait_ge(s["gates_act"], 4 * l + 3)
                    if n == 1:
                        pe.wait_ge(s["lat_std"], l + 1)
                    if n >= 2:
                        pe.wait_ge(s["lvl_masked"], 7 * l + n - 1)
                    q, k = (QE[0], KE[0]) if n < 6 else (QE[1], KE[1])
                    for m in range(8):
                        last = mm(o[:, m * P:m * P + P], k[:, m * P:m * P + P], q[:, m * P:m * P + P], True, True)
                    last.then_inc(s["lvl_score"], 1)

                level(0)
                VT = blk(9)
                pe.wait_ge(s["kdt_ready"], l + 1)
                pe.wait_ge(s["gates_act"], 4 * l + 4)
                for c in range(3):
                    lo = 64 * (c % 2)
                    for h in range(4):
                        o = (PA[:, 512 * c:512 * c + 512] if c < 2 else PC[:, 0:512])[:, h * P:h * P + P]
                        last = mm(o, KDT[lo:lo + 64, (2 * h + c // 2) * P:(2 * h + c // 2) * P + P],
                                  VT[lo:lo + 64, 512 * (c // 2) + h * P:512 * (c // 2) + h * P + P], True, True)
                last.then_inc(s["u_ready"], 1)
                for n in range(1, 7):
                    level(n)
                ST = XH[:, 2048:2048 + 1536]
                pe.wait_ge(s["lvl_added"], l + 1)
                pe.wait_ge(s["states_ready"], l + 1)
                pe.wait_ge(s["qb_ready"], l + 1)
                ATT, QB = blk(10), blk(8)
                for h in range(4):
                    for m in range(2):
                        mm(PA[:, h * S + m * P:h * S + m * P + P], VT[:, 512 * m + h * P:512 * m + h * P + P],
                           ATT[:, (2 * h + m) * P:(2 * h + m) * P + P], m == 0, False, skip_group_check=True)
                    for c in range(1, 4):
                        last = mm(PA[:, h * S + c * CH:h * S + c * CH + CH], ST[:, 512 * (c - 1) + h * P:512 * (c - 1) + h * P + P],
                                  QB[:, h * S + c * CH:h * S + c * CH + CH], False, c == 3, skip_group_check=True)
                last.then_inc(s["o_ready"], 1)
                CL = XH[:, 4096:4096 + 1280].rearrange("p (t n) -> p t n", t=5)
                pe.wait_ge(s["latn_ready"], l + 1)
                pe.wait_ge(s["lvl_masked"], 7 * l + 7)
                arrived(ck("qu", l))
                w = view(ck("qu", l), 3, 768)
                for h in range(8):
                    o = (PC if h < 4 else PD)[0:DQK, (h % 4) * S:(h % 4) * S + S]
                    for t in range(3):
                        last = mm(o, w[:, t, h * DQK:h * DQK + DQK], CL[:, t, :], t == 0, t == 2)
                done(last)
                pe.wait_ge(s["o_copied"], l + 1)
                for m in range(2):
                    last = mm(PB[:, 512 * m:512 * m + 512], ones, F[2][:, 512 * m:512 * m + 512], True, True)
                last.then_inc(s["o_sums"], 1)
                arrived(ck("kv", l))
                w = view(ck("kv", l), 2, 1024)
                pe.wait_ge(s["o_std"], l + 1)
                for h in range(8):
                    o = (PA if h < 4 else PB)[0:NOPE, (h % 4) * S:(h % 4) * S + S]
                    for t in range(2):
                        mm(o, w[:, t, h * P:h * P + NOPE], CL[:, 3 + t, :], t == 0, t == 1)
                pe.wait_ge(s["q_copied"], l + 1)
                wv = w.rearrange("p t (h d) -> p t h d", d=P)
                for m in range(2):
                    for t in range(2):
                        last = mm(PC[:, 512 * m:512 * m + 512], CL[:, 3 + t, m * P:m * P + P],
                                  wv[:, t, :, NOPE:P], t == 0, t == 1)
                done(last)
                QH = AR[:, 4 * 1024:4 * 1024 + 9 * S]
                rot = CS[64:96, C_PR:C_PR + 32]
                for m in range(2):
                    mm(PD[64:96, 512 * m:512 * m + 512], rot, QH[64:96, 512 * m:512 * m + 512], True, True)
                pe.wait_ge(s["k_copied"], l + 1)
                for m in range(2):
                    mm(PA[64:96, 512 * m:512 * m + 512], rot, QH[64:96, 1024 + 512 * m:1536 + 512 * m], True, True)
                mm(PB[64:96, 0:S], rot, QH[64:96, 2048:2048 + S], True, True).then_inc(s["kr_turned"], 1)
                KH = AR[:, 7 * 1024:9 * 1024].rearrange("p (h n) -> p h n", h=8)
                Q3 = QH.rearrange("p (h n) -> p h n", h=9)
                units = [(0, 0, 8, 128), (1, 0, 4, 256), (1, 4, 4, 256)]
                V2 = blk(9)

                def scores(u):
                    qb, h0, nh, nk = units[u]
                    o = PA if u % 2 == 0 else PC
                    for h in range(nh):
                        last = mm(o[:, h * nk:h * nk + nk], Q3[0:DQK, h0 + h, qb * P:qb * P + P],
                                  KH[0:DQK, h0 + h, 0:nk], True, True)
                    last.then_inc(s["sc_ready"], 1)

                def weighted(u):
                    qb, h0, nh, nk = units[u]
                    pe.wait_ge(s["p_ready"], 3 * l + u + 1)
                    if u == 0:
                        pe.wait_ge(s["rope_done"], 2 * l + 2)
                    pr = blk(10)
                    for m in range(8):
                        last = pe.transpose(PB[:, m * P:m * P + P], pr[:, m * P:m * P + P], ident)
                    last.then_inc(s["p_turned"], 1)
                    pe.wait_ge(s["pt_ready"], 3 * l + u + 1)
                    pt = blk(0).rearrange("p (h k q) -> p h k q", h=nh, q=P)
                    for h in range(nh):
                        g = h0 + h
                        o = PD[64 * (g % 2):64 * (g % 2) + 64, (g // 2) * S + qb * P:(g // 2) * S + qb * P + P]
                        for k in range(nk // P):
                            last = mm(o, V2[:, 512 * k + g * 64:512 * k + g * 64 + 64], pt[:, h, k, :],
                                      k == 0, k == nk // P - 1)
                    last.then_inc(s["om_ready"], 1)

                pe.wait_ge(s["rope_done"], 2 * l + 2)
                pe.wait_ge(s["v2_copied"], l + 1)
                scores(0)
                scores(1)
                weighted(0)
                pe.wait_ge(s["sm_max"], 3 * l + 1)
                scores(2)
                weighted(1)
                weighted(2)
                pe.wait_ge(s["oa_ready"], l + 1)
                OA = F[3].rearrange("p (t n) -> p t n", t=4)
                OM = blk(2).rearrange("p (t n) -> p t n", t=4)
                pe.wait_ge(s["sm_max"], 3 * l + 3)
                done(features(ck("ba", l), [half(PA if m < 4 else PB, m % 4) for m in range(8)],
                              lambda t: OA[:, t, :], 4, 1024))
                pe.wait_ge(s["om_copied"], 3 * l + 3)
                done(features(ck("bb", l), [half(PC if m < 4 else PD, m % 4) for m in range(8)],
                              lambda t: OM[:, t, :], 4, 1024, ada=BEFORE["bb", l]))
                MG = AR[:, 12 * 1024:14 * 1024].rearrange("p (t n) -> p t n", t=8)
                pe.wait_ge(s["merged_ready"], l + 1)
                done(features(ck("wo0", l), [half(PA, m) for m in range(4)], lambda t: MG[:, t, :], ada=BEFORE["wo0", l]))
                done(features(ck("wo1", l), [half(PB, m) for m in range(4)], lambda t: MG[:, t, :], ada=BEFORE["wo1", l]))

                n = 2 * l + 1
                sums(n, H1, S)
                h_arrived(n)
                pe.wait_ge(s["router_in"], 16)
                for m in range(2):
                    for t in range(KT):
                        last = mm(PD[:, 512 + NE * m:512 + NE * m + NE], H1[:, t, m * P:m * P + P], WR[:, t, :],
                                  t == 0, t == KT - 1)
                last.then_inc(s["rt_ready"], 1)
                for m in range(2):
                    for t in range(KT):
                        last = pe.transpose((PC, PB)[m][:, t * P:t * P + P], H1[:, t, m * P:m * P + P], ident)
                last.then_inc(s["h_turned"], 1)
                m0 = ck("moe", l)
                HE = [AR[:, (6 + j) * 1024:(7 + j) * 1024].rearrange("p (t n) -> p t n", t=4) for j in range(2)]

                def gate(c, e, i=0, wait=True):
                    if wait:
                        pe.wait_ge(s["sg_ready"], i * 2 + (16 * l + e))
                    done(features(c, [half(PA, m) for m in range(4)], hk, i=i))

                def up(c, e, i=0, wait=True):
                    if wait:
                        pe.wait_ge(s["gu_ready"], i * 2 + (16 * l + e))
                    done(features(c, [half(PB, m) for m in range(4)], hk, i=i))

                def down(c, e, i=0, parity=0):
                    arrived(c, i)
                    pe.wait_ge(s["he_ready"], i * 2 + (16 * l + e + 1))
                    w = view(c, 4, 1024)
                    for m in range(8):
                        for t in range(4):
                            last = mm(half(PC if m < 4 else PD, m % 4), w[:, t, m * P:m * P + P], HE[parity][:, t, :],
                                      False, False, skip_group_check=True)
                    done(last)

                def broadcast(g):
                    for m in range(2):
                        pe.wait_ge(s["diag_ready"], 8 * l + 2 * g + m + 1)
                        if g >= 1 and m == 0:
                            pe.wait_ge(s["cbc_copied"], 4 * l + g)
                        mm(PC[:, 512 * m:512 * m + 512], ones, blk(9 + m, 512), True, True).then_inc(s["cbc_ready"], 1)

                def zero_sum():
                    for q in (PC, PD):
                        for m in range(2):
                            mm(q[:, 512 * m:512 * m + 512], blk(11, 128), XH[:, 2048:2560], True, False,
                               skip_group_check=True)

                gate(m0, 0, wait=False)
                pe.wait_ge(s["slots_in"], 16)
                pe.wait_ge(s["sel_ready"], l + 1)
                before = CS[:, C_U:C_U + P]
                mm(PD[:, 0:NE], before, R_RK[:, 0:NE], True, True)
                mm(PD[:, NE:2 * NE], before, R_RK[:, NE:2 * NE], True, False)
                mm(PD[:, NE:2 * NE], ones, R_RK[:, 0:NE], False, True)
                mm(PD[:, 2 * NE:3 * NE], ones, R_RK[:, 0:NE], True, False)
                mm(PD[:, 2 * NE:3 * NE], ones, R_RK[:, NE:2 * NE], False, True).then_inc(s["places_ready"], 1)
                pe.wait_ge(s["ht_ready"], l + 1)
                up(m0 + 1, 0, wait=False)
                broadcast(0)
                pe.wait_ge(s["rt_sig"], l + 1)
                pe.wait_ge(s["acc_zero"], l + 1)
                pe.wait_ge(s["overflow_ready"], l + 1)
                overflow = pe.value_load(OVERFLOW[0:1, :], min_val=0, max_val=1)
                with pe.If(overflow):
                    for g in range(1, 4):
                        broadcast(g)
                    pe.wait_ge(s["cbc_copied"], 4 * l + 4)
                    zero_sum()
                    with pe.Fori(0, 7) as i:
                        for j in range(2):
                            c = m0 + 2 + 3 * j
                            gate(c, 1 + j, i)
                            up(c + 1, 1 + j, i)
                            down(c + 2, j, i, j)
                    gate(m0 + 44, 15)
                    up(m0 + 45, 15)
                    down(m0 + 46, 14, 0, 0)
                    down(m0 + 47, 15, 0, 1)
                    pe.sem_inc(s["gathered"], NE - 1)
                    pe.sem_inc(s["scattered"], NE - 1)
                with pe.Else():
                    b0 = (NE - 1) * l

                    def c_gather(e, i=0):
                        pe.wait_ge(s["slot_ready"], i * 2 + (b0 + e))
                        for t in range(KT):
                            o = PA[:, 512 * (t // 4) + CAP * (t % 4):512 * (t // 4) + CAP * (t % 4) + CAP]
                            for m in range(2):
                                last = mm(o, HT[m][:, t * P:t * P + P], SLOT[e % 2][:, 0, m, :], m == 0, m == 1)
                        last.then_inc(s["gathered"], 1)

                    def c_features(c, e, n, i):
                        pe.transpose(PB[0:CAP, 512 * n + 4 * CAP:512 * n + 512], SLOT[e % 2][:, 1, n, :], ident)
                        done(features(c, [PB[:, 512 * n + CAP * m:512 * n + CAP * m + CAP] for m in range(4)],
                                      lambda t: XE[e % 2][:, t, :], i=i))

                    def c_gate(c, e, i=0):
                        pe.wait_ge(s["xe_ready"], i * 2 + (b0 + e))
                        if e > 1:
                            pe.wait_ge(s["tok0_ready"], i * 2 + (b0 + e - 1))
                        c_features(c, e, 0, i)

                    def c_up(c, e, i=0):
                        if e > 1:
                            pe.wait_ge(s["tok1_ready"], i * 2 + (b0 + e - 1))
                        c_features(c, e, 1, i)

                    def c_down(c, e, i=0):
                        arrived(c, i)
                        pe.wait_ge(s["he_ready"], i * 2 + (NE * l + e + 1))
                        w = view(c, 4, 1024)
                        for m in range(2):
                            for t in range(4):
                                last = mm(PA[0:CAP, 512 * m:512 * m + 512], HEC[e % 2][:, CAP * t:CAP * t + CAP],
                                          w[:, t, 512 * m:512 * m + 512], t == 0, t == 3)
                        done(last)

                    def c_scatter(e, i=0):
                        pe.wait_ge(s["yes_ready"], i * 2 + (b0 + e))
                        pe.wait_ge(s["tok0_ready"], i * 2 + (b0 + e))
                        pe.wait_ge(s["tok1_ready"], i * 2 + (b0 + e))
                        for m in range(8):
                            last = mm(half(PC if m < 4 else PD, m % 4), YES[0:CAP, m * P:m * P + P], TOK[e % 2],
                                      False, False, skip_group_check=True)
                        last.then_inc(s["scattered"], 1)

                    pe.wait_ge(s["sg_ready"], NE * l + 1)
                    c_gather(1)
                    pe.wait_ge(s["cbc_copied"], 4 * l + 1)
                    zero_sum()
                    pe.wait_ge(s["gu_ready"], NE * l + 1)
                    c_gate(m0 + 2, 1)
                    c_gather(2)
                    c_up(m0 + 3, 1)
                    down(m0 + 4, 0)
                    c_gate(m0 + 5, 2)
                    pe.wait_ge(s["xe_ready"], b0 + 2)
                    c_gather(3)
                    c_up(m0 + 6, 2)
                    pe.wait_ge(s["xe_ready"], b0 + 3)
                    c_down(m0 + 7, 1)
                    with pe.Fori(0, 6) as i:
                        for e in (3, 4):
                            c = m0 + 3 * e - 1
                            c_gate(c, e, i)
                            pe.wait_ge(s["yes_ready"], i * 2 + (b0 + e - 2))
                            c_gather(e + 1, i)
                            c_scatter(e - 2, i)
                            c_up(c + 1, e, i)
                            pe.wait_ge(s["xe_ready"], i * 2 + (b0 + e + 1))
                            c_down(c + 2, e - 1, i)
                    c_gate(m0 + 44, 15)
                    c_scatter(13)
                    c_up(m0 + 45, 15)
                    c_down(m0 + 46, 14)
                    c_scatter(14)
                    c_down(m0 + 47, 15)
                    c_scatter(15)
                    pe.sem_inc(s["cbc_ready"], 6)

            sums(4, H1, S)
            pe.wait_ge(s["const2_in"], 16)
            cB, cP = CS[:, C1_OVER + D_B64:C1_OVER + D_B64 + P], CS[:, C1_OVER + D_P64:C1_OVER + D_P64 + P]
            sums(5, H2, 512)
            h_arrived(5)

            def banks(n0):
                return [(PA, PB, PC, PD)[(n0 + k) // 2 % 4][:, ((n0 + k) % 2) * 512:((n0 + k) % 2) * 512 + 512]
                        for k in range(4)]
            h2k = lambda t: H2[:, t, :]
            done(features(ck("wqkv", 0), banks(0), h2k))
            done(features(ck("wqkv", 1), banks(4), h2k))
            pe.wait_ge(s["wq_copied"], 2)
            arrived(ck("wqkv", 2))
            w = view(ck("wqkv", 2), KT, 512)
            for m in range(2):
                for t in range(KT):
                    mm(PA[:, 512 * m:512 * m + 512], w[:, t, m * P:m * P + P], h2k(t), t == 0, t == KT - 1)
            for m in range(4):
                for t in range(KT):
                    last = mm(PB[:, S * m:S * m + S], H2[:, t, m * P:m * P + P], w[:, t, 256:512], t == 0, t == KT - 1)
            done(last)
            QT = [AR[:, k * 1024:k * 1024 + 1024] for k in range(5)]
            for u in range(5):
                pe.wait_ge(s["wsq_ready"], u + 1)
                if u >= 1:
                    pe.wait_ge(s["wstd_ready"], u)
                for m in range(2):
                    last = mm(PC[:, 512 * m:512 * m + 512], cB, XH[:, 2048 * (u % 2) + 512 * m:2048 * (u % 2) + 512 * m + 512],
                              True, True)
                last.then_inc(s["wsum_ready"], 1)
                pe.wait_ge(s["wn_ready"], u + 1)
                if u >= 1:
                    pe.wait_ge(s["wroped"], u)
                for m in range(2):
                    last = mm(PD[:, S * m:S * m + S], cP, QT[u][:, 512 * m:512 * m + S], True, True)
                last.then_inc(s["wrot_ready"], 1)
            pe.wait_ge(s["wroped"], 5)
            for g in range(4):
                sel = CS[:, C1_OVER + D_SEL + P * (g % 2):C1_OVER + D_SEL + P * (g % 2) + P]
                o = (PA, PC)[g // 2][:, 512 * (g % 2):512 * (g % 2) + 512]
                last = mm(o, sel, QT[4][:, 512 * (g // 2):512 * (g // 2) + 512], True, True)
            last.then_inc(s["k_dup"], 1)
            KDUP = AR[:, 5 * 1024:7 * 1024].rearrange("p (g n) -> p g n", g=4)
            WV = blk(7).rearrange("p (t n) -> p t n", t=4)
            Q2 = AR[:, 0:4096].rearrange("p (t n) -> p t n", t=8)
            units = [(t, k) for t in range(8) for k in range(3)]

            def wscores(u):
                t, kind = units[u]
                g = t // 2
                o = (PA, PB)[u % 2]
                if u >= 2:
                    pe.wait_ge(s["sm_max"], 3 * DEPTH + u - 1)
                if kind < 2:
                    lo = 64 * kind
                    for b in range(2):
                        last = mm(o[:, 512 * b:512 * b + 512], Q2[lo:lo + 64, t, b * P:b * P + P],
                                  KDUP[lo:lo + 64, g, :], True, True)
                else:
                    for h in range(2):
                        for b in range(2):
                            last = mm(o[:, 512 * h + S * b:512 * h + S * b + S],
                                      Q2[64 * h:64 * h + 64, t, S + b * P:S + b * P + P],
                                      KDUP[64 * h:64 * h + 64, g, S:2 * S], True, True)
                last.then_inc(s["sc_ready"], 1)

            def wweighted(u):
                t, kind = units[u]
                g = t // 2
                pe.wait_ge(s["p_ready"], 3 * DEPTH + u + 1)
                if u >= 1:
                    pe.wait_ge(s["pt_ready"], 3 * DEPTH + u)
                pr = blk(12 + u % 2)
                for m in range(8):
                    if kind < 2:
                        src = pr[:, (m % 2) * 512 + (m // 2) * P:(m % 2) * 512 + (m // 2) * P + P]
                    else:
                        h, k, b = m // 4, (m // 2) % 2, m % 2
                        src = pr[:, 512 * h + S * b + P * k:512 * h + S * b + P * k + P]
                    last = pe.transpose(PC[:, m * P:m * P + P], src, ident)
                last.then_inc(s["p_turned"], 1)
                if u + 2 < 24:
                    wscores(u + 2)
                pe.wait_ge(s["pt_ready"], 3 * DEPTH + u + 1)
                pt = blk(14 + u % 2)
                o = PD[:, 512 * (t % 2):512 * (t % 2) + 512]
                if kind == 0 and t >= 2:
                    pe.wait_ge(s["ot_copied"], t - 1)
                if kind < 2:
                    for k in range(4):
                        last = mm(o[64 * kind:64 * kind + 64, 0:S], WV[:, k, g * 64:g * 64 + 64],
                                  pt[:, S * k:S * k + S], k == 0, k == 3)
                else:
                    for h in range(2):
                        for k in range(2):
                            last = mm(o[64 * h:64 * h + 64, S:2 * S], WV[:, 2 + k, g * 64:g * 64 + 64],
                                      pt[:, 512 * h + S * k:512 * h + S * k + S], k == 0, k == 1)
                last.then_inc(s["ot_ready"], 1)

            pe.wait_ge(s["kdup_copied"], 1)
            pe.wait_ge(s["wv_copied"], 1)
            wscores(0)
            wscores(1)
            for u in range(24):
                wweighted(u)
            OT = AR[:, 8 * 1024:12 * 1024].rearrange("p (t n) -> p t n", t=8)
            pe.wait_ge(s["ot_copied"], 8)
            done(features(ck("wwo", 0), banks(0), lambda t: OT[:, t, :]))
            done(features(ck("wwo", 1), banks(4), lambda t: OT[:, t, :]))

            def ffn(l, n, H, N):
                sums(n, H, N)
                h_arrived(n)
                done_tiles = 22 * l
                for k in range(11):
                    c = ck(f"up{k}", l)
                    bs = banks(4 * (k % 2))
                    if k >= 2:
                        pe.wait_ge(s["cv_conv"], 2 * (done_tiles + 2 * (k - 1)))
                    turn_modulation(BEFORE[f"up{k}", l], bs[3])
                    arrived(c)
                    w = ring[c % RING][:, :].rearrange("p (t h n) -> p t h n", t=KT, h=2)
                    for j in range(2):
                        for h in range(2):
                            if j and h and BEFORE[f"up{k}", l]:
                                pe.wait_ge(s["mod_taken"], ADA_NO[BEFORE[f"up{k}", l][-1]] + 1)
                            for t in range(KT):
                                last = mm(bs[2 * j + h][:, 0:N], w[:, t, h, j * P:j * P + P], H[:, t, :],
                                          t == 0, t == KT - 1)
                    done(last)
                A = AR[:, 0:22 * N].rearrange("p (t n) -> p t n", n=N)
                for hf in range(2):
                    if hf == 0:
                        pe.wait_ge(s["cv_conv"], 2 * (done_tiles + 22))
                    for k, (a, nk) in enumerate(((0, 8), (8, 8), (16, 6))):
                        c = ck(f"down{3 * hf + k}", l)
                        arrived(c)
                        w = view(c, nk, 512)
                        pe.wait_ge(s["ff_act"], done_tiles + a + nk)
                        for m in range(4):
                            for t in range(nk):
                                last = mm(banks(4 * hf)[m][:, 0:N], w[:, t, m * P:m * P + P], A[:, a + t, :],
                                          a + t == 0, a + t == 21)
                        done(last)

            ffn(0, 6, H2, 512)
            HL = XH[:, 0:2048].rearrange("p (t n) -> p t n", t=8)
            sums(7, HL, S)
            h_arrived(7)
            hl = lambda t: HL[:, t, :]
            for hf in range(2):
                if hf:
                    pe.wait_ge(s["gc_copied"], 1)
                done(features(ck("sci", 3 * hf), [half(PA, m) for m in range(4)], hl))
                if hf:
                    pe.wait_ge(s["scv_ready"], 1)
                done(features(ck("sci", 3 * hf + 1), [half(PB, m) for m in range(4)], hl))
                done(features(ck("sci", 3 * hf + 2), [half((PC, PD)[hf], m) for m in range(4)], hl))
            Z = AR[:, 0:2048].rearrange("p (t n) -> p t n", t=8)
            pe.wait_ge(s["scz_ready"], 2)
            done(features(ck("sco", 0), [half(PA, m) for m in range(4)], lambda t: Z[:, t, :]))
            done(features(ck("sco", 1), [half(PB, m) for m in range(4)], lambda t: Z[:, t, :]))
            ffn(1, 8, HL, S)

        @block.scalar
        def _(act):
            steps = [0]

            def step(ins):
                steps[0] += 1
                ins.then_inc(s["act_step"], 1)

            def settle():
                act.wait_ge(s["act_step"], steps[0])

            def multiplied(c):
                act.wait_ge(s["multiplied"], c + 1)

            A = act.activation
            act.wait_ge(s["vec_in"], 16)
            A(CACT[:, :, :, :].rearrange("p a t w -> p (a t w)"), VEC[:, V_C:V_C + 32], ACT.Silu).then_inc(s["cact_ready"], 1)
            act.wait_ge(s["lb_ready"], 1)
            A(LB[:, 0, :, :].rearrange("p a b -> p (a b)"), LB[:, 0, :, :].rearrange("p a b -> p (a b)"), ACT.Exp).then_inc(s["lb_ready"], 1)
            act.wait_ge(s["angle_ready"], 1)
            A(RT[0:DQK, :], RT[0:DQK, :], ACT.Sin).then_inc(s["rope_ready"], 1)

            def squares(n, X, H):
                if n == 0:
                    act.wait_ge(s["x_in"], 16)
                else:
                    act.wait_ge(s["x_done"], n)
                if n == 5:
                    act.wait_ge(s["ctx_in"], 16)
                A(H, X, ACT.Square).then_inc(s["squares_ready"], 1)

            def norm(n, X, H, N, a, l, which, ws):
                squares(n, X, H)
                act.wait_ge(s["sums_ready"], n + 1)
                A(RST[:, 0:N], PD[:, 0:N], ACT.Sqrt, scale=1.0 / D, bias=EPSC[:, 0:1]).then_inc(s["std_ready"], 1)
                act.wait_ge(s["scaled_ready"], h_count(n))
                for t in range(4):
                    for w in range(ws):
                        sl = H[:, t, w * S:w * S + S]
                        ins = A(sl, sl, ACT.Identity, scale=COEF[:, a, l, which, t, w:w + 1],
                                bias=MOD[:, a, l, 24 * which + t, w:w + 1])
                        if t == 3 and w == ws - 1:
                            ins.then_inc(s["h_act"], 1)

            EE = blk(4)
            for l in range(DEPTH):
                norm(2 * l, X1, H1, S, 0, l, 0, 1)
                multiplied(ck("hf", l))
                A(EE, PA, ACT.Sigmoid).then_inc(s["hf_sig"], 1)
                multiplied(ck("hq", l))
                A(blk(0), PB, ACT.Silu).then_inc(s["hq_silu"], 1)
                multiplied(ck("hi", l))
                A(blk(9), PC, ACT.Copy).then_inc(s["v_copied"], 1)
                multiplied(ck("hg", l))
                A(blk(3), PD, ACT.Silu).then_inc(s["hg_silu"], 1)
                CLf = XH[:, 4096:4096 + 1280]
                SQ = AR[:, 4 * 1024:4 * 1024 + 1280]
                multiplied(ck("lat1", l))
                A(CLf[:, 0:1024], PA, ACT.Copy)
                act.wait_ge(s["f_ready"], l + 1)
                A(SQ[:, 0:1024], PA, ACT.Square).then_inc(s["lat1_copied"], 1)
                multiplied(ck("lat2", l))
                A(CLf[:, 1024:1280], PB[:, 0:S], ACT.Copy)
                A(KR, PB[64:96, 512:512 + S], ACT.Copy)
                A(SQ[:, 1024:1280], PB[:, 0:S], ACT.Square).then_inc(s["lat2_copied"], 1)
                A(blk(2), blk(2), ACT.Ln).then_inc(s["lnf_ready"], 1)
                multiplied(ck("gt0", l))
                A(blk(12), PC, ACT.Sigmoid).then_inc(s["gates_act"], 1)
                multiplied(ck("gt1", l))
                A(blk(13), PA, ACT.Sigmoid).then_inc(s["gates_act"], 1)
                multiplied(ck("gt2", l))
                A(blk(14), PB, ACT.Sigmoid).then_inc(s["gates_act"], 1)
                act.wait_ge(s["lat_sums"], l + 1)
                A(LRS[:, 0, :], PD[:, 0:S], ACT.Sqrt, scale=1.0 / QL, bias=EPSC[:, 0:1])
                A(LRS[:, 1, :], PD[:, 512:512 + S], ACT.Sqrt, scale=1.0 / KVL, bias=EPSC[:, 0:1]).then_inc(s["lat_std"], 1)
                act.wait_ge(s["kdiff_ready"], l + 1)
                A(blk(7), blk(7), ACT.Exp).then_inc(s["kexp_ready"], 1)
                A(DEC, BLAST, ACT.Exp).then_inc(s["dec_ready"], 1)
                A(blk(8), blk(2), ACT.Exp).then_inc(s["eb_ready"], 1)
                for n in range(6):
                    act.wait_ge(s["lvl_diff"], 6 * l + n + 1)
                    A(EE, EE, ACT.Exp).then_inc(s["lvl_exp"], 1)
                    if n == 0:
                        act.wait_ge(s["kd_turned"], l + 1)
                        A(F[2], PA, ACT.Copy).then_inc(s["kdt_ready"], 1)
                    if n == 1:
                        multiplied(ck("gt3", l))
                        A(blk(15), PC, ACT.Sigmoid).then_inc(s["gates_act"], 1)
                act.wait_ge(s["o_ready"], l + 1)
                A(F[3], PA, ACT.Copy)
                A(F[2], PA, ACT.Square).then_inc(s["o_copied"], 1)
                multiplied(ck("qu", l))
                QH = AR[:, 4 * 1024:4 * 1024 + 9 * S]
                A(QH[0:DQK, 0:1024], PC[0:DQK, :], ACT.Copy)
                A(QH[64:96, 2048:2048 + S], KR, ACT.Copy)
                A(QH[0:DQK, 1024:2048], PD[0:DQK, :], ACT.Copy).then_inc(s["q_copied"], 1)
                act.wait_ge(s["o_sums"], l + 1)
                A(blk(11), PB, ACT.Sqrt, scale=1.0 / HG_D, bias=EPSC[:, 0:1]).then_inc(s["o_std"], 1)
                multiplied(ck("kv", l))
                A(AR[0:NOPE, 7 * 1024:8 * 1024], PA[0:NOPE, :], ACT.Copy)
                A(AR[0:NOPE, 8 * 1024:9 * 1024], PB[0:NOPE, :], ACT.Copy).then_inc(s["k_copied"], 1)
                A(blk(9), PC, ACT.Copy).then_inc(s["v2_copied"], 1)

                def soft(u, nh, nk):
                    act.wait_ge(s["sm_max"], 3 * l + u + 1)
                    pr = blk(10)
                    for h in range(nh):
                        ins = A(pr[:, h * nk:h * nk + nk], pr[:, h * nk:h * nk + nk], ACT.Exp,
                                bias=NM[:, h:h + 1], accum_out=RSUM[:, h:h + 1])
                    ins.then_inc(s["sm_exp"], 1)

                def turned(u):
                    act.wait_ge(s["p_turned"], 3 * l + u + 1)
                    A(blk(0), PB, ACT.Copy).then_inc(s["pt_ready"], 1)
                OMf = blk(2).rearrange("p (t n) -> p t n", t=4)
                for u, (nh, nk) in enumerate(((8, 128), (4, 256), (4, 256))):
                    soft(u, nh, nk)
                    turned(u)
                    act.wait_ge(s["om_ready"], 3 * l + u + 1)
                    if u == 0:
                        o_, i_ = OMf[:, :, 0:P], PD.rearrange("p (t n) -> p t n", t=4)[:, :, 0:P]
                    else:
                        o_ = OMf[:, 2 * u - 2:2 * u, P:2 * P]
                        i_ = PD.rearrange("p (t n) -> p t n", t=4)[:, 2 * u - 2:2 * u, P:2 * P]
                    A(o_, i_, ACT.Copy).then_inc(s["om_copied"], 1)
                norm(2 * l + 1, X1, H1, S, 0, l, 1, 1)
                act.wait_ge(s["rt_ready"], l + 1)
                A(SCO_, PD[:, 512:512 + 2 * NE], ACT.Sigmoid).then_inc(s["rt_sig"], 1)
                act.wait_ge(s["h_turned"], l + 1)
                A(HT[0], PC, ACT.Copy)
                A(HT[1], PB, ACT.Copy).then_inc(s["ht_ready"], 1)
                m0 = ck("moe", l)
                SG = [blk(4), blk(5)]
                multiplied(m0)
                A(SG[0], PA, ACT.Silu).then_inc(s["sg_ready"], 1)
                CB = AR[:, 0:4096].rearrange("p (e t) -> p e t", e=16)

                def copy_weights(g):
                    act.wait_ge(s["cbc_ready"], 8 * l + 2 * g + 2)
                    for m in range(2):
                        ins = A(CB[:, 4 * g:4 * g + 4, m * P:m * P + P],
                                PC[:, 512 * m:512 * m + 512].rearrange("p (e t) -> p e t", e=4), ACT.Copy)
                    ins.then_inc(s["cbc_copied"], 1)

                copy_weights(0)
                act.wait_ge(s["overflow_ready"], l + 1)
                overflow = act.value_load(OVERFLOW[0:1, :], min_val=0, max_val=1)
                with act.If(overflow):
                    for g in range(1, 4):
                        copy_weights(g)
                    with act.Fori(0, 7) as i:
                        for j in range(2):
                            act.wait_ge(s["gu_ready"], i * 2 + (16 * l + 1 + j))
                            act.wait_ge(s["multiplied"], i * 6 + (m0 + 2 + 3 * j + 1))
                            A(SG[(1 + j) % 2], PA, ACT.Silu).then_inc(s["sg_ready"], 1)
                    multiplied(m0 + 44)
                    act.wait_ge(s["gu_ready"], 16 * l + 14)
                    A(SG[1], PA, ACT.Silu).then_inc(s["sg_ready"], 1)
                    act.sem_inc(s["tok0_ready"], NE - 1)
                    act.sem_inc(s["yes_ready"], NE - 1)
                with act.Else():
                    b0 = (NE - 1) * l

                    def c_silu(e, i=0):
                        act.wait_ge(s["multiplied"], i * 6 + (m0 + 3 * e))
                        act.wait_ge(s["he_ready"], i * 2 + (NE * l + e))
                        A(SGC, PB[:, 0:4 * CAP], ACT.Silu).then_inc(s["sg_ready"], 1)
                        if e > 2:
                            act.wait_ge(s["scattered"], i * 2 + (b0 + e - 2))
                        A(TOK[e % 2][:, 0:P], PB[0:CAP, 4 * CAP:512], ACT.Copy).then_inc(s["tok0_ready"], 1)

                    def c_outputs(e, c, i=0):
                        act.wait_ge(s["multiplied"], i * 6 + (c + 1))
                        A(YES[0:CAP, :], PA[0:CAP, :], ACT.Copy).then_inc(s["yes_ready"], 1)
                    c_silu(1)
                    c_silu(2)
                    c_outputs(1, m0 + 7)
                    with act.Fori(0, 6) as i:
                        for e in (3, 4):
                            c_silu(e, i)
                            c_outputs(e - 1, m0 + 3 * e + 1, i)
                    c_silu(15)
                    c_outputs(14, m0 + 46)
                    c_outputs(15, m0 + 47)
                    act.sem_inc(s["cbc_copied"], 3)

            squares(4, X1, H1)
            act.wait_ge(s["sums_ready"], 5)
            A(RST[:, 0:S], PD[:, 0:S], ACT.Sqrt, scale=1.0 / D, bias=EPSC[:, 0:1]).then_inc(s["std_ready"], 1)
            norm(5, X2, H2, 512, 1, 0, 0, 2)
            QT = [AR[:, k * 1024:k * 1024 + 1024] for k in range(5)]
            pairs = [(PA, ck("wqkv", 0)), (PB, ck("wqkv", 0)), (PC, ck("wqkv", 1)), (PD, ck("wqkv", 1))]
            for u in range(4):
                multiplied(pairs[u][1])
                A(QT[u], pairs[u][0], ACT.Copy).then_inc(s["wq_copied"], 1)
            multiplied(ck("wqkv", 2))
            A(blk(7), PB, ACT.Copy).then_inc(s["wv_copied"], 1)
            A(QT[4], PA, ACT.Copy).then_inc(s["wq_copied"], 1)
            del pairs

            def wsquare(u):
                act.wait_ge(s["wq_copied"], u + 1)
                if u >= 2:
                    act.wait_ge(s["wsum_ready"], u - 1)
                A(XH[:, 2048 * (u % 2):2048 * (u % 2) + 1024], QT[u], ACT.Square).then_inc(s["wsq_ready"], 1)
            for u in range(5):
                if u == 0:
                    wsquare(0)
                if u + 1 < 5:
                    wsquare(u + 1)
                act.wait_ge(s["wsum_ready"], u + 1)
                if u >= 1:
                    act.wait_ge(s["wn_ready"], u)
                A(blk(8), PC, ACT.Sqrt, scale=1.0 / WHD, bias=EPSC[:, 0:1]).then_inc(s["wstd_ready"], 1)
            act.wait_ge(s["k_dup"], 1)
            A(blk(5), PA, ACT.Copy)
            A(blk(6), PC, ACT.Copy).then_inc(s["kdup_copied"], 1)

            def wsoft(u):
                t, kind = u // 3, u % 3
                act.wait_ge(s["sm_max"], 3 * DEPTH + u + 1)
                pr = blk(12 + u % 2)
                if kind < 2:
                    for b in range(2):
                        A(pr[:, 512 * b:512 * b + 512], pr[:, 512 * b:512 * b + 512], ACT.Exp,
                          bias=WNM[:, u % 2, b:b + 1], accum_out=WRS[:, u % 2, b:b + 1])
                    h = 2 * t + kind
                    A(WES[:, u % 2, 0:2], WNM[:, u % 2, 0:2], ACT.Exp,
                      bias=VEC[:, V_SINK + h:V_SINK + h + 1]).then_inc(s["sm_exp"], 1)
                else:
                    for b in range(4):
                        A(pr[:, S * b:S * b + S], pr[:, S * b:S * b + S], ACT.Exp,
                          bias=WNM[:, u % 2, b:b + 1], accum_out=WRS[:, u % 2, b:b + 1])
                    for h in range(2):
                        ins = A(WES[:, u % 2, 2 * h:2 * h + 2], WNM[:, u % 2, 2 * h:2 * h + 2], ACT.Exp,
                                bias=VEC[:, V_SINK + 2 * t + h:V_SINK + 2 * t + h + 1])
                    ins.then_inc(s["sm_exp"], 1)

            OT = AR[:, 8 * 1024:12 * 1024].rearrange("p (t n) -> p t n", t=8)
            wsoft(0)
            wsoft(1)
            for u in range(24):
                act.wait_ge(s["p_turned"], 3 * DEPTH + u + 1)
                if u >= 2:
                    act.wait_ge(s["ot_ready"], u - 1)
                A(blk(14 + u % 2), PC, ACT.Copy).then_inc(s["pt_ready"], 1)
                if u % 3 == 0 and u:
                    t = u // 3 - 1
                    act.wait_ge(s["ot_ready"], 3 * t + 3)
                    A(OT[:, t, :], PD[:, 512 * (t % 2):512 * (t % 2) + 512], ACT.Copy).then_inc(s["ot_copied"], 1)
                if u + 2 < 24:
                    wsoft(u + 2)
            act.wait_ge(s["ot_ready"], 24)
            A(OT[:, 7, :], PD[:, 512:1024], ACT.Copy).then_inc(s["ot_copied"], 1)

            def bank(k):
                return (PA, PB, PC, PD)[k // 2][:, (k % 2) * 512:(k % 2) * 512 + 512]

            def ffn(l, n, X, H, N):
                norm(n, X, H, N, 1, l, 1, N // S)
                for j in range(22):
                    b0 = (4 * ((j // 2) % 2) + 2 * (j % 2))
                    multiplied(ck(f"up{j // 2}", l))
                    tmp = CVT[j % 2]
                    if j >= 2:
                        act.wait_ge(s["ff_act"], 22 * l + j - 1)
                    for h in range(2):
                        w1 = VEC[:, V_FC + 132 * l + 44 + 22 * h + j:V_FC + 132 * l + 44 + 22 * h + j + 1]
                        A(tmp[:, h, 0:N], bank(b0 + h)[:, 0:N], ACT.Copy, scale=w1).then_inc(s["cv_mid"], 1)
                    act.wait_ge(s["cv_conv"], 2 * (22 * l + j) + 1)
                    A(tmp[:, 0, 0:N], tmp[:, 0, 0:N], ACT.Silu).then_inc(s["cv_silu"], 1)
            ffn(0, 6, X2, H2, 512)
            HL = XH[:, 0:2048].rearrange("p (t n) -> p t n", t=8)
            XL = X2[:, :, 0:S]
            norm(7, XL, HL, S, 1, 1, 0, 1)
            GC, CV = blk(2), blk(3)
            for hf in range(2):
                if hf:
                    act.wait_ge(s["scv_ready"], 1)
                multiplied(ck("sci", 3 * hf))
                A(GC, PA, ACT.Copy).then_inc(s["gc_copied"], 1)
                act.wait_ge(s["scv_ready"], hf + 1)
                if hf:
                    act.wait_ge(s["scz_ready"], 1)
                for m in range(4):
                    w1 = VEC[:, V_SC + 8 + 4 * hf + m:V_SC + 8 + 4 * hf + m + 1]
                    ins = A(blk(5)[:, m * S:m * S + S], CV[:, m * S:m * S + S], ACT.Copy, scale=w1)
                ins.then_inc(s["sc_mid"], 1)
            ffn(1, 8, XL, HL, S)

        @block.vector
        def _(dve):
            steps = [0]

            def step(ins):
                steps[0] += 1
                ins.then_inc(s["dve_step"], 1)

            def settle():
                dve.wait_ge(s["dve_step"], steps[0])

            def link(ins):
                step(ins)
                settle()

            def multiplied(c):
                dve.wait_ge(s["multiplied"], c + 1)

            V = dve
            V.memset(EPSC[:, :], EPS)
            V.wait_ge(s["vec_in"], 16)
            L0, L1 = VEC[:, V_LB:V_LB + 4], VEC[:, V_LB + 4:V_LB + 8]
            link(V.tensor_tensor(LB[:, 1, 0, :], L0, L1, ALU.max))
            link(V.tensor_tensor(LB[:, 0, 0, :], L0, LB[:, 1, 0, :], ALU.subtract))
            V.tensor_tensor(LB[:, 0, 1, :], L1, LB[:, 1, 0, :], ALU.subtract).then_inc(s["lb_ready"], 1)
            V.wait_ge(s["lb_ready"], 2)
            link(V.tensor_tensor(LB[:, 1, 0, :], LB[:, 0, 0, :], LB[:, 0, 1, :], ALU.add))
            link(V.reciprocal(LB[:, 1, 1, :], LB[:, 1, 0, :]))
            for l in range(2):
                link(V.tensor_tensor(LB[:, 0, l, :], LB[:, 0, l, :], LB[:, 1, 1, :], ALU.mult))
            link(V.tensor_tensor(LB[:, 1, 0, :], LB[:, 0, 0, :], LB[:, 0, 1, :], ALU.add))
            link(V.tensor_tensor(LB[:, 0, 1, :], LB[:, 1, 0, :], LB[:, 0, 0, :], ALU.subtract))
            link(V.tensor_tensor(LB[:, 0, 0, :], LB[:, 0, 0, :], LB[:, 0, 0, :], ALU.subtract))
            for l in range(2):
                link(V.tensor_scalar(LB[:, 1, l, :], LB[:, 0, l, :], -1.0, 1.0, ALU.mult, ALU.add))
            V.wait_ge(s["pos_in"], 16)
            V.wait_ge(s["const1_in"], 16)
            ang, kk = ANG, KK
            link(V.tensor_copy(kk, POS.bitcast(I32)))
            link(V.tensor_scalar(ang, kk, CS[0:DQK, C_INV:C_INV + 1], None, ALU.mult))
            two_pi = 2.0 * np.pi
            p1 = 6.28125
            p2 = float(np.float32(np.round((two_pi - p1) * 2 ** 22) / 2 ** 22))
            p3 = float(np.float32(two_pi - p1 - p2))
            magic = float(1.5 * 2 ** 23)
            for k, off in enumerate((0.25, 0.0)):
                r = RT[0:DQK, k * S:k * S + S]
                link(V.tensor_scalar(kk, ang, float(1.0 / two_pi), off, ALU.mult, ALU.add))
                link(V.tensor_scalar(kk, kk, magic, None, ALU.add))
                link(V.tensor_scalar(kk, kk, -magic, None, ALU.add))
                link(V.scalar_tensor_tensor(r, kk, -p1, ang, ALU.mult, ALU.add))
                link(V.scalar_tensor_tensor(r, kk, -p2, r, ALU.mult, ALU.add))
                link(V.scalar_tensor_tensor(r, kk, -p3, r, ALU.mult, ALU.add))
                if off:
                    link(V.tensor_scalar(r, r, float(np.pi / 2), None, ALU.add))
                ins = V.tensor_scalar(r, r, 3.1415925, -3.1415925, ALU.min, ALU.max)
                if k:
                    ins.then_inc(s["angle_ready"], 1)
                else:
                    link(ins)
            COS, SIN = RT[64:96, 0:S], RT[64:96, S:2 * S]
            def sum_rows(a, l, k):
                c = CHUNK_OF["ada", (a, l, k)]
                V.wait_ge(full[c % RING], 16 * (c // RING + 1 + extra(c)))
                w = ring[c % RING][:, :].rearrange("p (t n) -> p t n", t=KT)
                for v in range(n_vec(a, l)):
                    acc = acc_of(a, l, k, v)
                    for t in range(KT):
                        cs = CACT[:, a, t, v:v + 1]
                        if t == 0:
                            ins = V.tensor_scalar(acc, w[:, 0, :], cs, None, ALU.mult)
                        else:
                            ins = V.scalar_tensor_tensor(acc, w[:, t, :], cs, acc, ALU.mult, ALU.add)
                        if t < KT - 1 or v < n_vec(a, l) - 1:
                            link(ins)
                ins.then_inc(s["rows_summed"], 1)

            def take_modulation(a, l, k, q, last_job):
                multiplied(CHUNK_OF["ada", last_job])
                b0 = V_ADAB + 48 * (2 * a + l) + 4 * k
                for v in range(n_vec(a, l)):
                    ins = V.tensor_tensor(MOD[:, a, l, 4 * k:4 * k + 4, v], q[:, 4 * v:4 * v + 4], VEC[:, b0:b0 + 4], ALU.add)
                ins.then_inc(s["mod_taken"], 1)

            def sum_all(jobs):
                for job in jobs:
                    sum_rows(*job)

            def take_all(jobs, q):
                for n, job in enumerate(jobs):
                    take_modulation(*job, q[:, 8 * n:8 * n + 8], jobs[-1])

            def modulation(jobs, q):
                if not jobs:
                    return
                if n_vec(*jobs[0][:2]) == 1:
                    sum_all(jobs)
                    take_all(jobs, q)
                else:
                    for n, job in enumerate(jobs):
                        sum_rows(*job)
                        take_modulation(*job, q[:, 8 * n:8 * n + 8], job)

            def coef(a, l, k, last_job):
                V.wait_ge(s["mod_taken"], ADA_NO[last_job] + 1)
                g0 = V_NG + ((a * 2 + l) * 2 + k) * 8
                for v in range(n_vec(a, l)):
                    ins = V.scalar_tensor_tensor(COEF[:, a, l, k, :, v], MOD[:, a, l, 24 * k + 8:24 * k + 16, v], 1.0,
                                                 VEC[:, g0:g0 + 8], ALU.add, ALU.mult)
                ins.then_inc(s["coef_ready"], 1)
                n_coef[0] += 1
                V.wait_ge(s["coef_ready"], n_coef[0])

            n_coef = [0]
            V.wait_ge(s["cact_ready"], 1)
            for pair_ in (0, 2):
                for job in FIRST_ADA[pair_:pair_ + 2]:
                    sum_rows(*job)
                for n, job in enumerate(FIRST_ADA[pair_:pair_ + 2]):
                    take_modulation(*job, PA[:, 8 * (pair_ + n):8 * (pair_ + n) + 8], FIRST_ADA[pair_ + 1])
            coef(0, 0, 0, (0, 0, 3))

            def norm(n, X, H, N, a, l, which, ws):
                V.wait_ge(s["std_ready"], n + 1)
                link(V.reciprocal(RST[:, 0:N], RST[:, 0:N]))
                r = RST[:, 0:N].rearrange("p (a n) -> p a n", a=1).to_broadcast([P, KT, N])
                V.tensor_tensor(H, X, r, ALU.mult).then_inc(s["scaled_ready"], 1)
                V.wait_ge(s["scaled_ready"], h_count(n))
                for t in range(4, 8):
                    for w in range(ws):
                        sl = H[:, t, w * S:w * S + S]
                        ins = V.tensor_scalar(sl, sl, COEF[:, a, l, which, t, w:w + 1],
                                              MOD[:, a, l, 24 * which + t, w:w + 1], ALU.mult, ALU.add)
                ins.then_inc(s["h_dve"], 1)

            def residual(X, ts, a, l, col, w=0):
                for n, (t, q) in enumerate(ts):
                    ins = V.scalar_tensor_tensor(X[:, t, :], q, MOD[:, a, l, col + t, w:w + 1], X[:, t, :], ALU.mult, ALU.add)
                return ins

            EE = blk(4)
            T = blk(11)
            MK = float(2.0 ** 64 - 2.0 ** 40)
            for l in range(DEPTH):
                norm(2 * l, X1, H1, S, 0, l, 0, 1)
                RM, EE2 = blk(11), blk(8)
                link(V.memset(RM, 1.0))
                step(V.memset(RM.rearrange("p (c n) -> p c n", n=CH)[:, :, 0:1], 0.0))
                def place(name):
                    return dict(hf=PA[:, 768:], hq=PB[:, 768:], hi=PC[:, 512:], hg=PD[:, 768:], lat1=PA[:, 768:],
                                lat2=PB[:, 768:], gt0=PC[:, 768:], gt1=PA[:, 768:], gt2=PB[:, 768:], gt3=PC[:, 768:])[name]

                def between(*names):
                    for name in names:
                        modulation(BEFORE[name, l], place(name))
                between("hf", "hq")
                V.wait_ge(s["hf_sig"], l + 1)
                for h in range(4):
                    step(V.tensor_scalar(blk(2)[:, h * S:h * S + S], EE[:, h * S:h * S + S],
                                         LB[:, 1, l, h:h + 1], LB[:, 0, l, h:h + 1], ALU.mult, ALU.add))
                settle()
                step(V.tensor_scalar(blk(1), blk(2), -1.0, 1.0, ALU.mult, ALU.add))
                link(V.tensor_scalar(EE2, blk(2), float(2.0 ** -60), MK, ALU.is_lt, ALU.mult))
                V.scalar_tensor_tensor(blk(2), EE2, 1.0, blk(2), ALU.add, ALU.mult).then_inc(s["f_ready"], 1)
                between("hi")
                V.wait_ge(s["hq_silu"], l + 1)
                V.tensor_scalar(blk(0), blk(0), float(HG_D ** -0.5), None, ALU.mult).then_inc(s["hq_scaled"], 1)
                between("hg", "lat1", "lat2", "gt0")
                V.wait_ge(s["lnf_ready"], l + 1)
                link(V.scalar_tensor_tensor(blk(2), EE2, -float(np.log1p(MK) / MK), blk(2), ALU.mult, ALU.add))
                B = blk(2)
                link(V.tensor_tensor_scan(B, RM, B, 0.0, ALU.mult, ALU.add))
                B4 = B.rearrange("p (c n) -> p c n", n=CH)
                link(V.tensor_copy(BLAST, B4[:, :, CH - 1]))
                bl = BLAST.rearrange("p (c a) -> p c a", a=1).to_broadcast([P, 16, CH])
                V.tensor_tensor(blk(7).rearrange("p (c n) -> p c n", n=CH), bl, B4, ALU.subtract).then_inc(s["kdiff_ready"], 1)
                between("gt1", "gt2", "gt3")
                if l == 0:
                    coef(0, 0, 1, (0, 0, 11))
                V.wait_ge(s["lat_std"], l + 1)
                link(V.reciprocal(LRS[:, :, :].rearrange("p a n -> p (a n)"), LRS[:, :, :].rearrange("p a n -> p (a n)")))
                CL = XH[:, 4096:4096 + 1280].rearrange("p (t n) -> p t n", t=5)
                for t in range(5):
                    ins = V.scalar_tensor_tensor(CL[:, t, :], CL[:, t, :], VEC[:, V_CL + 5 * l + t:V_CL + 5 * l + t + 1],
                                                 LRS[:, t // 3, :], ALU.mult, ALU.mult)
                ins.then_inc(s["latn_ready"], 1)
                V.wait_ge(s["kexp_ready"], l + 1)
                V.tensor_tensor(blk(7), blk(7), blk(1), ALU.mult).then_inc(s["kd_ready"], 1)

                def diff(n):
                    hs = LEVELS[n]
                    nb = 1024 // (2 * hs)
                    b3 = B.rearrange("p (c n) -> p c n", n=2 * hs)
                    e3 = EE.rearrange("p (c n) -> p c n", n=2 * hs)
                    ref = b3[:, :, hs - 1:hs].to_broadcast([P, nb, hs])
                    if n == 0:
                        V.wait_ge(s["lat_sums"], l + 1)
                    else:
                        V.wait_ge(s["lvl_qk"], 6 * l + n)
                    V.tensor_tensor(e3[:, :, hs:2 * hs], b3[:, :, hs:2 * hs], ref, ALU.subtract)
                    V.tensor_tensor(e3[:, :, 0:hs], ref, b3[:, :, 0:hs], ALU.subtract).then_inc(s["lvl_diff"], 1)

                def qk(n):
                    if n >= 1:
                        V.wait_ge(s["lvl_score"], 7 * l + n)
                    V.wait_ge(s["lvl_exp"], 6 * l + n + 1)
                    V.tensor_tensor(blk(5), blk(0), EE, ALU.mult)
                    V.tensor_tensor(blk(6), blk(1), EE, ALU.mult).then_inc(s["lvl_qk"], 1)

                def masked(n):
                    if n == 0:
                        V.wait_ge(s["levels_in"], 16)
                    o = PB if n % 2 == 0 else PD
                    V.wait_ge(s["lvl_score"], 7 * l + n + 1)
                    mk = LVM[:, P * n:P * n + P].rearrange("p (a n) -> p a n", a=1).to_broadcast([P, 8, P])
                    dst = blk(10) if n == 0 else T
                    V.tensor_tensor(dst.rearrange("p (c n) -> p c n", n=P), o.rearrange("p (c n) -> p c n", n=P),
                                    mk, ALU.mult).then_inc(s["lvl_masked"], 1)
                    V.wait_ge(s["lvl_masked"], 7 * l + n + 1)
                    if n:
                        ins = V.tensor_tensor(blk(10), blk(10), T, ALU.add)
                        if n == 6:
                            ins.then_inc(s["lvl_added"], 1)
                        else:
                            link(ins)

                diff(0)
                qk(0)
                V.wait_ge(s["eb_ready"], l + 1)
                V.tensor_tensor(blk(8), blk(8), blk(0), ALU.mult).then_inc(s["qb_ready"], 1)
                for n in range(6):
                    if n < 5:
                        diff(n + 1)
                        if n == 1:
                            V.wait_ge(s["u_ready"], l + 1)
                            V.wait_ge(s["dec_ready"], l + 1)
                            ST = XH[:, 2048:2048 + 1536]
                            link(V.tensor_copy(ST[:, 0:512], PA[:, 0:512]))
                            for c in (1, 2):
                                src = PA[:, 512:1024] if c == 1 else PC[:, 0:512]
                                for h in range(4):
                                    ins = V.scalar_tensor_tensor(
                                        ST[:, 512 * c + h * P:512 * c + h * P + P],
                                        ST[:, 512 * (c - 1) + h * P:512 * (c - 1) + h * P + P],
                                        DEC[:, 4 * h + c:4 * h + c + 1], src[:, h * P:h * P + P], ALU.mult, ALU.add)
                                    if c == 1:
                                        step(ins)
                                settle()
                            ins.then_inc(s["states_ready"], 1)
                        masked(n)
                        qk(n + 1)
                    else:
                        masked(5)
                masked(6)
                V.wait_ge(s["o_std"], l + 1)
                link(V.reciprocal(T, T))
                link(V.tensor_tensor(T, T, blk(3), ALU.mult))
                for h in range(4):
                    sl = slice(h * S, h * S + S)
                    ins = V.scalar_tensor_tensor(F[3][:, sl], F[3][:, sl], VEC[:, V_HG + 4 * l + h:V_HG + 4 * l + h + 1],
                                                 T[:, sl], ALU.mult, ALU.mult)
                ins.then_inc(s["oa_ready"], 1)
                QH = AR[:, 4 * 1024:4 * 1024 + 9 * S].rearrange("p (h n) -> p h n", h=9)
                KH = AR[:, 7 * 1024:9 * 1024].rearrange("p (h n) -> p h n", h=8)
                V.wait_ge(s["kr_turned"], l + 1)
                V.wait_ge(s["rope_ready"], 1)
                V.wait_ge(s["q_copied"], l + 1)
                tmp = blk(0)[64:96, :].rearrange("p (h n) -> p h n", h=4)

                def wide(a, n):
                    return a.rearrange("p (a n) -> p a n", a=1).to_broadcast([ROPE, n, S])
                for k, (src, n) in enumerate(((PD, 4), (PA, 4), (PB, 1))):
                    link(V.tensor_tensor(tmp[:, 0:n, :], src[64:96, 0:n * S].rearrange("p (h n) -> p h n", h=n),
                                         wide(SIN, n), ALU.mult))
                    q = QH[64:96, 4 * k:4 * k + n, :]
                    link(V.tensor_tensor(q, q, wide(COS, n), ALU.mult))
                    link(V.tensor_tensor(q, q, tmp[:, 0:n, :], ALU.add))
                V.tensor_copy(KH[64:96, :, :], QH[64:96, 8:9, :].to_broadcast([ROPE, 8, S])).then_inc(s["rope_done"], 2)

                def softmax(u, nh, nk):
                    o = PA if u % 2 == 0 else PC
                    pr = blk(10).rearrange("p (h k) -> p h k", h=nh)
                    V.wait_ge(s["sc_ready"], 3 * l + u + 1)
                    if u:
                        V.wait_ge(s["p_turned"], 3 * l + u)
                    m0_ = C_MM if u == 0 else C_MM + 128
                    mk = CS[:, m0_:m0_ + nk].rearrange("p (a k) -> p a k", a=1).to_broadcast([P, nh, nk])
                    link(V.scalar_tensor_tensor(pr, o.rearrange("p (h k) -> p h k", h=nh), float(DQK ** -0.5), mk,
                                                ALU.mult, ALU.add))
                    link(V.tensor_reduce(NM[:, 0:nh], pr, axis=AXX, op=ALU.max))
                    V.tensor_scalar(NM[:, 0:nh], NM[:, 0:nh], -1.0, None, ALU.mult).then_inc(s["sm_max"], 1)
                    V.wait_ge(s["sm_exp"], 3 * l + u + 1)
                    link(V.reciprocal(RSUM[:, 0:nh], RSUM[:, 0:nh]))
                    V.tensor_tensor(pr, pr, RSUM[:, 0:nh].rearrange("p (h a) -> p h a", a=1).to_broadcast([P, nh, nk]),
                                    ALU.mult).then_inc(s["p_ready"], 1)
                softmax(0, 8, 128)
                softmax(1, 4, 256)
                softmax(2, 4, 256)
                sum_all(BEFORE["bb", l])
                multiplied(ck("ba", l))
                V.wait_ge(s["gates_act"], 4 * l + 4)
                V.tensor_tensor(blk(12), blk(12), PA, ALU.mult).then_inc(s["bra_mul"], 1)
                V.tensor_tensor(blk(13), blk(13), PB, ALU.mult).then_inc(s["bra_mul"], 1)
                take_all(BEFORE["bb", l], PD[:, 768:])
                sum_all(BEFORE["wo0", l])
                multiplied(ck("bb", l))
                step(V.tensor_tensor(blk(14), blk(14), PC, ALU.mult))
                link(V.tensor_tensor(blk(15), blk(15), PD, ALU.mult))
                V.wait_ge(s["bra_mul"], 2 * l + 2)
                V.tensor_tensor(AR[:, 12 * 1024:14 * 1024], AR[:, 12 * 1024:14 * 1024], AR[:, 14 * 1024:16 * 1024],
                                ALU.add).then_inc(s["merged_ready"], 1)
                take_all(BEFORE["wo0", l], PA[:, 768:])
                sum_all(BEFORE["wo1", l])
                take_all(BEFORE["wo1", l], PB[:, 768:])
                for k in range(2):
                    coef(*((0, 1) if l == 0 else (1, 0)), k, BEFORE["wo1", l][-1])
                multiplied(ck("wo1", l))
                residual(X1, [(m, (PA, PB)[m // 4][:, (m % 4) * S:(m % 4) * S + S]) for m in range(8)], 0, l, 16)\
                    .then_inc(s["x_done"], 1)
                norm(2 * l + 1, X1, H1, S, 0, l, 1, 1)
                V.wait_ge(s["rt_sig"], l + 1)
                sc = SCO_.rearrange("p (m g e) -> p (m g) e", m=2, g=NG)
                bi = R_BI.rearrange("p (q e) -> p q e", e=EG)
                rb = VEC[:, V_RB:V_RB + 16].rearrange("p (a n) -> p a n", a=1).to_broadcast([P, 2, 16])
                link(V.tensor_tensor(R_BI.rearrange("p (m n) -> p m n", m=2), SCO_.rearrange("p (m n) -> p m n", m=2), rb, ALU.add))

                def rank(val, rk, ge, q, n):
                    link(V.memset(rk, 0.0))
                    for d in range(1, n):
                        lo, hi = val[:, :, 0:n - d], val[:, :, d:n]
                        g_ = ge[:, :, 0:n - d]
                        link(V.tensor_tensor(g_, lo, hi, ALU.is_ge))
                        link(V.tensor_tensor(rk[:, :, d:n], rk[:, :, d:n], g_, ALU.add))
                        link(V.tensor_scalar(g_, g_, -1.0, 1.0, ALU.mult, ALU.add))
                        link(V.tensor_tensor(rk[:, :, 0:n - d], rk[:, :, 0:n - d], g_, ALU.add))
                rk, ge = R_RK.rearrange("p (q e) -> p q e", e=EG), R_GE.rearrange("p (q e) -> p q e", e=EG)
                rank(bi, rk, ge, 8, EG)
                link(V.tensor_scalar(R_RK, R_RK, 2.0, None, ALU.is_lt))
                link(V.tensor_tensor(R_GE, R_BI, R_RK, ALU.mult))
                link(V.tensor_reduce(R_GS, ge, axis=AXX, op=ALU.add))
                gs = R_GS.rearrange("p (m g) -> p m g", m=2)
                gr = R_GR.rearrange("p (m g) -> p m g", m=2)
                gg = R_GG.rearrange("p (m g) -> p m g", m=2)
                rank(gs, gr, gg, 2, NG)
                link(V.tensor_scalar(R_GR, R_GR, 1.0, None, ALU.is_lt))
                step(V.tensor_tensor(rk, rk, R_GR.rearrange("p (q a) -> p q a", a=1).to_broadcast([P, 8, 4]), ALU.mult))
                settle()
                V.sem_inc(s["sel_ready"], 1)
                link(V.tensor_tensor(R_GE, SCO_, R_RK, ALU.mult))
                link(V.tensor_reduce(R_DN, R_GE.rearrange("p (m n) -> p m n", m=2), axis=AXX, op=ALU.add))
                link(V.reciprocal(R_DN, R_DN))
                link(V.tensor_tensor(R_GE.rearrange("p (m n) -> p m n", m=2), R_GE.rearrange("p (m n) -> p m n", m=2),
                                     R_DN.rearrange("p (m a) -> p m a", a=1).to_broadcast([P, 2, 16]), ALU.mult))
                V.wait_ge(s["places_ready"], l + 1)
                link(V.scalar_tensor_tensor(R_BI, PD[:, 0:2 * NE], 1.0, R_RK, ALU.add, ALU.mult))
                link(V.tensor_scalar(R_BI, R_BI, -1.0, None, ALU.add))
                link(V.tensor_reduce(R_DN[:, 0:1], PD[:, 2 * NE:3 * NE], axis=AXX, op=ALU.max))
                V.tensor_scalar(OVERFLOW, R_DN[:, 0:1], float(CAP), None, ALU.is_gt).then_inc(s["overflow_ready"], 1)
                idb = ident.rearrange("p (a n) -> p a n", a=1).to_broadcast([P, 4, P])

                def diagonal(g):
                    for m in range(2):
                        if g >= 1:
                            V.wait_ge(s["cbc_ready"], 8 * l + 2 * (g - 1) + m + 1)
                        cw = R_GE[:, 16 * m + 4 * g:16 * m + 4 * g + 4].rearrange("p (e a) -> p e a", a=1).to_broadcast([P, 4, P])
                        V.tensor_tensor(blk(9 + m, 512).rearrange("p (e n) -> p e n", e=4), idb, cw, ALU.mult)\
                            .then_inc(s["diag_ready"], 1)

                def slots(e, col=None):
                    for m in range(2):
                        at = slice(NE * m + e, NE * m + e + 1) if col is None else bass.ds(col + NE * m, 1)
                        G = SLOT[e % 2]
                        V.tensor_scalar(G[:, 0, m, :], CS[:, C_IOTA:C_IOTA + CAP], R_BI[:, at], None, ALU.is_equal)
                        ins = V.tensor_scalar(G[:, 1, m, :], CS[:, C_IOTA:C_IOTA + CAP], R_BI[:, at], R_GE[:, at],
                                              ALU.is_equal, ALU.mult)
                    ins.then_inc(s["slot_ready"], 1)

                V.wait_ge(s["iota_in"], 16)
                slots(1)
                diagonal(0)
                V.memset(blk(11, 128), 0.0).then_inc(s["acc_zero"], 1)
                slots(2)
                m0 = ck("moe", l)
                SG, HE = [blk(4), blk(5)], [blk(6), blk(7)]

                def weigh(e, i, j, loop):
                    cu = m0 + 1 if e == 0 else (m0 + 45 if e == 15 else m0 + 2 + 3 * (e - 1) + 1)
                    V.wait_ge(s["multiplied"], i * 6 + (cu + 1))
                    V.wait_ge(s["sg_ready"], i * 2 + (16 * l + e + 1))
                    V.tensor_tensor(GU[j], SG[j], PB, ALU.mult).then_inc(s["gu_ready"], 1)
                    V.wait_ge(s["gu_ready"], i * 2 + (16 * l + e + 1))
                    cb = AR[:, bass.ds((i * 2 + e) * S, S)] if loop else AR[:, e * S:e * S + S]
                    V.tensor_tensor(HE[j].rearrange("p (t n) -> p t n", t=4), GU[j].rearrange("p (t n) -> p t n", t=4),
                                    cb.rearrange("p (a n) -> p a n", a=1).to_broadcast([P, 4, S]), ALU.mult)\
                        .then_inc(s["he_ready"], 1)
                V.wait_ge(s["cbc_copied"], 4 * l + 1)
                weigh(0, 0, 0, False)
                overflow = V.value_load(OVERFLOW[0:1, :], min_val=0, max_val=1)
                with V.If(overflow):
                    for g in range(1, 4):
                        diagonal(g)
                    V.wait_ge(s["cbc_copied"], 4 * l + 4)
                    with V.Fori(0, 7) as i:
                        for j in range(2):
                            weigh(1 + j, i, (1 + j) % 2, True)
                    weigh(15, 0, 1, False)
                    V.sem_inc(s["slot_ready"], NE - 3)
                    V.sem_inc(s["xe_ready"], NE - 1)
                    V.sem_inc(s["tok1_ready"], NE - 1)
                with V.Else():
                    b0 = (NE - 1) * l

                    def c_gathered(e, i=0):
                        V.wait_ge(s["gathered"], i * 2 + (b0 + e))
                        V.tensor_copy(XE[e % 2].rearrange("p (b t) n -> p b (t n)", b=2),
                                      PA.rearrange("p (b n) -> p b n", b=2)[:, :, 0:4 * CAP]).then_inc(s["xe_ready"], 1)

                    def c_hidden(e, i=0):
                        V.wait_ge(s["multiplied"], i * 6 + (m0 + 3 * e + 1))
                        V.wait_ge(s["sg_ready"], i * 2 + (NE * l + e + 1))
                        V.tensor_tensor(HEC[e % 2], SGC, PB[:, 512:512 + 4 * CAP], ALU.mult).then_inc(s["he_ready"], 1)
                        V.tensor_copy(TOK[e % 2][:, P:2 * P], PB[0:CAP, 512 + 4 * CAP:1024]).then_inc(s["tok1_ready"], 1)
                    c_gathered(1)
                    with V.Fori(0, 6) as i:
                        for e in (1, 2):
                            c_gathered(e + 1, i)
                            c_hidden(e, i)
                            slots(e + 2, i * 2 + (e + 2))
                    c_gathered(14)
                    c_hidden(13)
                    slots(15)
                    c_gathered(15)
                    c_hidden(14)
                    c_hidden(15)
                    V.wait_ge(s["scattered"], b0 + NE - 1)
                    V.sem_inc(s["gu_ready"], NE - 1)
                    V.sem_inc(s["diag_ready"], 6)
                multiplied(m0 + 47)
                residual(X1, [(m, (PC, PD)[m // 4][:, (m % 4) * S:(m % 4) * S + S]) for m in range(8)], 0, l, 40)\
                    .then_inc(s["x_done"], 1)

            V.wait_ge(s["std_ready"], 5)
            link(V.reciprocal(RST[:, 0:S], RST[:, 0:S]))
            for t in range(8):
                ins = V.scalar_tensor_tensor(X2[:, t, 0:S], X1[:, t, :], VEC[:, V_FIN + t:V_FIN + t + 1], RST[:, 0:S],
                                             ALU.mult, ALU.mult)
            ins.then_inc(s["x_done"], 1)
            norm(5, X2, H2, 512, 1, 0, 0, 2)
            V.wait_ge(s["const2_in"], 16)
            wcos = CS[:, C1_OVER + D_COS:C1_OVER + D_COS + S].rearrange("p (a n) -> p a n", a=1).to_broadcast([P, 2, S])
            wsin = CS[:, C1_OVER + D_SIN:C1_OVER + D_SIN + S].rearrange("p (a n) -> p a n", a=1).to_broadcast([P, 2, S])
            QT = [AR[:, k * 1024:k * 1024 + 1024] for k in range(5)]
            for u in range(5):
                gcol = V_WQ if u < 4 else V_WK
                V.wait_ge(s["wstd_ready"], u + 1)
                link(V.reciprocal(blk(8), blk(8)))
                V.scalar_tensor_tensor(QT[u], QT[u], VEC[:, gcol:gcol + 1], blk(8), ALU.mult, ALU.mult).then_inc(s["wn_ready"], 1)
                V.wait_ge(s["wrot_ready"], u + 1)
                q = QT[u].rearrange("p (t n) -> p t n", t=2)[:, :, 0:S]
                t_ = blk(9, 512).rearrange("p (t n) -> p t n", t=2)
                step(V.tensor_tensor(t_, PD[:, 0:512].rearrange("p (t n) -> p t n", t=2), wsin, ALU.mult))
                link(V.tensor_tensor(q, q, wcos, ALU.mult))
                V.tensor_tensor(q, q, t_, ALU.add).then_inc(s["wroped"], 1)

            def finish_softmax(u):
                nb = 2 if u % 3 < 2 else 4
                V.wait_ge(s["sm_exp"], 3 * DEPTH + u + 1)
                link(V.tensor_tensor(WRS[:, u % 2, 0:nb], WRS[:, u % 2, 0:nb], WES[:, u % 2, 0:nb], ALU.add))
                link(V.reciprocal(WRS[:, u % 2, 0:nb], WRS[:, u % 2, 0:nb]))
                p3 = blk(12 + u % 2).rearrange("p (b k) -> p b k", b=nb)
                V.tensor_tensor(p3, p3, WRS[:, u % 2, 0:nb].rearrange("p (b a) -> p b a", a=1)
                                .to_broadcast([P, nb, 1024 // nb]), ALU.mult).then_inc(s["p_ready"], 1)

            for u in range(24):
                t, kind = u // 3, u % 3
                o = (PA, PB)[u % 2]
                pr = blk(12 + u % 2)
                nb = 2 if kind < 2 else 4
                V.wait_ge(s["sc_ready"], 3 * DEPTH + u + 1)
                if u >= 2:
                    V.wait_ge(s["p_turned"], 3 * DEPTH + u - 1)
                if kind < 2:
                    o3, p3_ = o.rearrange("p (b k) -> p b k", b=2), pr.rearrange("p (b k) -> p b k", b=2)
                    mk = CS[:, C1_OVER + D_WM:C1_OVER + D_WM + 512].rearrange("p (b k) -> p b k", b=2)
                    step(V.scalar_tensor_tensor(p3_[:, :, 0:S], o3[:, :, 0:S], float(WHD ** -0.5), mk, ALU.mult, ALU.add))
                    link(V.tensor_scalar(p3_[:, :, S:512], o3[:, :, S:512], float(WHD ** -0.5), None, ALU.mult))
                else:
                    link(V.tensor_scalar(pr, o, float(WHD ** -0.5), None, ALU.mult))
                link(V.tensor_reduce(WNM[:, u % 2, 0:nb], pr.rearrange("p (b k) -> p b k", b=nb), axis=AXX, op=ALU.max))
                if kind < 2:
                    h = 2 * t + kind
                    V.tensor_scalar(WNM[:, u % 2, 0:2], WNM[:, u % 2, 0:2], VEC[:, V_SINK + h:V_SINK + h + 1], -1.0,
                                    ALU.max, ALU.mult).then_inc(s["sm_max"], 1)
                else:
                    for h in range(2):
                        ins = V.tensor_scalar(WNM[:, u % 2, 2 * h:2 * h + 2], WNM[:, u % 2, 2 * h:2 * h + 2],
                                              VEC[:, V_SINK + 2 * t + h:V_SINK + 2 * t + h + 1], -1.0, ALU.max, ALU.mult)
                    ins.then_inc(s["sm_max"], 1)
                finish_softmax(u)

            def bank(k):
                return (PA, PB, PC, PD)[k // 2][:, (k % 2) * 512:(k % 2) * 512 + 512]
            multiplied(ck("wwo", 1))
            for w in range(2):
                ins = residual(X2[:, :, w * S:w * S + S], [(m, bank(m)[:, w * S:w * S + S]) for m in range(8)], 1, 0, 16, w)
            ins.then_inc(s["x_done"], 1)

            def ffn(l, n, X, H, N):
                norm(n, X, H, N, 1, l, 1, N // S)
                A = AR[:, 0:22 * N].rearrange("p (t n) -> p t n", n=N)
                ws = N // S
                modulation(BEFORE["up0", l], bank(3))
                for j in range(22):
                    if j % 2 == 0 and j < 20:
                        modulation(BEFORE[f"up{j // 2 + 1}", l], bank(4 * ((j // 2 + 1) % 2) + 3))
                    b0 = (4 * ((j // 2) % 2) + 2 * (j % 2))
                    tmp = CVT[j % 2]
                    for h in range(2):
                        V.wait_ge(s["cv_mid"], 2 * (22 * l + j) + h + 1)
                        x3 = bank(b0 + h)[:, 0:N].rearrange("p (w n) -> p w n", w=ws)
                        t3 = tmp[:, h, 0:N].rearrange("p (w n) -> p w n", w=ws)
                        wc = V_FC + 132 * l + 22 * h + j
                        link(V.scalar_tensor_tensor(t3[:, :, 1:S], x3[:, :, 0:S - 1], VEC[:, wc:wc + 1], t3[:, :, 1:S],
                                                    ALU.mult, ALU.add))
                        V.scalar_tensor_tensor(t3[:, :, 0:S - 1], x3[:, :, 1:S], VEC[:, wc + 88:wc + 89], t3[:, :, 0:S - 1],
                                               ALU.mult, ALU.add).then_inc(s["cv_conv"], 1)
                    V.wait_ge(s["cv_silu"], 22 * l + j + 1)
                    V.wait_ge(s["cv_conv"], 2 * (22 * l + j) + 2)
                    V.tensor_tensor(A[:, j, :], tmp[:, 0, 0:N], tmp[:, 1, 0:N], ALU.mult).then_inc(s["ff_act"], 1)
                if l == 0:
                    coef(1, 1, 0, (1, 1, 11))
                    coef(1, 1, 1, (1, 1, 11))
                multiplied(ck("down5", l))
                for w in range(ws):
                    ins = residual(X[:, :, w * S:w * S + S], [(m, bank(m)[:, w * S:w * S + S]) for m in range(8)], 1, l, 40, w)
                ins.then_inc(s["x_done"], 1)
            ffn(0, 6, X2, H2, 512)
            HL = XH[:, 0:2048].rearrange("p (t n) -> p t n", t=8)
            XL = X2[:, :, 0:S]
            norm(7, XL, HL, S, 1, 1, 0, 1)
            GC, CV, CM = blk(2), blk(3), blk(5)
            for hf in range(2):
                multiplied(ck("sci", 3 * hf + 1))
                V.wait_ge(s["gc_copied"], hf + 1)
                V.tensor_tensor(CV, GC, PB, ALU.mult).then_inc(s["scv_ready"], 1)
                V.wait_ge(s["sc_mid"], hf + 1)
                for m in range(4):
                    wc = V_SC + 4 * hf + m
                    o = m * S
                    link(V.scalar_tensor_tensor(CM[:, o + 1:o + S], CV[:, o:o + S - 1], VEC[:, wc:wc + 1], CM[:, o + 1:o + S],
                                                ALU.mult, ALU.add))
                    step(V.scalar_tensor_tensor(CM[:, o:o + S - 1], CV[:, o + 1:o + S], VEC[:, wc + 16:wc + 17],
                                                CM[:, o:o + S - 1], ALU.mult, ALU.add))
                settle()
                multiplied(ck("sci", 3 * hf + 2))
                V.tensor_tensor(AR[:, 1024 * hf:1024 * hf + 1024], CM, (PC, PD)[hf], ALU.mult).then_inc(s["scz_ready"], 1)
            multiplied(ck("sco", 1))
            residual(XL, [(m, (PA, PB)[m // 4][:, (m % 4) * S:(m % 4) * S + S]) for m in range(8)], 1, 1, 16)\
                .then_inc(s["x_done"], 1)
            ffn(1, 8, XL, HL, S)


def level_masks():
    s_, t_ = np.arange(P)[:, None], np.arange(P)[None, :]
    out = [(s_ // (2 * h) == t_ // (2 * h)) & (s_ % (2 * h) < h) & (t_ % (2 * h) >= h) if h else s_ == t_ for h in LEVELS]
    return np.concatenate(out, 1).astype(np.float32)


def constants():
    c1 = np.zeros((P, N_C1), np.float32)
    c1[:, C_ID:C_ID + P] = np.eye(P)
    c1[:, C_ONE:C_ONE + P] = 1.0
    inv = np.float32(10000.0) ** (-np.arange(16, dtype=np.float32) / np.float32(16))
    c1[64:80, C_INV] = inv
    c1[80:96, C_INV] = inv
    for i in range(16):
        c1[80 + i, C_PR + i] = -1.0
        c1[64 + i, C_PR + 16 + i] = 1.0
    q, k = np.arange(P)[:, None] // CH, np.arange(S)[None, :] // CH
    c1[:, C_MM:C_MM + P] = np.where(k[:, :P] <= q, 0.0, -1e30)
    c1[:, C_MM + P:C_MM + P + S] = np.where(k <= q + 2, 0.0, -1e30)
    c2 = np.zeros((P, N_C2), np.float32)
    for i in range(2):
        c2[64 * i:64 * i + 64, D_B64 + 64 * i:D_B64 + 64 * i + 64] = 1.0
        for d in range(32):
            c2[64 * i + 32 + d, D_P64 + 64 * i + d] = -1.0
            c2[64 * i + d, D_P64 + 64 * i + 32 + d] = 1.0
        for h in range(2):
            c2[64 * i:64 * i + 64, D_SEL + P * i + 64 * h:D_SEL + P * i + 64 * h + 64] = np.eye(64)
    inv = np.float32(10000.0) ** (-np.arange(16, dtype=np.float32) / np.float32(16))
    tok = np.arange(S)
    ang = np.concatenate([(tok // 64)[None, :] * inv[:, None], (tok % 64)[None, :] * inv[:, None]], 0).astype(np.float32)
    c2[:, D_COS:D_COS + S] = np.tile(np.cos(ang), (4, 1))
    c2[:, D_SIN:D_SIN + S] = np.tile(np.sin(ang), (4, 1))
    q, k = np.arange(P)[:, None], np.arange(S)[None, :]
    for b in range(2):
        c2[:, D_WM + S * b:D_WM + S * b + S] = np.where(np.abs(q + P * b - k) <= 128, 0.0, -1e30)
    return c1, c2


def packed(i):
    def fm(a):
        a = np.asarray(a)
        return np.moveaxis(a.reshape(a.shape[:-1] + (a.shape[-1] // P, P)), -1, 0).reshape(P, -1)

    out = [fm(i["norm1_g"][0]), fm(i["norm2_g"][0]), fm(i["norm1_g"][1]), fm(i["norm2_g"][1]),
           fm(i["norm_mix_2"][0]), fm(i["norm_ffn_2"][0]), fm(i["norm_mix_2"][1]), fm(i["norm_ffn_2"][1]),
           fm(i["final_g"]), fm(i["hg_norm_g"]),
           fm(i["q_norm_g"][0]), fm(i["kv_norm_g"][0]), fm(i["q_norm_g"][1]), fm(i["kv_norm_g"][1]),
           fm(i["hg_lb_logits"]), np.tile(i["router_bias"][None, :], (P, 1))]
    for pair in ((i["c"][0], i["c"][0]), (i["c_2"][0], i["c_ctx_2"])):
        out.append(np.stack([fm(v) for v in pair], -1).reshape(P, -1))
    out += [fm(i["ada_b"]), fm(i["ada_b_2"]),
            np.tile(i["win_q_norm_2"][0], 2)[:, None], np.tile(i["win_k_norm_2"][0], 2)[:, None],
            np.tile(i["win_sink_2"], (P, 1)), fm(i["ffn_conv_2"]), fm(i["sc_conv_2"][0])]
    return np.ascontiguousarray(np.concatenate(out, 1))


WEIGHTS = ["ada_w", "ada_w_2", "w_in", "w_q_up", "w_kv_up", "w_br_a", "w_br_b", "w_out", "w_router", "w_gate", "w_up",
           "w_down"]
WEIGHTS_2 = {"win_w_qkv": "win_w_qkv_2", "win_w_o": "win_w_o_2", "ffn_w_up": "ffn_w_up_2", "ffn_w_down": "ffn_w_down_2",
             "sc_w_in": "sc_w_in_2", "sc_w_out": "sc_w_out_2"}


def kernel(**inputs):
    import concourse.bacc as _bacc
    from concourse.bass_utils import run_bass_kernel_spmd as _run

    i = {k: np.asarray(v) for k, v in inputs.items()}
    a = {n: i[n] for n in WEIGHTS}
    for n, m in WEIGHTS_2.items():
        a[n] = i[m][0] if i[m].shape[0] == 1 else i[m]
    c1, c2 = constants()
    import ml_dtypes
    a["levels"] = level_masks().astype(ml_dtypes.bfloat16)
    a["const1"], a["const2"], a["vec"] = c1, c2, packed(i)
    a["before"] = np.triu(np.ones((P, P), np.float32), 1)
    a["iota"] = np.tile(np.arange(CAP, dtype=np.float32), (P, 1))
    a["x"], a["ctx"] = i["x"][0].T, i["ctx_2"][0].T
    a["pos"] = np.tile(i["positions"].astype(np.int32), (DQK, 1))
    nc = _bacc.Bacc("TRN2", target_bir_lowering=False, num_devices=1)
    arrays, aps = {}, {}
    for n, v in a.items():
        v = np.ascontiguousarray(v)
        arrays["in_" + n] = v
        aps[n] = nc.dram_tensor("in_" + n, v.shape, mybir.dt.from_np(v.dtype), kind="ExternalInput").ap()
    out = nc.dram_tensor("out_0", (D, S), F32, kind="ExternalOutput").ap()
    stack_program(nc, aps, out)
    r = _run(nc, [arrays], core_ids=[0])
    return np.ascontiguousarray(r.results[0]["out_0"].T)[None]
```
